# Optimizing a Trainium2 kernel written in Bass

```python
import math
import jax, jax.numpy as jnp
from jax import lax
import numpy as np

D_MODEL = 1024
BATCH = 1
SEQ = 512
DEPTH = 1

N_MIXERS = 2
MEM_LEN = 256
D_FF = 2752
LN_EPS = 1e-5
ALPHA = (2 * DEPTH) ** 0.25
BETA_INIT = (8 * DEPTH) ** -0.25
GDN_HEADS = 6
GDN_DK = 128
GDN_DV = 128
GDN_W = GDN_HEADS * GDN_DV
GDN_CONV = 4
GDN_CHUNK = 64
DSA_HEADS = 12
DSA_DH = 64
DSA_W = DSA_HEADS * DSA_DH
DSA_KV_RANK = 256
IDX_HEADS = 8
IDX_DIM = 64
TOPK_MAX = 256
Q_BLOCK = 128
MEM_HEADS = 4
MEM_DH = 64
MEM_W = MEM_HEADS * MEM_DH
GDN_IN = 4 * GDN_W + 2 * GDN_HEADS + MEM_W
DSA_IN = DSA_W + DSA_KV_RANK + IDX_HEADS * IDX_DIM + IDX_DIM + IDX_HEADS + MEM_W
MIX_OUT = GDN_W + MEM_W

kernel_name = "hybrid_gdn_dsa_macaron_deepnorm"

def layer_norm(x, g, b):
    xf = x.astype(jnp.float32)
    mu = jnp.mean(xf, -1, keepdims=True)
    var = jnp.mean(jnp.square(xf - mu), -1, keepdims=True)
    return ((xf - mu) * lax.rsqrt(var + LN_EPS) * g + b).astype(x.dtype)

def rms_norm(x, g):
    xf = x.astype(jnp.float32)
    return (xf * lax.rsqrt(jnp.mean(jnp.square(xf), -1, keepdims=True) + LN_EPS) * g).astype(x.dtype)

def l2_normalize(x):
    xf = x.astype(jnp.float32)
    return xf * lax.rsqrt(jnp.sum(jnp.square(xf), -1, keepdims=True) + 1e-6)

def post_norm_residual(x, y, g, b):
    return layer_norm(ALPHA * x + y, g, b)

def swiglu(x, w_in, w_out):
    gate, up = jnp.split(x @ w_in, 2, axis=-1)
    return (jax.nn.silu(gate) * up) @ w_out

def causal_dwconv(x, w):
    k, c = w.shape
    return lax.conv_general_dilated(x, w[:, None, :], window_strides=(1,), padding=((k - 1, 0),),
                                    dimension_numbers=("NWC", "WIO", "NWC"), feature_group_count=c)

def alibi_slopes(n_heads):
    return jnp.exp2(-8.0 * jnp.arange(1, n_heads + 1, dtype=jnp.float32) / n_heads)

def memory_attention(q_mem, mem, w_mem_kv):
    b, t, _ = q_mem.shape
    m = mem.shape[1]
    k, v = jnp.split(mem @ w_mem_kv, 2, axis=-1)
    q = q_mem.reshape(b, t, MEM_HEADS, MEM_DH)
    k = k.reshape(b, m, MEM_HEADS, MEM_DH)
    v = v.reshape(b, m, MEM_HEADS, MEM_DH)
    s = jnp.einsum("bthd,bmhd->bhtm", q, k).astype(jnp.float32) * (MEM_DH ** -0.5)
    p = jax.nn.softmax(s, axis=-1).astype(v.dtype)
    return jnp.einsum("bhtm,bmhd->bthd", p, v).reshape(b, t, MEM_W)

def gated_delta_rule(q, k, v, g, beta):
    b, t, h, dk = q.shape
    dv = v.shape[-1]
    c = GDN_CHUNK
    n = t // c
    f32 = jnp.float32

    def to_chunks(a):
        return jnp.swapaxes(a.reshape(b, n, c, *a.shape[2:]), 2, 3)

    q = to_chunks(q.astype(f32) * (dk ** -0.5))
    k = to_chunks(k.astype(f32))
    v = to_chunks(v.astype(f32))
    beta = to_chunks(beta.astype(f32))
    g = jnp.cumsum(to_chunks(g.astype(f32)), axis=-1)

    tri_incl = jnp.tril(jnp.ones((c, c), dtype=bool))
    tri_strict = jnp.tril(jnp.ones((c, c), dtype=bool), -1)
    gdiff = g[..., :, None] - g[..., None, :]
    decay = jnp.where(tri_incl, jnp.exp(jnp.where(tri_incl, gdiff, 0.0)), 0.0)

    kb = k * beta[..., None]
    a_mat = jnp.where(tri_strict, jnp.einsum("bnhid,bnhjd->bnhij", kb, k) * decay, 0.0)
    eye = jnp.eye(c, dtype=f32)
    t_mat = lax.linalg.triangular_solve(eye + a_mat, jnp.broadcast_to(eye, a_mat.shape),
                                        left_side=True, lower=True, unit_diagonal=True)
    u_base = jnp.einsum("bnhij,bnhje->bnhie", t_mat, v * beta[..., None])
    w_dec = jnp.einsum("bnhij,bnhjd->bnhid", t_mat, kb * jnp.exp(g)[..., None])
    qk = jnp.where(tri_incl, jnp.einsum("bnhid,bnhjd->bnhij", q, k) * decay, 0.0)
    q_dec = q * jnp.exp(g)[..., None]
    k_dec = k * jnp.exp(g[..., -1:] - g)[..., None]
    g_last = jnp.exp(g[..., -1])

    def step(state, inp):
        u_b, w_c, qk_c, qd, kd, gl = inp
        u = u_b - jnp.einsum("bhcd,bhde->bhce", w_c, state)
        o = jnp.einsum("bhcd,bhde->bhce", qd, state) + jnp.einsum("bhij,bhje->bhie", qk_c, u)
        state = state * gl[..., None, None] + jnp.einsum("bhcd,bhce->bhde", kd, u)
        return state, o

    xs = tuple(jnp.moveaxis(a, 1, 0) for a in (u_base, w_dec, qk, q_dec, k_dec, g_last))
    s0 = jnp.zeros((b, h, dk, dv), f32)
    _, o = lax.scan(step, s0, xs)
    o = jnp.swapaxes(jnp.moveaxis(o, 0, 1), 2, 3)
    return o.reshape(b, t, h, dv)

def gdn_mixer(x, mem, w_in, conv_w, a_log, dt_bias, onorm_g, w_mem_kv, w_o):
    b, t, _ = x.shape
    proj = x @ w_in
    qkv, gate, b_raw, a_raw, q_mem = jnp.split(
        proj, [3 * GDN_W, 4 * GDN_W, 4 * GDN_W + GDN_HEADS, 4 * GDN_W + 2 * GDN_HEADS], axis=-1)
    qkv = jax.nn.silu(causal_dwconv(qkv, conv_w))
    q, k, v = jnp.split(qkv, 3, axis=-1)
    q = l2_normalize(q.reshape(b, t, GDN_HEADS, GDN_DK))
    k = l2_normalize(k.reshape(b, t, GDN_HEADS, GDN_DK))
    v = v.reshape(b, t, GDN_HEADS, GDN_DV)
    beta = jax.nn.sigmoid(b_raw.astype(jnp.float32))
    g = -jnp.exp(a_log.astype(jnp.float32)) * jax.nn.softplus(a_raw.astype(jnp.float32) + dt_bias)
    o = gated_delta_rule(q, k, v, g, beta)
    o = rms_norm(o, onorm_g) * jax.nn.silu(gate.reshape(b, t, GDN_HEADS, GDN_DV).astype(jnp.float32))
    o = o.astype(x.dtype).reshape(b, t, GDN_W)
    o_mem = memory_attention(q_mem, mem, w_mem_kv)
    return jnp.concatenate([o, o_mem], axis=-1) @ w_o

def dsa_mixer(x, mem, w_in, kv_norm_g, w_uk, w_uv, kidx_ln_g, kidx_ln_b, w_mem_kv, w_o):
    b, t, _ = x.shape
    f32 = jnp.float32
    proj = x @ w_in
    o1 = DSA_W
    o2 = o1 + DSA_KV_RANK
    o3 = o2 + IDX_HEADS * IDX_DIM
    o4 = o3 + IDX_DIM
    o5 = o4 + IDX_HEADS
    q, c_kv, q_idx, k_idx, w_idx, q_mem = jnp.split(proj, [o1, o2, o3, o4, o5], axis=-1)
    c_kv = rms_norm(c_kv, kv_norm_g)
    k_idx = layer_norm(k_idx, kidx_ln_g, kidx_ln_b)
    w_idx = w_idx.astype(f32) * (IDX_HEADS ** -0.5 * IDX_DIM ** -0.5)
    topk = min(TOPK_MAX, t // 4)
    slopes = alibi_slopes(DSA_HEADS)
    nb = t // Q_BLOCK

    def blocks(a):
        return jnp.moveaxis(a.reshape(b, nb, Q_BLOCK, *a.shape[2:]), 1, 0)

    xs = (jnp.arange(nb, dtype=jnp.int32) * Q_BLOCK,
          blocks(q.reshape(b, t, DSA_HEADS, DSA_DH)),
          blocks(q_idx.reshape(b, t, IDX_HEADS, IDX_DIM)),
          blocks(w_idx))
    s_pos = jnp.arange(t, dtype=jnp.int32)

    def block(args):
        start, qb, qxb, wxb = args
        t_pos = start + jnp.arange(Q_BLOCK, dtype=jnp.int32)
        causal = s_pos[None, :] <= t_pos[:, None]
        isc = jax.nn.relu(jnp.einsum("bqhd,bsd->bqhs", qxb, k_idx).astype(f32))
        isc = jnp.einsum("bqhs,bqh->bqs", isc, wxb)
        isc = jnp.where(causal[None], isc, -jnp.inf)
        _, idx = lax.top_k(isc, topk)
        valid = idx <= t_pos[None, :, None]
        c_sel = jax.vmap(lambda cb, ib: cb[ib])(c_kv, idx)
        q_lat = jnp.einsum("bqhd,hdr->bqhr", qb, w_uk)
        s = jnp.einsum("bqhr,bqkr->bhqk", q_lat, c_sel).astype(f32) * (DSA_DH ** -0.5)
        dist = (t_pos[None, :, None] - idx).astype(f32)
        s = s - slopes[None, :, None, None] * dist[:, None]
        s = jnp.where(valid[:, None], s, -jnp.inf)
        p = jax.nn.softmax(s, axis=-1).astype(c_sel.dtype)
        o_lat = jnp.einsum("bhqk,bqkr->bqhr", p, c_sel)
        return jnp.einsum("bqhr,hrd->bqhd", o_lat, w_uv)

    o = lax.map(block, xs)
    o = jnp.moveaxis(o, 0, 1).reshape(b, t, DSA_W)
    o_mem = memory_attention(q_mem, mem, w_mem_kv)
    return jnp.concatenate([o, o_mem], axis=-1) @ w_o

def setup_inputs(seed: int = 0) -> dict:
    key = jax.random.key(seed)
    keys = iter(jax.random.split(key, 64))

    def nrm(shape, scale):
        return jax.random.normal(next(keys), shape, jnp.float32) * scale

    def gain(n):
        return 1.0 + nrm((n,), 0.02)

    def bias(n):
        return nrm((n,), 0.02)

    def ffn_in():
        return nrm((D_MODEL, 2 * D_FF), D_MODEL ** -0.5)

    def ffn_out():
        return nrm((D_FF, D_MODEL), D_FF ** -0.5 * BETA_INIT)

    dt = jnp.exp(jax.random.uniform(next(keys), (GDN_HEADS,), jnp.float32, math.log(1e-3), math.log(0.1)))
    inp = {}
    inp["x"] = nrm((BATCH, SEQ, D_MODEL), 1.0)
    inp["mem"] = nrm((BATCH, MEM_LEN, D_MODEL), 1.0)
    inp["l0_ffn1_w_in"] = ffn_in()
    inp["l0_ffn1_w_out"] = ffn_out()
    inp["l0_ln1_g"] = gain(D_MODEL)
    inp["l0_ln1_b"] = bias(D_MODEL)
    inp["l0_w_in"] = nrm((D_MODEL, GDN_IN), D_MODEL ** -0.5)
    inp["l0_conv_w"] = nrm((GDN_CONV, 3 * GDN_W), GDN_CONV ** -0.5)
    inp["l0_a_log"] = jnp.log(jax.random.uniform(next(keys), (GDN_HEADS,), jnp.float32, 1.0, 16.0))
    inp["l0_dt_bias"] = dt + jnp.log(-jnp.expm1(-dt))
    inp["l0_onorm_g"] = gain(GDN_DV)
    inp["l0_w_mem_kv"] = nrm((D_MODEL, 2 * MEM_W), D_MODEL ** -0.5)
    inp["l0_w_o"] = nrm((MIX_OUT, D_MODEL), MIX_OUT ** -0.5 * BETA_INIT)
    inp["l0_ln2_g"] = gain(D_MODEL)
    inp["l0_ln2_b"] = bias(D_MODEL)
    inp["l0_ffn2_w_in"] = ffn_in()
    inp["l0_ffn2_w_out"] = ffn_out()
    inp["l0_ln3_g"] = gain(D_MODEL)
    inp["l0_ln3_b"] = bias(D_MODEL)
    inp["l1_ffn1_w_in"] = ffn_in()
    inp["l1_ffn1_w_out"] = ffn_out()
    inp["l1_ln1_g"] = gain(D_MODEL)
    inp["l1_ln1_b"] = bias(D_MODEL)
    inp["l1_w_in"] = nrm((D_MODEL, DSA_IN), D_MODEL ** -0.5)
    inp["l1_kv_norm_g"] = gain(DSA_KV_RANK)
    inp["l1_w_uk"] = nrm((DSA_HEADS, DSA_DH, DSA_KV_RANK), DSA_KV_RANK ** -0.5)
    inp["l1_w_uv"] = nrm((DSA_HEADS, DSA_KV_RANK, DSA_DH), DSA_KV_RANK ** -0.5)
    inp["l1_kidx_ln_g"] = gain(IDX_DIM)
    inp["l1_kidx_ln_b"] = bias(IDX_DIM)
    inp["l1_w_mem_kv"] = nrm((D_MODEL, 2 * MEM_W), D_MODEL ** -0.5)
    inp["l1_w_o"] = nrm((MIX_OUT, D_MODEL), MIX_OUT ** -0.5 * BETA_INIT)
    inp["l1_ln2_g"] = gain(D_MODEL)
    inp["l1_ln2_b"] = bias(D_MODEL)
    inp["l1_ffn2_w_in"] = ffn_in()
    inp["l1_ffn2_w_out"] = ffn_out()
    inp["l1_ln3_g"] = gain(D_MODEL)
    inp["l1_ln3_b"] = bias(D_MODEL)
    return inp

def reference(x, mem,
              l0_ffn1_w_in, l0_ffn1_w_out, l0_ln1_g, l0_ln1_b,
              l0_w_in, l0_conv_w, l0_a_log, l0_dt_bias, l0_onorm_g, l0_w_mem_kv, l0_w_o, l0_ln2_g, l0_ln2_b,
              l0_ffn2_w_in, l0_ffn2_w_out, l0_ln3_g, l0_ln3_b,
              l1_ffn1_w_in, l1_ffn1_w_out, l1_ln1_g, l1_ln1_b,
              l1_w_in, l1_kv_norm_g, l1_w_uk, l1_w_uv, l1_kidx_ln_g, l1_kidx_ln_b, l1_w_mem_kv, l1_w_o,
              l1_ln2_g, l1_ln2_b,
              l1_ffn2_w_in, l1_ffn2_w_out, l1_ln3_g, l1_ln3_b):
    ffn_pre = ((l0_ffn1_w_in, l0_ffn1_w_out, l0_ln1_g, l0_ln1_b),
               (l1_ffn1_w_in, l1_ffn1_w_out, l1_ln1_g, l1_ln1_b))
    mixer_params = ((l0_w_in, l0_conv_w, l0_a_log, l0_dt_bias, l0_onorm_g, l0_w_mem_kv, l0_w_o),
                    (l1_w_in, l1_kv_norm_g, l1_w_uk, l1_w_uv, l1_kidx_ln_g, l1_kidx_ln_b, l1_w_mem_kv, l1_w_o))
    mixer_norm = ((l0_ln2_g, l0_ln2_b), (l1_ln2_g, l1_ln2_b))
    ffn_post = ((l0_ffn2_w_in, l0_ffn2_w_out, l0_ln3_g, l0_ln3_b),
                (l1_ffn2_w_in, l1_ffn2_w_out, l1_ln3_g, l1_ln3_b))
    for i in range(DEPTH):
        w1, w2, g, b = ffn_pre[i]
        x = post_norm_residual(x, 0.5 * swiglu(x, w1, w2), g, b)
        if i % N_MIXERS == 0:
            y = gdn_mixer(x, mem, *mixer_params[i])
        else:
            y = dsa_mixer(x, mem, *mixer_params[i])
        g, b = mixer_norm[i]
        x = post_norm_residual(x, y, g, b)
        w1, w2, g, b = ffn_post[i]
        x = post_norm_residual(x, 0.5 * swiglu(x, w1, w2), g, b)
    return x


_drawn_inputs = setup_inputs


def setup_inputs(seed=0):
    import zlib

    import numpy as np

    out = dict(_drawn_inputs(seed))
    spreads = {}
    factors = {'l0_onorm_g': 40.402,
     'l0_ln2_g': 2.722,
     'l0_ln2_b': 2.842,
     'l0_ln3_g': 23.658,
     'l0_ln3_b': 23.93,
     'mem': 4.161,
     'l0_w_mem_kv': 3.974}
    for name, (base, spread) in spreads.items():
        noise = np.random.default_rng([zlib.crc32(name.encode()), seed]).standard_normal(out[name].shape)
        drawn = base * np.exp(spread * noise) if base else spread * noise
        out[name] = __import__('jax').numpy.asarray(drawn.astype(out[name].dtype))
    for name, factor in factors.items():
        out[name] = (out[name] * factor).astype(out[name].dtype)
    return out
```

```python
from contextlib import ExitStack

import concourse.bass as bass
from concourse import mybir

P = 128
T = 512
D = 1024
F = 2752
KC = D // P
TC = T // P
FC = F // P
FR = F - FC * P
NB_IN = 2 * FC + 1
NB_OUT = FC + 1
RING = 4
ALPHA = 2.0 ** 0.25
LN_EPS = 1e-5

H = 6
G = 2
HG = H // G
TAPS = 4
LEVELS = 7
M = 256
MC = M // P
MDH = 64
NQ, NK, NV, NG = 0, H, 2 * H, 3 * H
NC = 4 * H
NBA = 2 * H

F32 = mybir.dt.float32
F32R = mybir.dt.float32r
ALU = mybir.AluOpType
ACT = mybir.ActivationFunctionType
AX = mybir.AxisListType

FFN1 = 0
MIX = FFN1 + NB_IN + NB_OUT
QM = MIX + NC
KV = QM + 2
WO = KV + 4
FFN2 = WO + KC


def build(nc, a, out):
    with ExitStack() as ctx:
        def sb(name, shape, dt=F32):
            return ctx.enter_context(nc.sbuf_tensor(name, shape, dt))

        def sem(name):
            return ctx.enter_context(nc.semaphore(name))

        w_raw = sb("w_raw", [P, RING, D])
        w_hi = sb("w_hi", [P, RING, D], F32R)
        w_lo = sb("w_lo", [P, RING, D], F32R)
        xT_hi = sb("xT_hi", [P, KC, T], F32R)
        xT_lo = sb("xT_lo", [P, KC, T], F32R)
        ax = sb("ax", [P, TC, D])
        ln_g = sb("ln_g", [P, D])
        ln_b = sb("ln_b", [P, D])
        ident = sb("ident", [P, P])
        ones = sb("ones", [P, P])
        tri = sb("tri", [P, P])
        below = sb("below", [P, P])
        level = sb("level", [P, LEVELS, P])
        eps = sb("eps", [P, 1])
        stats = sb("stats", [P, TC, 2, 6])
        mv = sb("mv", [P, TC, 2])
        std = sb("std", [P, TC])
        rstd = sb("rstd", [P, TC])
        wba = sb("wba", [P, KC, NBA])
        wba_hi = sb("wba_hi", [P, KC, NBA], F32R)
        wba_lo = sb("wba_lo", [P, KC, NBA], F32R)
        conv_rows = sb("conv_rows", [TAPS * 3 * H, P])
        conv_w = sb("conv_w", [P, TAPS, 3 * H])
        onorm = sb("onorm", [P, 1])
        a_log = sb("a_log", [P, H])
        dt_bias = sb("dt_bias", [P, H])
        cols = sb("cols", [P, 29, H * TC])
        small = sb("small", [P, 8, 2])

        zoff = (nc.sbuf_base + 31) // 32 * 32
        sb("fence", [P, 16384 + 65536 + 9216 + 32], mybir.dt.uint8)

        def placed(name, offset, shape, dt=F32):
            return nc.alloc_sbuf_tensor_at(name, shape, dt, offset=zoff + offset)

        z = placed("z", 0, [P, TC, D])
        memT_hi = placed("memT_hi", 0, [P, KC, M], F32R)
        memT_lo = placed("memT_lo", 8192, [P, KC, M], F32R)
        HREG = 16384
        h = placed("h", HREG, [P, FC + 1, T])
        h_hi = placed("h_hi", HREG + 45056, [P, RING, T], F32R)
        h_lo = placed("h_lo", HREG + 53248, [P, RING, T], F32R)
        silu_g = placed("silu_g", HREG + 61440, [P, 2, T])
        chan = placed("chan", HREG, [P, NC, T])
        qm = placed("qm", HREG + 49152, [P, 2, T])
        km = placed("km", HREG + 53248, [P, 2, M])
        vm = placed("vm", HREG + 55296, [P, MC, M])
        sq = placed("sq", HREG + 57344, [P, 2, T])
        prob = placed("prob", HREG + 61440, [P, 2, 2, M])
        EXT = HREG + 65536
        mem_tok = placed("mem_tok", EXT, [P, MC, D])
        probT = placed("probT", EXT, [P, 2, 2 * MC, P])
        UB = HG * P * 4

        def group_buffers(name, offset):
            return [placed(f"{name}{g}", offset + g * UB, [P, HG, P]) for g in range(G)]
        decay = group_buffers("decay", 0)
        amat = group_buffers("amat", 2 * UB)
        qk = group_buffers("qk", 4 * UB)
        qdec = group_buffers("qdec", 6 * UB)
        inv = group_buffers("inv", 8 * UB)
        assert 10 * UB <= 16384
        invT = group_buffers("invT", HREG + 57344)
        quart = group_buffers("quart", HREG + 57344 + 2 * UB)
        assert 57344 + 4 * UB <= 65536
        part = [[placed(f"part{g}{s}", EXT + (2 * g + s) * UB, [P, HG, P]) for s in range(2)] for g in range(G)]
        rhs = group_buffers("rhs", EXT + 4 * UB)
        squares = placed("squares", HREG + 49152, [P, H, P])
        state = sb("state", [P, H, P])
        assert 6 * UB <= 9216

        ps = ctx.enter_context(nc.psum_tensor("ps", [P, 8, T], F32))

        raw_loaded = [sem(f"raw_loaded{i}") for i in range(RING)]
        hi_ready = sem("hi_ready")
        lo_ready = sem("lo_ready")
        block_done = sem("block_done")
        silu_ready = sem("silu_ready")
        h_ready = sem("h_ready")
        h_hi_ready = sem("h_hi_ready")
        h_lo_ready = sem("h_lo_ready")
        acc_done = sem("acc_done")
        stats_ready = sem("stats_ready")
        std_ready = sem("std_ready")
        dve_step = sem("dve_step")
        x_loaded = sem("x_loaded")
        small_loaded = sem("small_loaded")
        mem_loaded = sem("mem_loaded")
        gb_loaded = sem("gb_loaded")
        xtok_ready = sem("xtok_ready")
        ax_ready = sem("ax_ready")
        xT_psum = sem("xT_psum")
        xT_hi_ready = sem("xT_hi_ready")
        xT_lo_ready = sem("xT_lo_ready")
        const_ready = sem("const_ready")
        out_stored = sem("out_stored")
        ba_split = sem("ba_split")
        conv_psum = sem("conv_psum")
        conv_w_ready = sem("conv_w_ready")
        ba_done = sem("ba_done")
        mem_psum = sem("mem_psum")
        memT_hi_ready = sem("memT_hi_ready")
        memT_lo_ready = sem("memT_lo_ready")
        conv_step = sem("conv_step")
        conv_done = sem("conv_done")
        chan_ready = sem("chan_ready")
        gate_ready = sem("gate_ready")
        sq_ready = sem("sq_ready")
        ssq_done = sem("ssq_done")
        scores_done = sem("scores_done")
        negmax_ready = sem("negmax_ready")
        exp_ready = sem("exp_ready")
        prob_ready = sem("prob_ready")
        probT_done = sem("probT_done")
        probT_ready = sem("probT_ready")
        pv_done = sem("pv_done")
        cat_hi_ready = sem("cat_hi_ready")
        cat_lo_ready = sem("cat_lo_ready")
        col_vec = sem("col_vec")
        col_act = sem("col_act")
        g_ready = sem("g_ready")
        gcum_done = sem("gcum_done")
        gcol_ready = sem("gcol_ready")
        grow_done = sem("grow_done")
        kq_done = sem("kq_done")
        vT_done = sem("vT_done")
        dist_ready = sem("dist_ready")
        egrow_ready = sem("egrow_ready")
        decay_ready = sem("decay_ready")
        kdec_ready = sem("kdec_ready")
        vb_ready = sem("vb_ready")
        masks_ready = sem("masks_ready")
        qdec_ready = sem("qdec_ready")
        a_ready = sem("a_ready")
        qk_ready = sem("qk_ready")
        part_ready = sem("part_ready")
        inv_ready = sem("inv_ready")
        quart_done = sem("quart_done")
        quart_ready = sem("quart_ready")
        double_done = sem("double_done")
        ks_done = sem("ks_done")
        rhs_ready = sem("rhs_ready")
        u_done = sem("u_done")
        u_ready = sem("u_ready")
        supd_done = sem("supd_done")
        o_done = sem("o_done")
        state_ready = sem("state_ready")
        o_ready = sem("o_ready")
        on_ready = sem("on_ready")
        oT_done = sem("oT_done")
        oT_ready = sem("oT_ready")

        two_piece = {FFN1 + NB_IN - 1, FFN2 + NB_IN - 1}

        def raw_count(n):
            return 16 * sum(2 if b in two_piece else 1 for b in range(n % RING, n + 1, RING))

        def by_k(n, width=P):
            return w_raw[:, n % RING, :].rearrange("p (k c) -> p k c", k=KC)[:, :, 0:width]

        def h_at(rows, f, i, step):
            return h[0:rows, f, :] if isinstance(i, int) else h[0:rows, bass.ds(f + step * i, 1), :]

        def pair_bank(m):
            return ps[:, 2 * m:2 * m + 2, :].rearrange("p b t -> p (b t)")

        def by_tokens(m):
            return ps[:, 2 * m:2 * m + 2, :].rearrange("p b (k t) -> p (b k) t", t=P)

        def col(j):
            return cols[:, j, :]

        def col_ht(j):
            return cols[:, j, :].rearrange("p (h t) -> p h t", h=H)

        def unit(j, hh, t):
            return cols[:, j, hh * TC + t:hh * TC + t + 1]

        (GA, AA, BC, EA, EB, LNU, U1, EB1, BETA, CORR, RU, SP, DEC, GCUM, GL, DGL, EG, EGL, EDEC,
         KK, R2, RR, BR, BR2, NBG, EPSQ, SS, RO, NEGG) = range(29)

        def bank(g, j):
            return ps[:, 4 * g + j, 0:HG * P]

        def bank3(g, j):
            return bank(g, j).rearrange("p (h c) -> p h c", h=HG)

        def tile(c, t):
            return chan[:, c, t * P:(t + 1) * P]

        def group_tiles(first, g, t):
            return chan[:, first + g * HG:first + (g + 1) * HG, t * P:(t + 1) * P]

        units = [(t, g) for t in range(TC) for g in range(G)]

        def nth(t, g):
            return t * G + g + 1

        def nth_level(t, g, lev, first):
            return (t * (LEVELS - first) + lev - first) * G + g + 1

        block = ctx.enter_context(nc.Block())

        @block.sync
        def _(sp):
            sp.dma_start(z[:, :, :], a["x"][0].rearrange("(m p) d -> p m d", p=P)).then_inc(x_loaded, 16)

            def load(n, dst, src, i=0):
                if n >= RING:
                    sp.wait_ge(hi_ready, n - RING + 1 + RING * i)
                    sp.wait_ge(lo_ready, n - RING + 1 + RING * i)
                sp.dma_start(dst, src).then_inc(raw_loaded[n % RING], 16)

            def ffn_loads(base, w_in, w_out):
                in_cols = w_in.rearrange("(k p) c -> p k c", p=P)
                out_rows = w_out[0:FC * P, :].rearrange("(f p) d -> p f d", p=P)

                def gate_up(b, f, i=0):
                    for j in range(2):
                        n = base + b + j
                        load(n, by_k(n), in_cols[:, :, bass.ds(f * P + j * F, P)], i)
                gate_up(0, 0)
                gate_up(2, 1)
                with sp.Fori(0, FC // 2 - 1) as i:
                    gate_up(4, 2 * i + 2, i)
                    gate_up(6, 2 * i + 3, i)
                gate_up(2 * FC - 2, FC - 1)
                n = base + NB_IN - 1
                load(n, by_k(n, FR), in_cols[:, :, FC * P:F])
                sp.dma_start(w_raw[:, n % RING, :].rearrange("p (k c) -> p k c", k=KC)[:, :, FR:P],
                             in_cols[:, :, F + FC * P:2 * F]).then_inc(raw_loaded[n % RING], 16)
                n = base + NB_IN
                with sp.Fori(0, FC // RING) as i:
                    for j in range(RING):
                        load(n + j, w_raw[:, (n + j) % RING, :], out_rows[:, bass.ds(i * RING + j, 1), :], i)
                for f in range(FC // RING * RING, FC):
                    load(n + f, w_raw[:, (n + f) % RING, :], out_rows[:, f, :])
                load(n + FC, w_raw[0:FR, (n + FC) % RING, :], w_out[FC * P:F, :])

            ffn_loads(FFN1, a["l0_ffn1_w_in"], a["l0_ffn1_w_out"])
            mix_cols = a["l0_w_in"].rearrange("(k p) c -> p k c", p=P)
            with sp.Fori(0, NC // RING) as i:
                for j in range(RING):
                    load(MIX + j, by_k(MIX + j), mix_cols[:, :, bass.ds((i * RING + j) * P, P)], i)
            for j in range(2):
                load(QM + j, by_k(QM + j), mix_cols[:, :, NC * P + NBA + j * P:NC * P + NBA + (j + 1) * P])
            kv_cols = a["l0_w_mem_kv"].rearrange("(k p) c -> p k c", p=P)
            for j in range(4):
                load(KV + j, by_k(KV + j), kv_cols[:, :, j * P:(j + 1) * P])
            o_rows = a["l0_w_o"].rearrange("(k p) d -> p k d", p=P)
            for k in range(KC):
                load(WO + k, w_raw[:, (WO + k) % RING, :], o_rows[:, k, :])
            ffn_loads(FFN2, a["l0_ffn2_w_in"], a["l0_ffn2_w_out"])
            for m in range(TC):
                sp.wait_ge(xtok_ready, 2 * TC + m + 1)
                sp.dma_start(out[0, m * P:(m + 1) * P, :], z[:, m, :]).then_inc(out_stored, 16)
            sp.wait_ge(out_stored, 16 * TC)

        @block.gpsimd
        def _(pool):
            made = [0]

            def step(ins):
                made[0] += 1
                ins.then_inc(const_ready, 1)
                pool.wait_ge(const_ready, made[0])

            step(pool.memset(ident[:, :], 0.0))
            step(pool.affine_select(out=ident[:, :], in_=ident[:, :], compare_op=ALU.not_equal, fill=1.0,
                                    base=0, pattern=[[-1, P]], channel_multiplier=1))
            step(pool.memset(eps[:, :], LN_EPS))
            step(pool.memset(ones[:, :], 1.0))
            pool.dma_start(ln_g[:, :], a["l0_ln1_g"].partition_broadcast(P)).then_inc(gb_loaded, 16)
            pool.dma_start(ln_b[:, :], a["l0_ln1_b"].partition_broadcast(P)).then_inc(gb_loaded, 16)
            pool.dma_start(wba[:, :, :], a["l0_w_in"].rearrange("(k p) c -> p k c", p=P)[:, :, NC * P:NC * P + NBA])\
                .then_inc(small_loaded, 16)
            pool.dma_start(conv_rows[:, :], a["l0_conv_w"].rearrange("j (c p) -> (j c) p", p=P)).then_inc(small_loaded, 16)
            pool.dma_start(onorm[:, :], a["l0_onorm_g"].rearrange("(p o) -> p o", o=1)).then_inc(small_loaded, 16)
            pool.dma_start(a_log[:, :], a["l0_a_log"].partition_broadcast(P)).then_inc(small_loaded, 16)
            pool.dma_start(dt_bias[:, :], a["l0_dt_bias"].partition_broadcast(P)).then_inc(small_loaded, 16)
            pool.dma_start(mem_tok[:, :, :], a["mem"][0].rearrange("(c p) d -> p c d", p=P)).then_inc(mem_loaded, 16)
            step(pool.memset(tri[:, :], 1.0))
            step(pool.affine_select(out=tri[:, :], in_=tri[:, :], compare_op=ALU.is_ge, fill=0.0,
                                    base=0, pattern=[[1, P]], channel_multiplier=-1))
            step(pool.memset(below[:, :], 1.0))
            step(pool.affine_select(out=below[:, :], in_=below[:, :], compare_op=ALU.is_gt, fill=0.0,
                                    base=0, pattern=[[-1, P]], channel_multiplier=1))
            step(pool.memset(level[:, :, :], 0.0))
            for lev in range(LEVELS):
                s = 2 << lev
                view = level[:, lev, :].rearrange("p (b c) -> p b c", c=s)
                step(pool.memset(level[:, lev, :], 1.0))
                step(pool.affine_select(out=view, in_=view, compare_op=ALU.is_ge, fill=0.0, base=0,
                                        pattern=[[-s, P // s], [0, s]], channel_multiplier=1))
                step(pool.affine_select(out=view, in_=view, compare_op=ALU.is_gt, fill=0.0, base=s,
                                        pattern=[[s, P // s], [0, s]], channel_multiplier=-1))
            for lev in range(LEVELS - 1, 0, -1):
                step(pool.tensor_tensor(level[:, lev, :], level[:, lev, :], level[:, lev - 1, :], ALU.subtract))
            step(pool.tensor_tensor(level[:, 0, :], level[:, 0, :], ident[:, :], ALU.subtract))
            step(pool.tensor_tensor(level[:, :, :], level[:, :, :],
                                    below[:, :].unsqueeze(1).to_broadcast([P, LEVELS, P]), ALU.mult))

            def scale_residual(L):
                for m in range(TC):
                    if L == 0:
                        pool.wait_ge(x_loaded, 16)
                    else:
                        pool.wait_ge(xtok_ready, TC * (L - 1) + m + 1)
                    pool.tensor_scalar(ax[:, m, :], z[:, m, :], ALPHA, 1.0, ALU.mult, ALU.mult).then_inc(ax_ready, 1)

            def load_gb(L, g, b):
                pool.wait_ge(xtok_ready, TC * L)
                pool.dma_start(ln_g[:, :], g.partition_broadcast(P)).then_inc(gb_loaded, 16)
                pool.dma_start(ln_b[:, :], b.partition_broadcast(P)).then_inc(gb_loaded, 16)

            scale_residual(0)
            scale_residual(1)
            load_gb(1, a["l0_ln2_g"], a["l0_ln2_b"])
            for c in range(2 * H):
                pool.wait_ge(chan_ready, c + 1)
                if c >= 2:
                    pool.wait_ge(ssq_done, c - 1)
                pool.tensor_tensor(sq[:, c % 2, :], chan[:, c, :], chan[:, c, :], ALU.mult).then_inc(sq_ready, 1)
            pool.wait_ge(small_loaded, 16 * 5)
            for hh in range(H):
                pool.wait_ge(chan_ready, NG + hh + 1)
                pool.tensor_scalar(chan[:, NG + hh, :], chan[:, NG + hh, :], onorm[:, 0:1], 1.0,
                                   ALU.mult, ALU.mult).then_inc(gate_ready, 1)
            def mask3(m):
                return m.unsqueeze(1).to_broadcast([P, HG, P])

            for t in range(TC):
                for g in range(G):
                    pool.wait_ge(decay_ready, nth(t, g))
                    pool.tensor_tensor(amat[g][:, :, :], decay[g][:, :, :], mask3(below[:, :]), ALU.mult)
                    if t:
                        pool.wait_ge(o_done, nth(t - 1, g))
                    pool.tensor_tensor(qk[g][:, :, :], decay[g][:, :, :], mask3(tri[:, :]), ALU.mult).then_inc(masks_ready, 1)
                    pool.wait_ge(egrow_ready, nth(t, g))
                    pool.tensor_tensor(qdec[g][:, :, :], qdec[g][:, :, :], group_tiles(NQ, g, t), ALU.mult).then_inc(qdec_ready, 1)
                for lev in range(LEVELS):
                    for g in range(G):
                        if lev == 0:
                            pool.wait_ge(a_ready, nth(t, g))
                            if t:
                                pool.wait_ge(quart_done, nth_level(t - 1, g, LEVELS - 1, 1))
                        if lev == 2:
                            pool.wait_ge(inv_ready, nth_level(t, g, 0, 0))
                        if lev > 2:
                            pool.wait_ge(quart_done, nth_level(t, g, lev - 2, 1))
                        pool.tensor_tensor(part[g][lev % 2][:, :, :], amat[g][:, :, :], mask3(level[:, lev, :]),
                                           ALU.mult).then_inc(part_ready, 1)
            scale_residual(2)
            load_gb(2, a["l0_ln3_g"], a["l0_ln3_b"])

        @block.scalar
        def _(act):
            def w_split_hi(n, i=0, rows=P):
                act.wait_ge(raw_loaded[n % RING], raw_count(n) + 16 * i)
                if n >= RING:
                    act.wait_ge(block_done, n - RING + 1 + RING * i)
                act.activation(w_hi[0:rows, n % RING, :], w_raw[0:rows, n % RING, :], ACT.Copy).then_inc(hi_ready, 1)

            def transposed_hi(L, m):
                act.wait_ge(xT_psum, TC * L + m + 1)
                act.activation(xT_hi[:, :, m * P:(m + 1) * P], by_tokens(m), ACT.Copy).then_inc(xT_hi_ready, 1)

            def ffn(base, hb):
                def silu(f, i=0, rows=P):
                    act.wait_ge(block_done, base + 2 * f + 1 + RING * i)
                    if f >= 2:
                        act.wait_ge(h_ready, hb + f - 1 + 2 * i)
                    act.activation(silu_g[0:rows, f % 2, :], ps[0:rows, 2 * (f % 2), :], ACT.Silu).then_inc(silu_ready, 1)

                def chunk(f, i=0):
                    w_split_hi(base + 2 * f + 2, i)
                    w_split_hi(base + 2 * f + 3, i)
                    silu(f, i)
                chunk(0)
                chunk(1)
                with act.Fori(0, FC // 2 - 1) as i:
                    chunk(2, i)
                    chunk(3, i)
                w_split_hi(base + 2 * FC)
                silu(FC - 1)
                silu(FC, rows=FR)
                nb = base + NB_IN

                def out_hi(f, i=0, rows=P):
                    n = nb + f
                    w_split_hi(n, i, rows)
                    act.wait_ge(h_ready, hb + f + 1 + RING * i)
                    act.activation(h_hi[0:rows, n % RING, :], h_at(rows, f, i, RING), ACT.Copy).then_inc(h_hi_ready, 1)
                with act.Fori(0, FC // RING) as i:
                    for j in range(RING):
                        out_hi(j, i)
                for f in range(FC // RING * RING, FC):
                    out_hi(f)
                out_hi(FC, rows=FR)

            def layer_norm(L, last=False):
                for m in range(TC):
                    act.wait_ge(stats_ready, TC * (L - 1) + m + 1)
                    act.activation(std[:, m:m + 1], mv[:, m, 1:2], ACT.Sqrt, bias=eps[:, :]).then_inc(std_ready, 1)
                    if not last:
                        transposed_hi(L, m)

            act.wait_ge(const_ready, 3)
            for m in range(TC):
                transposed_hi(0, m)
                if m < 2:
                    w_split_hi(FFN1 + m)
            act.wait_ge(small_loaded, 16 * 5)
            act.activation(wba_hi[:, :, :], wba[:, :, :], ACT.Copy).then_inc(ba_split, 1)
            ffn(FFN1, 0)
            layer_norm(1)

            w_split_hi(MIX)
            w_split_hi(MIX + 1)

            def mem_hi(c):
                act.wait_ge(mem_psum, c + 1)
                if c == 0:
                    act.wait_ge(ax_ready, 2 * TC)
                act.activation(memT_hi[:, :, c * P:(c + 1) * P], by_tokens(3), ACT.Copy).then_inc(memT_hi_ready, 1)

            def channel(c, i=0):
                w_split_hi(MIX + c + 2, i)
                if c < NG:
                    act.wait_ge(conv_done, c + 1 + RING * i)
                    dst = chan[:, c, :] if isinstance(i, int) else chan[:, bass.ds(c + RING * i, 1), :]
                    act.activation(dst, dst, ACT.Silu).then_inc(chan_ready, 1)
                elif c < NC:
                    act.wait_ge(block_done, MIX + c + 1 + RING * i)
                    act.activation(chan[:, c, :], ps[:, c % 4, :], ACT.Silu).then_inc(chan_ready, 1)
                elif c < NC + 2:
                    act.wait_ge(block_done, MIX + c + 1)
                    act.activation(qm[:, c - NC, :], ps[:, c % 4, :], ACT.Copy).then_inc(chan_ready, 1)
            channel(0)
            mem_hi(0)
            channel(1)
            channel(2)
            channel(3)
            mem_hi(1)
            with act.Fori(0, 3) as i:
                for j in range(RING):
                    channel(RING + j, i)
            for c in range(4 * RING, NC + 2):
                channel(c)
            for j in range(4):
                if j < 2:
                    w_split_hi(KV + 2 + j)
                act.wait_ge(block_done, KV + j + 1)
                if j < 2:
                    act.activation(km[:, j, :], ps[:, (NC + 2 + j) % 4, 0:M], ACT.Copy).then_inc(chan_ready, 1)
                else:
                    act.activation(vm[:, :, (j - 2) * P:(j - 1) * P], ps[:, (NC + 2 + j) % 4, 0:M].rearrange("p (c n) -> p c n", c=MC),
                                   ACT.Copy).then_inc(chan_ready, 1)
            for j in range(RING):
                w_split_hi(WO + j)

            def column(dst, src, func, need, scale=1.0):
                act.wait_ge(col_vec, need)
                act.activation(dst, src, func, scale=scale).then_inc(col_act, 1)
            column(col(EA), col(AA), ACT.Exp, 1)
            column(col(EB), col(BC), ACT.Exp, 1, -1.0)
            column(a_log[:, :], a_log[:, :], ACT.Exp, 1)
            column(col(LNU), col(U1), ACT.Ln, 2)
            act.wait_ge(gcol_ready, 1)
            column(col(EG), col(GCUM), ACT.Exp, 2)
            column(col(EGL), col(GL), ACT.Exp, 2)
            column(col(EDEC), col(DGL), ACT.Exp, 2)
            column(col(RR), col(R2), ACT.Sqrt, 3)

            def exps(s):
                act.wait_ge(negmax_ready, s + 1)
                if s >= 2:
                    act.wait_ge(probT_done, s - 1)
                for e in range(2):
                    ins = act.activation(prob[:, s % 2, e, :], ps[:, 4 + 2 * (s % 2) + e, 0:M], ACT.Exp,
                                         bias=small[:, 2 + s % 2, e:e + 1], scale=MDH ** -0.5,
                                         accum_out=small[:, 4 + s % 2, e:e + 1])
                ins.then_inc(exp_ready, 1)
            exps(0)
            for s in range(2 * TC):
                if s + 1 < 2 * TC:
                    exps(s + 1)
                t, hp = divmod(s, 2)
                act.wait_ge(probT_done, s + 1)
                if s >= 2:
                    act.wait_ge(pv_done, s - 1)
                act.activation(probT[:, s % 2, :, :].rearrange("p c n -> p (c n)"), ps[:, 0, :], ACT.Copy).then_inc(probT_ready, 1)
                act.wait_ge(pv_done, s + 1)
                act.activation(xT_hi[:, H + hp, t * P:(t + 1) * P], ps[:, 1, 0:P], ACT.Copy).then_inc(cat_hi_ready, 1)

            act.wait_ge(col_vec, 4)
            for t in range(TC):
                for g in range(G):
                    act.wait_ge(grow_done, nth(t, g))
                    if t:
                        act.wait_ge(o_done, nth(t - 1, g))
                    for j in range(HG):
                        ins = act.activation(decay[g][:, j, :], bank3(g, 0)[:, j, :], ACT.Abs, bias=unit(NEGG, g * HG + j, t))
                    ins.then_inc(dist_ready, 1)
                    act.activation(qdec[g][:, :, :], bank3(g, 0), ACT.Exp).then_inc(egrow_ready, 1)
                    act.wait_ge(dist_ready, nth(t, g))
                    act.activation(decay[g][:, :, :], decay[g][:, :, :], ACT.Exp, scale=-1.0).then_inc(decay_ready, 1)
                for g in range(G):
                    act.wait_ge(kq_done, nth(t, g))
                    act.wait_ge(masks_ready, nth(t, g))
                    for j in range(HG):
                        ins = act.activation(decay[g][:, j, :], bank3(g, 3)[:, j, :], ACT.Copy, scale=unit(EDEC, g * HG + j, t))
                    ins.then_inc(kdec_ready, 1)
                    act.wait_ge(vT_done, nth(t, g))
                    for j in range(HG):
                        ins = act.activation(rhs[g][:, j, :], bank3(g, 0)[:, j, :], ACT.Copy, scale=unit(BR, g * HG + j, t))
                    ins.then_inc(vb_ready, 1)
                for lev in range(1, LEVELS):
                    for g in range(G):
                        act.wait_ge(quart_done, nth_level(t, g, lev, 1))
                        act.activation(quart[g][:, :, :], bank3(g, 1), ACT.Copy).then_inc(quart_ready, 1)
                for g in range(G):
                    act.wait_ge(u_done, nth(t, g))
                    act.activation(quart[g][:, :, :], bank3(g, 1), ACT.Copy).then_inc(u_ready, 1)
                for g in range(G):
                    act.wait_ge(o_done, nth(t, g))
                    if t:
                        act.wait_ge(o_ready, nth(t - 1, g))
                    for j in range(HG):
                        act.activation(squares[:, g * HG + j, :], bank3(g, 3)[:, j, :], ACT.Square, accum_out=unit(SS, g * HG + j, t))
                    act.activation(group_tiles(NV, g, t), bank3(g, 3), ACT.Copy).then_inc(o_ready, 1)
            column(col(RO), col(RO), ACT.Sqrt, 5)
            for hh in range(H):
                act.wait_ge(oT_ready, hh + 1)
                act.activation(xT_hi[:, hh, :], chan[:, NG + hh, :], ACT.Copy).then_inc(cat_hi_ready, 1)
            for k in range(RING, KC):
                w_split_hi(WO + k)
            layer_norm(2)
            w_split_hi(FFN2)
            w_split_hi(FFN2 + 1)
            ffn(FFN2, FC + 1)
            layer_norm(3, last=True)

        @block.vector
        def _(dve):
            steps = [0]

            def then_next(ins):
                steps[0] += 1
                ins.then_inc(dve_step, 1)
                dve.wait_ge(dve_step, steps[0])

            def w_split_lo(n, i=0, rows=P):
                dve.wait_ge(hi_ready, n + 1 + RING * i)
                dve.tensor_tensor(w_lo[0:rows, n % RING, :], w_raw[0:rows, n % RING, :],
                                  w_hi[0:rows, n % RING, :].bitcast(F32), ALU.subtract).then_inc(lo_ready, 1)

            def transposed_lo(L, m):
                dve.wait_ge(xT_hi_ready, TC * L + m + 1)
                dve.tensor_tensor(xT_lo[:, :, m * P:(m + 1) * P], by_tokens(m),
                                  xT_hi[:, :, m * P:(m + 1) * P].bitcast(F32), ALU.subtract).then_inc(xT_lo_ready, 1)

            def ffn(base, hb):
                def gated(f, i=0, rows=P):
                    dve.wait_ge(silu_ready, hb + f + 1 + 2 * i)
                    if rows == P:
                        dve.wait_ge(block_done, base + 2 * f + 2 + RING * i)
                        up = ps[:, 2 * (f % 2) + 1, :]
                    else:
                        up = ps[FR:P, 2 * (f % 2), :]
                    dve.tensor_tensor(h_at(rows, f, i, 2), silu_g[0:rows, f % 2, :], up, ALU.mult).then_inc(h_ready, 1)

                def chunk(f, i=0):
                    w_split_lo(base + 2 * f + 2, i)
                    w_split_lo(base + 2 * f + 3, i)
                    gated(f, i)
                chunk(0)
                chunk(1)
                with dve.Fori(0, FC // 2 - 1) as i:
                    chunk(2, i)
                    chunk(3, i)
                w_split_lo(base + 2 * FC)
                gated(FC - 1)
                gated(FC, rows=FR)
                nb = base + NB_IN

                def out_lo(f, i=0, rows=P):
                    n = nb + f
                    w_split_lo(n, i, rows)
                    dve.wait_ge(h_hi_ready, hb + f + 1 + RING * i)
                    dve.tensor_tensor(h_lo[0:rows, n % RING, :], h_at(rows, f, i, RING),
                                      h_hi[0:rows, n % RING, :].bitcast(F32), ALU.subtract).then_inc(h_lo_ready, 1)
                with dve.Fori(0, FC // RING) as i:
                    for j in range(RING):
                        out_lo(j, i)
                for f in range(FC // RING * RING, FC):
                    out_lo(f)
                out_lo(FC, rows=FR)

            def layer_norm(L, factor, last=False):
                dve.wait_ge(gb_loaded, 32 * L)
                dve.wait_ge(ax_ready, TC * L)
                for m in range(TC):
                    if m < TC - 1:
                        dve.wait_ge(acc_done, (TC - 1) * (L - 1) + m + 1)
                    else:
                        dve.wait_ge(block_done, (FFN1 + NB_IN + NB_OUT, FFN2, FFN2 + NB_IN + NB_OUT)[L - 1])
                    zm = z[:, m, :]
                    then_next(dve.scalar_tensor_tensor(zm, pair_bank(m), factor, ax[:, m, :], ALU.mult, ALU.add))
                    dve.bn_stats(stats[:, m, 0, :], z[:, m, 0:D // 2])
                    then_next(dve.bn_stats(stats[:, m, 1, :], z[:, m, D // 2:D]))
                    dve.bn_aggr(mv[:, m, :], stats[:, m, :, :].rearrange("p a s -> p (a s)")).then_inc(stats_ready, 1)
                    dve.wait_ge(std_ready, TC * (L - 1) + m + 1)
                    then_next(dve.reciprocal(rstd[:, m:m + 1], std[:, m:m + 1]))
                    then_next(dve.tensor_scalar(zm, zm, mv[:, m, 0:1], rstd[:, m:m + 1], ALU.subtract, ALU.mult))
                    then_next(dve.tensor_tensor(zm, zm, ln_g[:, :], ALU.mult))
                    dve.tensor_tensor(zm, zm, ln_b[:, :], ALU.add).then_inc(xtok_ready, 1)
                    if not last:
                        transposed_lo(L, m)

            for m in range(TC):
                transposed_lo(0, m)
                if m < 2:
                    w_split_lo(FFN1 + m)
            dve.wait_ge(ba_split, 1)
            dve.tensor_tensor(wba_lo[:, :, :], wba[:, :, :], wba_hi[:, :, :].bitcast(F32), ALU.subtract).then_inc(ba_split, 1)
            ffn(FFN1, 0)
            layer_norm(1, 0.5)

            w_split_lo(MIX)
            w_split_lo(MIX + 1)
            dve.wait_ge(conv_psum, 1)
            then_next(dve.tensor_copy(conv_w[:, :, :].rearrange("p j c -> p (j c)"), ps[:, 5, 0:TAPS * 3 * H]))
            dve.wait_ge(ba_done, 1)
            ba = ps[:, 4, 0:TC * NBA].rearrange("p (t w h) -> p w h t", t=TC, w=2)
            dve.tensor_copy(col_ht(BC), ba[:, 0])
            then_next(dve.tensor_tensor(col_ht(GA), ba[:, 1], dt_bias[:, :].unsqueeze(2).to_broadcast([P, H, TC]), ALU.add))
            dve.scalar_tensor_tensor(col(AA), col(GA), -1.0, col(GA), ALU.mult, ALU.min).then_inc(col_vec, 1)

            def mem_lo(c):
                dve.wait_ge(memT_hi_ready, c + 1)
                dve.tensor_tensor(memT_lo[:, :, c * P:(c + 1) * P], by_tokens(3),
                                  memT_hi[:, :, c * P:(c + 1) * P].bitcast(F32), ALU.subtract).then_inc(memT_lo_ready, 1)

            def conv(c, i=0):
                w_split_lo(MIX + c + 2, i)
                if c >= NG:
                    return
                dve.wait_ge(block_done, MIX + c + 1 + RING * i)
                at = c if isinstance(i, int) else bass.ds(c + RING * i, 1)

                def y(s):
                    return chan[:, at, s:T]

                def tap(j):
                    return conv_w[:, j, c:c + 1] if isinstance(i, int) else conv_w[:, j, bass.ds(c + RING * i, 1)]
                for s in range(TAPS):
                    src = ps[:, c % 4, 0:T - s]
                    if s == 0:
                        ins = dve.tensor_scalar(y(0), src, tap(TAPS - 1), None, ALU.mult)
                    else:
                        dve.wait_ge(conv_step, (TAPS - 1) * (c + (0 if isinstance(i, int) else RING * i)) + s)
                        ins = dve.scalar_tensor_tensor(y(s), src, tap(TAPS - 1 - s), y(s), ALU.mult, ALU.add)
                    ins.then_inc(conv_step if s < TAPS - 1 else conv_done, 1)
            conv(0)
            mem_lo(0)
            conv(1)
            conv(2)
            conv(3)
            mem_lo(1)
            with dve.Fori(0, 3) as i:
                for j in range(RING):
                    conv(RING + j, i)
            for c in range(4 * RING, NC + 2):
                conv(c)
            for j in range(2):
                w_split_lo(KV + 2 + j)
            for j in range(RING):
                w_split_lo(WO + j)

            dve.wait_ge(col_act, 3)
            dve.tensor_scalar(col(U1), col(EA), 1.0, None, ALU.add).then_inc(col_vec, 1)
            then_next(dve.tensor_scalar(col(EB1), col(EB), 1.0, None, ALU.add))
            then_next(dve.reciprocal(col(BETA), col(EB1)))
            then_next(dve.scalar_tensor_tensor(col(CORR), col(U1), 1.0, col(EA), ALU.subtract, ALU.subtract))
            then_next(dve.reciprocal(col(RU), col(U1)))
            then_next(dve.tensor_tensor(col(CORR), col(CORR), col(RU), ALU.mult))
            dve.wait_ge(col_act, 4)
            then_next(dve.tensor_tensor(col(SP), col(LNU), col(CORR), ALU.subtract))
            then_next(dve.scalar_tensor_tensor(col(SP), col(GA), 0.0, col(SP), ALU.max, ALU.add))
            dve.scalar_tensor_tensor(col_ht(DEC), col_ht(SP), -1.0, a_log[:, :].unsqueeze(2).to_broadcast([P, H, TC]),
                                     ALU.mult, ALU.mult).then_inc(g_ready, 1)
            dve.wait_ge(gcum_done, 1)
            dve.tensor_copy(col(GCUM), ps[:, 4, 64:64 + H * TC])
            then_next(dve.tensor_copy(col(GL), ps[:, 4, 96:96 + H * TC]))
            dve.tensor_scalar(col(NEGG), col(GCUM), -1.0, None, ALU.mult)
            dve.tensor_tensor(col(DGL), col(GL), col(GCUM), ALU.subtract).then_inc(gcol_ready, 1)
            dve.wait_ge(ssq_done, 2 * H)
            ssq = ps[:, 5, 128:128 + 2 * H * TC]
            then_next(dve.tensor_scalar(col(KK), ssq[:, H * TC:2 * H * TC], 1e-6, None, ALU.add))
            dve.reciprocal(col(R2), col(KK)).then_inc(col_vec, 1)
            then_next(dve.tensor_scalar(col(EPSQ), ssq[:, 0:H * TC], 1e-6, LN_EPS * P, ALU.add, ALU.mult))
            dve.wait_ge(col_act, 8)
            dve.tensor_tensor(col(BR), col(BETA), col(RR), ALU.mult)
            then_next(dve.tensor_tensor(col(BR2), col(BETA), col(R2), ALU.mult))
            dve.scalar_tensor_tensor(col(NBG), col(BR2), -1.0, col(EG), ALU.mult, ALU.mult).then_inc(col_vec, 1)

            def negmax(s):
                dve.wait_ge(scores_done, s + 1)
                if s >= 2:
                    dve.wait_ge(exp_ready, s - 1)
                then_next(dve.tensor_reduce(small[:, 6 + s % 2, :], ps[:, 4 + 2 * (s % 2):6 + 2 * (s % 2), 0:M],
                                            AX.X, ALU.max))
                dve.tensor_scalar(small[:, 2 + s % 2, :], small[:, 6 + s % 2, :], -(MDH ** -0.5), None, ALU.mult)\
                    .then_inc(negmax_ready, 1)
            negmax(0)
            for s in range(2 * TC):
                if s + 1 < 2 * TC:
                    negmax(s + 1)
                t, hp = divmod(s, 2)
                dve.wait_ge(exp_ready, s + 1)
                then_next(dve.reciprocal(small[:, 4 + s % 2, :], small[:, 4 + s % 2, :]))
                for e in range(2):
                    ins = dve.tensor_scalar(prob[:, s % 2, e, :], prob[:, s % 2, e, :], small[:, 4 + s % 2, e:e + 1], None, ALU.mult)
                ins.then_inc(prob_ready, 1)
                dve.wait_ge(cat_hi_ready, s + 1)
                dve.tensor_tensor(xT_lo[:, H + hp, t * P:(t + 1) * P], ps[:, 1, 0:P],
                                  xT_hi[:, H + hp, t * P:(t + 1) * P].bitcast(F32), ALU.subtract).then_inc(cat_lo_ready, 1)

            for t in range(TC):
                for g in range(G):
                    dve.wait_ge(kq_done, nth(t, g))
                    dve.wait_ge(masks_ready, nth(t, g))
                    for j in range(HG):
                        ins = dve.scalar_tensor_tensor(amat[g][:, j, :], bank3(g, 1)[:, j, :], unit(BR2, g * HG + j, t),
                                                       amat[g][:, j, :], ALU.mult, ALU.mult)
                    ins.then_inc(a_ready, 1)
                    dve.tensor_tensor(qk[g][:, :, :], bank3(g, 2), qk[g][:, :, :], ALU.mult).then_inc(qk_ready, 1)
                for g in range(G):
                    dve.wait_ge(part_ready, nth_level(t, g, 0, 0))
                    then_next(dve.tensor_tensor(inv[g][:, :, :], ident[:, :].unsqueeze(1).to_broadcast([P, HG, P]),
                                                part[g][0][:, :, :], ALU.subtract))
                    if t:
                        dve.wait_ge(u_done, nth(t - 1, g))
                    dve.transpose(invT[g][:, :, :].rearrange("p h c -> p (h c)"), inv[g][:, :, :].rearrange("p h c -> p (h c)"))\
                        .then_inc(inv_ready, 1)
                for lev in range(1, LEVELS):
                    for g in range(G):
                        dve.wait_ge(double_done, nth_level(t, g, lev, 1))
                        ins = dve.tensor_tensor(invT[g][:, :, :], invT[g][:, :, :], bank3(g, 2), ALU.subtract)
                        if lev < LEVELS - 1:
                            ins = dve.tensor_tensor(inv[g][:, :, :], inv[g][:, :, :], bank3(g, 3), ALU.subtract)
                        ins.then_inc(inv_ready, 1)
                if t:
                    for g in range(G):
                        dve.wait_ge(ks_done, nth(t - 1, g))
                        dve.wait_ge(vb_ready, nth(t, g))
                        for j in range(HG):
                            ins = dve.scalar_tensor_tensor(rhs[g][:, j, :], bank3(g, 0)[:, j, :], unit(NBG, g * HG + j, t),
                                                           rhs[g][:, j, :], ALU.mult, ALU.add)
                        ins.then_inc(rhs_ready, 1)
                if t < TC - 1:
                    for g in range(G):
                        dve.wait_ge(supd_done, nth(t, g))
                        dve.wait_ge(o_done, nth(t, g))
                        if t == 0:
                            ins = dve.tensor_copy(state[:, g * HG:(g + 1) * HG, :], bank3(g, 2))
                        else:
                            for j in range(HG):
                                ins = dve.scalar_tensor_tensor(state[:, g * HG + j, :], state[:, g * HG + j, :], unit(EGL, g * HG + j, t),
                                                               bank3(g, 2)[:, j, :], ALU.mult, ALU.add)
                        ins.then_inc(state_ready, 1)
            dve.wait_ge(o_ready, nth(TC - 1, G - 1))
            dve.scalar_tensor_tensor(col(RO), col(SS), 1.0 / P, col(EPSQ), ALU.mult, ALU.add).then_inc(col_vec, 1)
            dve.wait_ge(col_act, 9)
            then_next(dve.reciprocal(col(RO), col(RO)))
            for hh in range(H):
                for t in range(TC):
                    ins = dve.tensor_scalar(tile(NV + hh, t), tile(NV + hh, t), unit(RO, hh, t), None, ALU.mult)
                ins.then_inc(on_ready, 1)
            dve.wait_ge(gate_ready, H)
            for hh in range(H):
                dve.wait_ge(oT_done, hh + 1)
                dve.tensor_tensor(chan[:, NG + hh, :], chan[:, NG + hh, :], ps[:, hh, :], ALU.mult).then_inc(oT_ready, 1)
                dve.wait_ge(cat_hi_ready, 2 * TC + hh + 1)
                dve.tensor_tensor(xT_lo[:, hh, :], chan[:, NG + hh, :], xT_hi[:, hh, :].bitcast(F32), ALU.subtract)\
                    .then_inc(cat_lo_ready, 1)
            for k in range(RING, KC):
                w_split_lo(WO + k)
            layer_norm(2, 1.0)
            w_split_lo(FFN2)
            w_split_lo(FFN2 + 1)
            ffn(FFN2, FC + 1)
            layer_norm(3, 0.5, last=True)

        @block.tensor
        def _(pe):
            def transposes(L, m):
                for k in range(KC):
                    mm = pe.transpose(by_tokens(m)[:, k, :], z[:, m, k * P:(k + 1) * P], ident[:, :])
                mm.then_inc(xT_psum, 1)

            def split_mms(dst, w, x, first=True, last=True):
                pe.matmul(dst, w[0], x[0], start=first, stop=False)
                pe.matmul(dst, w[0], x[1], start=False, stop=False)
                return pe.matmul(dst, w[1], x[0], start=False, stop=last)

            def block_ready(n, i=0):
                pe.wait_ge(hi_ready, n + 1 + RING * i)
                pe.wait_ge(lo_ready, n + 1 + RING * i)

            def project(n, bank, i=0):
                block_ready(n, i)
                s = n % RING
                for k in range(KC):
                    ks = slice(k * P, (k + 1) * P)
                    mm = split_mms(ps[:, bank, :], (w_hi[:, s, ks], w_lo[:, s, ks]), (xT_hi[:, k, :], xT_lo[:, k, :]),
                                   k == 0, k == KC - 1)
                mm.then_inc(block_done, 1)

            def out_mms(n, m, acts, first, last, rows=P):
                s = n % RING
                hi, lo = acts
                for x, w in ((hi, w_hi), (hi, w_lo), (lo, w_hi)):
                    for b in range(2):
                        mm = pe.matmul(ps[:, 2 * m + b, :], x[:, m * P:(m + 1) * P], w[0:rows, s, b * T:(b + 1) * T],
                                       start=first and x is hi and w is w_hi, stop=last and x is lo)
                return mm

            def finish(n0, count, acts, rows_last=P):
                for m in range(TC):
                    for b in range(count):
                        lastb = b == count - 1
                        mm = out_mms(n0 + b, m, acts(b), False, lastb, rows_last if lastb else P)
                        if m == TC - 1:
                            mm.then_inc(block_done, 1)
                    if m < TC - 1:
                        mm.then_inc(acc_done, 1)

            def ffn(base, hb):
                def chunk(f, i=0):
                    if f >= 2:
                        pe.wait_ge(silu_ready, hb + f - 1 + 2 * i)
                    project(base + 2 * f, 2 * (f % 2), i)
                    if f >= 2:
                        pe.wait_ge(h_ready, hb + f - 1 + 2 * i)
                    project(base + 2 * f + 1, 2 * (f % 2) + 1, i)
                chunk(0)
                chunk(1)
                with pe.Fori(0, FC // 2 - 1) as i:
                    chunk(2, i)
                    chunk(3, i)
                chunk(FC - 1)
                pe.wait_ge(h_ready, hb + FC - 1)
                project(base + NB_IN - 1, 2 * (FC % 2))
                nb = base + NB_IN

                def acts(f, rows=P):
                    s = (nb + f) % RING
                    return h_hi[0:rows, s, :], h_lo[0:rows, s, :]

                def out_block(f, i=0, first=False):
                    block_ready(nb + f, i)
                    pe.wait_ge(h_lo_ready, hb + f + 1 + RING * i)
                    for m in range(TC):
                        mm = out_mms(nb + f, m, acts(f), first, False)
                    mm.then_inc(block_done, 1)
                pe.wait_ge(h_ready, hb + FC + 1)
                for f in range(RING):
                    out_block(f, first=(f == 0))
                with pe.Fori(0, FC // RING - 2) as i:
                    for j in range(RING):
                        out_block(RING + j, i)
                for f in range(RING * (FC // RING - 1), FC + 1 - RING):
                    out_block(f)
                block_ready(nb + FC)
                pe.wait_ge(h_lo_ready, hb + FC + 1)
                f0 = FC + 1 - RING
                finish(nb + f0, RING, lambda b: acts(f0 + b, P if f0 + b < FC else FR), FR)

            def next_x(L):
                for m in range(TC):
                    if L:
                        pe.wait_ge(xtok_ready, TC * (L - 1) + m + 1)
                    transposes(L, m)
                pe.wait_ge(xT_lo_ready, TC * (L + 1))

            pe.wait_ge(x_loaded, 16)
            pe.wait_ge(const_ready, 2)
            next_x(0)
            ffn(FFN1, 0)
            next_x(1)

            pe.wait_ge(ba_split, 2)
            pe.wait_ge(const_ready, 4)
            pe.transpose(ps[:, 5, 0:TAPS * 3 * H], conv_rows[:, :], ident[0:TAPS * 3 * H, 0:TAPS * 3 * H]).then_inc(conv_psum, 1)
            for t in range(TC):
                for k in range(KC):
                    ts = slice(t * P, (t + 1) * P)
                    mm = split_mms(ps[:, 4, t * NBA:(t + 1) * NBA], (xT_hi[:, k, ts], xT_lo[:, k, ts]),
                                   (wba_hi[:, k, :], wba_lo[:, k, :]), k == 0, k == KC - 1)
            mm.then_inc(ba_done, 1)

            def mem_transposes(c):
                if c == 0:
                    pe.wait_ge(mem_loaded, 16)
                else:
                    pe.wait_ge(memT_lo_ready, c)
                for k in range(KC):
                    mm = pe.transpose(by_tokens(3)[:, k, :], mem_tok[:, c, k * P:(k + 1) * P], ident[:, :])
                mm.then_inc(mem_psum, 1)

            def sums(c, i=0):
                pe.wait_ge(sq_ready, c + 1 + RING * i)
                for t in range(TC):
                    at = 128 + c * TC + t
                    dst = ps[:, 5, at:at + 1] if isinstance(i, int) else ps[:, 5, bass.ds(at + RING * TC * i, 1)]
                    mm = pe.matmul(dst, sq[:, c % 2, t * P:(t + 1) * P], ones[:, 0:1], start=True, stop=True)
                mm.then_inc(ssq_done, 1)

            def channel(c, i=0):
                if c >= RING:
                    pe.wait_ge(chan_ready, c - RING + 1 + RING * i)
                project(MIX + c, c % 4, i)
            mem_transposes(0)
            channel(0)
            channel(1)
            mem_transposes(1)
            for c in (2, 3):
                channel(c)
                sums(c - 2)
            with pe.Fori(0, 2) as i:
                for j in range(RING):
                    channel(RING + j, i)
                    sums(RING + j - 2, i)
            for c in range(3 * RING, NC + 2):
                channel(c)
                if c - 2 < 2 * H:
                    sums(c - 2)
            pe.wait_ge(memT_lo_ready, 2)
            for j in range(4):
                n = KV + j
                b = (NC + 2 + j) % 4
                pe.wait_ge(chan_ready, NC + 2 + j - RING + 1)
                block_ready(n)
                s = n % RING
                if j < 2:
                    for k in range(KC):
                        ks = slice(k * P, (k + 1) * P)
                        mm = split_mms(ps[:, b, 0:M], (w_hi[:, s, ks], w_lo[:, s, ks]),
                                       (memT_hi[:, k, :], memT_lo[:, k, :]), k == 0, k == KC - 1)
                else:
                    for c in range(MC):
                        for k in range(KC):
                            ks, cs = slice(k * P, (k + 1) * P), slice(c * P, (c + 1) * P)
                            mm = split_mms(ps[:, b, cs], (memT_hi[:, k, cs], memT_lo[:, k, cs]),
                                           (w_hi[:, s, ks], w_lo[:, s, ks]), k == 0, k == KC - 1)
                mm.then_inc(block_done, 1)
            pe.wait_ge(g_ready, 1)
            pe.wait_ge(const_ready, 6)
            pe.matmul(ps[:, 4, 64:64 + H * TC], tri[:, :], col(DEC), start=True, stop=True)
            pe.matmul(ps[:, 4, 96:96 + H * TC], ones[:, :], col(DEC), start=True, stop=True).then_inc(gcum_done, 1)

            def scores(s):
                t, hp = divmod(s, 2)
                if s >= 2:
                    pe.wait_ge(exp_ready, s - 1)
                for e in range(2):
                    rows = slice(e * MDH, (e + 1) * MDH)
                    mm = pe.matmul(ps[:, 4 + 2 * (s % 2) + e, 0:M], qm[rows, hp, t * P:(t + 1) * P], km[rows, hp, :],
                                   start=True, stop=True)
                mm.then_inc(scores_done, 1)
            pe.wait_ge(chan_ready, NC + 6)
            pe.wait_ge(gcol_ready, 1)
            pe.wait_ge(col_vec, 4)
            scores(0)
            scores(1)
            for s in range(2 * TC):
                t, hp = divmod(s, 2)
                pe.wait_ge(prob_ready, s + 1)
                if s:
                    pe.wait_ge(probT_ready, s)
                for e in range(2):
                    for c in range(MC):
                        q = e * MC + c
                        mm = pe.transpose(ps[:, 0, q * P:(q + 1) * P], prob[:, s % 2, e, c * P:(c + 1) * P], ident[:, :])
                mm.then_inc(probT_done, 1)
                if s + 2 < 2 * TC:
                    scores(s + 2)
                pe.wait_ge(probT_ready, s + 1)
                if s:
                    pe.wait_ge(cat_lo_ready, s)
                for e in range(2):
                    for c in range(MC):
                        mm = pe.matmul(ps[e * MDH:(e + 1) * MDH, 1, 0:P], vm[:, c, (2 * hp + e) * MDH:(2 * hp + e + 1) * MDH],
                                       probT[:, s % 2, e * MC + c, :], start=(c == 0), stop=(c == MC - 1))
                mm.then_inc(pv_done, 1)
            pe.wait_ge(cat_lo_ready, 2 * TC)

            for t in range(TC):
                for g in range(G):
                    if t == 1:
                        pe.wait_ge(vb_ready, nth(0, g))
                    if t > 1:
                        pe.wait_ge(rhs_ready, nth(t - 2, g))
                    for j in range(HG):
                        mm = pe.matmul(bank3(g, 0)[:, j, :], unit(DEC, g * HG + j, t).to_broadcast([P, P]), tri[:, :],
                                       start=True, stop=True)
                    mm.then_inc(grow_done, 1)
                for g in range(G):
                    if t:
                        pe.wait_ge(u_ready, nth(t - 1, g))
                        pe.wait_ge(state_ready, nth(t - 1, g))
                        pe.wait_ge(o_ready, nth(t - 1, g))
                    for j in range(HG):
                        hh = g * HG + j
                        pe.matmul(bank3(g, 1)[:, j, :], tile(NK + hh, t), tile(NK + hh, t), start=True, stop=True)
                        pe.matmul(bank3(g, 2)[:, j, :], tile(NK + hh, t), tile(NQ + hh, t), start=True, stop=True)
                        mm = pe.transpose(bank3(g, 3)[:, j, :], tile(NK + hh, t), ident[:, :])
                    mm.then_inc(kq_done, 1)
                    pe.wait_ge(dist_ready, nth(t, g))
                    pe.wait_ge(egrow_ready, nth(t, g))
                    for j in range(HG):
                        mm = pe.transpose(bank3(g, 0)[:, j, :], tile(NV + g * HG + j, t), ident[:, :])
                    mm.then_inc(vT_done, 1)
                for g in range(G):
                    pe.wait_ge(a_ready, nth(t, g))
                    pe.wait_ge(qk_ready, nth(t, g))
                    pe.wait_ge(kdec_ready, nth(t, g))
                for lev in range(1, LEVELS):
                    for g in range(G):
                        pe.wait_ge(inv_ready, nth_level(t, g, lev - 1, 0))
                        pe.wait_ge(part_ready, nth_level(t, g, lev, 0))
                        for j in range(HG):
                            mm = pe.matmul(bank3(g, 1)[:, j, :], part[g][lev % 2][:, j, :], invT[g][:, j, :], start=True, stop=True)
                        mm.then_inc(quart_done, 1)
                    for g in range(G):
                        pe.wait_ge(quart_ready, nth_level(t, g, lev, 1))
                        for j in range(HG):
                            mm = pe.matmul(bank3(g, 2)[:, j, :], inv[g][:, j, :], quart[g][:, j, :], start=True, stop=True)
                        if lev < LEVELS - 1:
                            for j in range(HG):
                                mm = pe.matmul(bank3(g, 3)[:, j, :], quart[g][:, j, :], inv[g][:, j, :], start=True, stop=True)
                        mm.then_inc(double_done, 1)
                if t:
                    for g in range(G):
                        pe.wait_ge(vb_ready, nth(t, g))
                        for j in range(HG):
                            hh = g * HG + j
                            mm = pe.matmul(bank3(g, 0)[:, j, :], tile(NK + hh, t), state[:, hh, :], start=True, stop=True)
                        mm.then_inc(ks_done, 1)
                for g in range(G):
                    pe.wait_ge(inv_ready, nth_level(t, g, LEVELS - 1, 0))
                    if t:
                        pe.wait_ge(rhs_ready, nth(t - 1, g))
                    else:
                        pe.wait_ge(vb_ready, nth(t, g))
                    for j in range(HG):
                        mm = pe.matmul(bank3(g, 1)[:, j, :], invT[g][:, j, :], rhs[g][:, j, :], start=True, stop=True)
                    mm.then_inc(u_done, 1)
                for g in range(G):
                    pe.wait_ge(u_ready, nth(t, g))
                    if t < TC - 1:
                        for j in range(HG):
                            mm = pe.matmul(bank3(g, 2)[:, j, :], decay[g][:, j, :], quart[g][:, j, :], start=True, stop=True)
                        mm.then_inc(supd_done, 1)
                    pe.wait_ge(qdec_ready, nth(t, g))
                    for j in range(HG):
                        hh = g * HG + j
                        if t:
                            pe.matmul(bank3(g, 3)[:, j, :], qdec[g][:, j, :], state[:, hh, :], start=True, stop=False)
                        mm = pe.matmul(bank3(g, 3)[:, j, :], qk[g][:, j, :], quart[g][:, j, :], start=(t == 0), stop=True)
                    mm.then_inc(o_done, 1)
            pe.wait_ge(o_ready, nth(TC - 1, G - 1))
            for hh in range(H):
                pe.wait_ge(on_ready, hh + 1)
                for t in range(TC):
                    mm = pe.transpose(ps[:, hh, t * P:(t + 1) * P], tile(NV + hh, t), ident[:, :])
                mm.then_inc(oT_done, 1)
            pe.wait_ge(cat_lo_ready, 2 * TC + H)

            def heads(k):
                return xT_hi[:, k, :], xT_lo[:, k, :]
            for k in range(RING):
                block_ready(WO + k)
                for m in range(TC):
                    mm = out_mms(WO + k, m, heads(k), k == 0, False)
                mm.then_inc(block_done, 1)
            block_ready(WO + KC - 1)
            finish(WO + RING, RING, lambda b: heads(RING + b))
            next_x(2)
            ffn(FFN2, FC + 1)


_INS = ["x", "mem", "l0_ffn1_w_in", "l0_ffn1_w_out", "l0_ln1_g", "l0_ln1_b", "l0_w_in", "l0_conv_w", "l0_a_log",
        "l0_dt_bias", "l0_onorm_g", "l0_w_mem_kv", "l0_w_o", "l0_ln2_g", "l0_ln2_b", "l0_ffn2_w_in", "l0_ffn2_w_out",
        "l0_ln3_g", "l0_ln3_b"]


def kernel(**inputs):
    import numpy as np
    import concourse.bacc as bacc
    from concourse.bass_utils import run_bass_kernel_spmd

    nc = bacc.Bacc("TRN2", target_bir_lowering=False, num_devices=1)
    arrays, aps = {}, {}
    for name in _INS:
        v = np.ascontiguousarray(inputs[name])
        arrays[name + "_dram"] = v
        aps[name] = nc.dram_tensor(name + "_dram", v.shape, mybir.dt.from_np(v.dtype), kind="ExternalInput").ap()
    out = nc.dram_tensor("out_dram", (1, T, D), F32, kind="ExternalOutput").ap()
    build(nc, aps, out)
    r = run_bass_kernel_spmd(nc, [arrays], core_ids=[0])
    return r.results[0]["out_dram"]
```

```python
from contextlib import ExitStack

import concourse.bass as bass
from concourse import mybir

P = 128
T = 512
D = 1024
F = 2752
KC = D // P
TC = T // P
FC = F // P
FR = F - FC * P
NB_IN = 2 * FC + 1
NB_OUT = FC + 1
RING = 4
ALPHA = 2.0 ** 0.25
LN_EPS = 1e-5

H = 6
G = 2
HG = H // G
TAPS = 4
LEVELS = 7
M = 256
MC = M // P
MDH = 64
NQ, NK, NV, NG = 0, H, 2 * H, 3 * H
NC = 4 * H
HP = 2
NBA = 2 * H

F32 = mybir.dt.float32
F32R = mybir.dt.float32r
ALU = mybir.AluOpType
ACT = mybir.ActivationFunctionType
AX = mybir.AxisListType

FFN1 = 0
MIX = FFN1 + NB_IN + NB_OUT
GATE = MIX
QM = GATE + H
KV = QM + HP
QKV = KV + 2 * HP
WO = QKV + 3 * H
FFN2 = WO + KC


def build(nc, a, out):
    with ExitStack() as ctx:
        def sb(name, shape, dt=F32):
            return ctx.enter_context(nc.sbuf_tensor(name, shape, dt))

        def sem(name):
            return ctx.enter_context(nc.semaphore(name))

        w_raw = sb("w_raw", [P, RING, D])
        w_hi = sb("w_hi", [P, RING, D], F32R)
        w_lo = sb("w_lo", [P, RING, D], F32R)
        xT_hi = sb("xT_hi", [P, KC, T], F32R)
        xT_lo = sb("xT_lo", [P, KC, T], F32R)
        ax = sb("ax", [P, TC, D])
        ln_g = sb("ln_g", [P, D])
        ln_b = sb("ln_b", [P, D])
        ident = sb("ident", [P, P])
        ones = sb("ones", [P, P])
        tri = sb("tri", [P, P])
        below = sb("below", [P, P])
        level = sb("level", [P, LEVELS, P])
        eps = sb("eps", [P, 1])
        stats = sb("stats", [P, TC, 2, 6])
        mv = sb("mv", [P, TC, 2])
        std = sb("std", [P, TC])
        rstd = sb("rstd", [P, TC])
        shift = sb("shift", [P, TC])
        wba = sb("wba", [P, KC, NBA])
        wba_hi = sb("wba_hi", [P, KC, NBA], F32R)
        wba_lo = sb("wba_lo", [P, KC, NBA], F32R)
        conv_rows = sb("conv_rows", [TAPS * 3 * H, P])
        conv_w = sb("conv_w", [P, TAPS, 3 * H])
        onorm = sb("onorm", [P, 1])
        a_log = sb("a_log", [P, H])
        dt_bias = sb("dt_bias", [P, H])
        cols = sb("cols", [P, 29, H * TC])
        neg_max = sb("neg_max", [P, 2, 2 * HP])
        prob_sum = sb("prob_sum", [P, 2 * HP])
        qm_now = sb("qm_now", [P, HP, P])

        zoff = (nc.sbuf_base + 31) // 32 * 32
        sb("fence", [P, 16384 + 65536 + 9216 + 32], mybir.dt.uint8)

        def placed(name, offset, shape, dt=F32):
            return nc.alloc_sbuf_tensor_at(name, shape, dt, offset=zoff + offset)

        z = placed("z", 0, [P, TC, D])
        memT_hi = placed("memT_hi", 0, [P, KC, M], F32R)
        memT_lo = placed("memT_lo", 8192, [P, KC, M], F32R)
        HREG = 16384
        h = placed("h", HREG, [P, FC + 1, T])
        h_hi = placed("h_hi", HREG + 45056, [P, RING, T], F32R)
        h_lo = placed("h_lo", HREG + 53248, [P, RING, T], F32R)
        silu_g = placed("silu_g", HREG + 61440, [P, 2, T])
        chan = placed("chan", HREG, [P, NC, T])
        qm = placed("qm", HREG + 49152, [P, 2, T])
        km = placed("km", HREG + 53248, [P, 2, M])
        vm = placed("vm", HREG + 55296, [P, MC, M])
        sq = placed("sq", HREG + 57344, [P, 2, T])
        prob = placed("prob", HREG + 61440, [P, 2 * HP, M])
        ba_rows = placed("ba_rows", HREG + 61440, [NBA, T])
        EXT = HREG + 65536
        mem_tok = placed("mem_tok", EXT, [P, MC, D])
        probT = placed("probT", EXT, [P, 2 * HP * MC, P])
        UB = HG * P * 4

        def group_buffers(name, offset):
            return [placed(f"{name}{g}", offset + g * UB, [P, HG, P]) for g in range(G)]
        kdec = group_buffers("kdec", 0)
        amat = group_buffers("amat", 2 * UB)
        qk = group_buffers("qk", 4 * UB)
        qdec = group_buffers("qdec", 6 * UB)
        inv = group_buffers("inv", 8 * UB)
        assert 10 * UB <= 16384
        invT = group_buffers("invT", HREG + 57344)
        quart = group_buffers("quart", HREG + 57344 + 2 * UB)
        assert 57344 + 4 * UB <= 65536
        part = [[placed(f"part{g}{s}", EXT + (2 * g + s) * UB, [P, HG, P]) for s in range(2)] for g in range(G)]
        rhs = group_buffers("rhs", EXT + 4 * UB)
        squares = placed("squares", HREG + 49152, [P, HG, P])
        decay = group_buffers("decay", HREG + 49152 + 4096)
        assert 4096 + 2 * UB <= 8192
        state = sb("state", [P, H, P])
        assert 6 * UB <= 9216

        ps = ctx.enter_context(nc.psum_tensor("ps", [P, 8, T], F32))

        raw_loaded = [sem(f"raw_loaded{i}") for i in range(RING)]
        hi_ready = sem("hi_ready")
        lo_ready = sem("lo_ready")
        block_done = sem("block_done")
        silu_ready = sem("silu_ready")
        h_ready = sem("h_ready")
        h_hi_ready = sem("h_hi_ready")
        h_lo_ready = sem("h_lo_ready")
        acc_done = sem("acc_done")
        stats_ready = sem("stats_ready")
        std_ready = sem("std_ready")
        norm_cols = sem("norm_cols")
        normed = sem("normed")
        gained = sem("gained")
        dve_step = sem("dve_step")
        x_loaded = [sem(f"x_loaded{m}") for m in range(TC)]
        small_loaded = sem("small_loaded")
        mem_loaded = sem("mem_loaded")
        gb_loaded = sem("gb_loaded")
        xtok_ready = sem("xtok_ready")
        ax_ready = sem("ax_ready")
        xT_psum = sem("xT_psum")
        xT_hi_ready = sem("xT_hi_ready")
        xT_lo_ready = sem("xT_lo_ready")
        const_ready = sem("const_ready")
        out_stored = sem("out_stored")
        ba_split = sem("ba_split")
        conv_psum = sem("conv_psum")
        ba_done = sem("ba_done")
        ba_copied = sem("ba_copied")
        baT_done = sem("baT_done")
        qm_copied = sem("qm_copied")
        mem_o_ready = sem("mem_o_ready")
        mem_psum = sem("mem_psum")
        memT_hi_ready = sem("memT_hi_ready")
        memT_lo_ready = sem("memT_lo_ready")
        conv_step = sem("conv_step")
        conv_done = sem("conv_done")
        chan_ready = sem("chan_ready")
        gate_ready = sem("gate_ready")
        sq_ready = sem("sq_ready")
        ssq_done = sem("ssq_done")
        scores_done = sem("scores_done")
        max_ready = sem("max_ready")
        negmax_ready = sem("negmax_ready")
        recip_ready = sem("recip_ready")
        exp_ready = sem("exp_ready")
        prob_ready = sem("prob_ready")
        probT_done = sem("probT_done")
        probT_ready = sem("probT_ready")
        pv_done = sem("pv_done")
        cat_hi_ready = sem("cat_hi_ready")
        cat_lo_ready = sem("cat_lo_ready")
        col_vec = sem("col_vec")
        col_act = sem("col_act")
        g_ready = sem("g_ready")
        gcum_done = sem("gcum_done")
        gcol_ready = sem("gcol_ready")
        grow_done = sem("grow_done")
        kk_done = sem("kk_done")
        kq_done = sem("kq_done")
        vT_done = sem("vT_done")
        dist_ready = sem("dist_ready")
        egrow_ready = sem("egrow_ready")
        decay_ready = sem("decay_ready")
        kdec_ready = sem("kdec_ready")
        vb_ready = sem("vb_ready")
        qk_masked = sem("qk_masked")
        ss_ready = sem("ss_ready")
        qdec_ready = sem("qdec_ready")
        a_ready = sem("a_ready")
        qk_ready = sem("qk_ready")
        part_ready = sem("part_ready")
        inv_ready = sem("inv_ready")
        quart_done = sem("quart_done")
        quart_ready = sem("quart_ready")
        double_done = sem("double_done")
        ks_done = sem("ks_done")
        rhs_ready = sem("rhs_ready")
        u_done = sem("u_done")
        u_ready = sem("u_ready")
        supd_done = sem("supd_done")
        o_done = sem("o_done")
        state_ready = sem("state_ready")
        o_ready = sem("o_ready")
        on_ready = sem("on_ready")
        oT_done = sem("oT_done")
        oT_ready = sem("oT_ready")

        two_piece = {FFN1 + NB_IN - 1, FFN2 + NB_IN - 1}

        def raw_count(n):
            return 16 * sum(2 if b in two_piece else 1 for b in range(n % RING, n + 1, RING))

        def by_k(n, width=P):
            return w_raw[:, n % RING, :].rearrange("p (k c) -> p k c", k=KC)[:, :, 0:width]

        def h_at(rows, f, i, step):
            return h[0:rows, f, :] if isinstance(i, int) else h[0:rows, bass.ds(f + step * i, 1), :]

        def pair_bank(m):
            return ps[:, 2 * m:2 * m + 2, :].rearrange("p b t -> p (b t)")

        def by_tokens(m):
            return ps[:, 2 * m:2 * m + 2, :].rearrange("p b (k t) -> p (b k) t", t=P)

        def col(j):
            return cols[:, j, :]

        def col_ht(j):
            return cols[:, j, :].rearrange("p (h t) -> p h t", h=H)

        def cols_t(j, t0, t1):
            return col_ht(j)[:, :, t0:t1]

        def unit(j, hh, t):
            return cols[:, j, hh * TC + t:hh * TC + t + 1]

        (GA, AA, BC, EA, EB, LNU, U1, EB1, BETA, CORR, RU, SP, DEC, GCUM, GL, DGL, EG, EGL, EDEC,
         KK, R2, RR, BR, BR2, NBG, EPSQ, SS, RO, NEGG) = range(29)

        def bank(g, j):
            return ps[:, 4 * g + j, 0:HG * P]

        def bank3(g, j):
            return bank(g, j).rearrange("p (h c) -> p h c", h=HG)

        def tile(c, t):
            return chan[:, c, t * P:(t + 1) * P]

        def group_tiles(first, g, t):
            return chan[:, first + g * HG:first + (g + 1) * HG, t * P:(t + 1) * P]

        units = [(t, g) for t in range(TC) for g in range(G)]

        def nth(t, g):
            return t * G + g + 1

        def nth_level(t, g, lev, first):
            return (t * (LEVELS - first) + lev - first) * G + g + 1

        block = ctx.enter_context(nc.Block())

        @block.sync
        def _(sp):

            def load(n, dst, src, i=0):
                if n >= RING:
                    sp.wait_ge(hi_ready, n - RING + 1 + RING * i)
                    sp.wait_ge(lo_ready, n - RING + 1 + RING * i)
                sp.dma_start(dst, src).then_inc(raw_loaded[n % RING], 16)

            def load_x(m):
                sp.dma_start(z[:, m, :], a["x"][0, m * P:(m + 1) * P, :]).then_inc(x_loaded[m], 16)

            def ffn_loads(base, w_in, w_out):
                in_cols = w_in.rearrange("(k p) c -> p k c", p=P)
                out_rows = w_out[0:FC * P, :].rearrange("(f p) d -> p f d", p=P)

                def gate_up(b, f, i=0):
                    for j in range(2):
                        n = base + b + j
                        load(n, by_k(n), in_cols[:, :, bass.ds(f * P + j * F, P)], i)
                if base == FFN1:
                    for m in (0, 1):
                        load_x(m)
                    gate_up(0, 0)
                    for m in (2, 3):
                        load_x(m)
                    gate_up(2, 1)
                else:
                    gate_up(0, 0)
                    gate_up(2, 1)
                with sp.Fori(0, FC // 2 - 1) as i:
                    gate_up(4, 2 * i + 2, i)
                    gate_up(6, 2 * i + 3, i)
                gate_up(2 * FC - 2, FC - 1)
                n = base + NB_IN - 1
                load(n, by_k(n, FR), in_cols[:, :, FC * P:F])
                sp.dma_start(w_raw[:, n % RING, :].rearrange("p (k c) -> p k c", k=KC)[:, :, FR:P],
                             in_cols[:, :, F + FC * P:2 * F]).then_inc(raw_loaded[n % RING], 16)
                n = base + NB_IN
                with sp.Fori(0, FC // RING) as i:
                    for j in range(RING):
                        load(n + j, w_raw[:, (n + j) % RING, :], out_rows[:, bass.ds(i * RING + j, 1), :], i)
                for f in range(FC // RING * RING, FC):
                    load(n + f, w_raw[:, (n + f) % RING, :], out_rows[:, f, :])
                load(n + FC, w_raw[0:FR, (n + FC) % RING, :], w_out[FC * P:F, :])

            ffn_loads(FFN1, a["l0_ffn1_w_in"], a["l0_ffn1_w_out"])
            mix_cols = a["l0_w_in"].rearrange("(k p) c -> p k c", p=P)
            for c in range(H):
                load(GATE + c, by_k(GATE + c), mix_cols[:, :, (NG + c) * P:(NG + c + 1) * P])
            for j in range(HP):
                load(QM + j, by_k(QM + j), mix_cols[:, :, NC * P + NBA + j * P:NC * P + NBA + (j + 1) * P])
            kv_cols = a["l0_w_mem_kv"].rearrange("(k p) c -> p k c", p=P)
            for j in range(2 * HP):
                load(KV + j, by_k(KV + j), kv_cols[:, :, j * P:(j + 1) * P])
            with sp.Fori(0, 3 * H // RING) as i:
                for j in range(RING):
                    load(QKV + j, by_k(QKV + j), mix_cols[:, :, bass.ds((i * RING + j) * P, P)], i)
            for c in range(3 * H // RING * RING, 3 * H):
                load(QKV + c, by_k(QKV + c), mix_cols[:, :, c * P:(c + 1) * P])
            o_rows = a["l0_w_o"].rearrange("(k p) d -> p k d", p=P)
            for k in range(KC):
                load(WO + k, w_raw[:, (WO + k) % RING, :], o_rows[:, k, :])
            ffn_loads(FFN2, a["l0_ffn2_w_in"], a["l0_ffn2_w_out"])
            for m in range(TC):
                sp.wait_ge(xtok_ready, 2 * TC + m + 1)
                sp.dma_start(out[0, m * P:(m + 1) * P, :], z[:, m, :]).then_inc(out_stored, 16)
            sp.wait_ge(out_stored, 16 * TC)

        @block.gpsimd
        def _(pool):
            made = [0]

            def step(ins):
                made[0] += 1
                ins.then_inc(const_ready, 1)
                pool.wait_ge(const_ready, made[0])

            step(pool.memset(ident[:, :], 0.0))
            step(pool.affine_select(out=ident[:, :], in_=ident[:, :], compare_op=ALU.not_equal, fill=1.0,
                                    base=0, pattern=[[-1, P]], channel_multiplier=1))
            step(pool.memset(eps[:, :], LN_EPS))
            step(pool.memset(ones[:, :], 1.0))
            pool.dma_start(ln_g[:, :], a["l0_ln1_g"].partition_broadcast(P)).then_inc(gb_loaded, 16)
            pool.dma_start(ln_b[:, :], a["l0_ln1_b"].partition_broadcast(P)).then_inc(gb_loaded, 16)
            pool.dma_start(wba[:, :, :], a["l0_w_in"].rearrange("(k p) c -> p k c", p=P)[:, :, NC * P:NC * P + NBA])\
                .then_inc(small_loaded, 16)
            pool.dma_start(conv_rows[:, :], a["l0_conv_w"].rearrange("j (c p) -> (j c) p", p=P)).then_inc(small_loaded, 16)
            pool.dma_start(onorm[:, :], a["l0_onorm_g"].rearrange("(p o) -> p o", o=1)).then_inc(small_loaded, 16)
            pool.dma_start(a_log[:, :], a["l0_a_log"].partition_broadcast(P)).then_inc(small_loaded, 16)
            pool.dma_start(dt_bias[:, :], a["l0_dt_bias"].partition_broadcast(P)).then_inc(small_loaded, 16)
            pool.dma_start(mem_tok[:, :, :], a["mem"][0].rearrange("(c p) d -> p c d", p=P)).then_inc(mem_loaded, 16)
            step(pool.memset(tri[:, :], 1.0))
            step(pool.affine_select(out=tri[:, :], in_=tri[:, :], compare_op=ALU.is_ge, fill=0.0,
                                    base=0, pattern=[[1, P]], channel_multiplier=-1))
            step(pool.memset(below[:, :], 1.0))
            step(pool.affine_select(out=below[:, :], in_=below[:, :], compare_op=ALU.is_gt, fill=0.0,
                                    base=0, pattern=[[-1, P]], channel_multiplier=1))
            step(pool.memset(level[:, :, :], 0.0))
            for lev in range(LEVELS):
                s = 2 << lev
                view = level[:, lev, :].rearrange("p (b c) -> p b c", c=s)
                step(pool.memset(level[:, lev, :], 1.0))
                step(pool.affine_select(out=view, in_=view, compare_op=ALU.is_ge, fill=0.0, base=0,
                                        pattern=[[-s, P // s], [0, s]], channel_multiplier=1))
                step(pool.affine_select(out=view, in_=view, compare_op=ALU.is_gt, fill=0.0, base=s,
                                        pattern=[[s, P // s], [0, s]], channel_multiplier=-1))
            for lev in range(LEVELS - 1, 0, -1):
                step(pool.tensor_tensor(level[:, lev, :], level[:, lev, :], level[:, lev - 1, :], ALU.subtract))
            step(pool.tensor_tensor(level[:, 0, :], level[:, 0, :], ident[:, :], ALU.subtract))
            step(pool.tensor_tensor(level[:, :, :], level[:, :, :],
                                    below[:, :].unsqueeze(1).to_broadcast([P, LEVELS, P]), ALU.mult))

            def scale_residual(L):
                for m in range(TC):
                    if L == 0:
                        pool.wait_ge(x_loaded[m], 16)
                    else:
                        pool.wait_ge(xtok_ready, TC * (L - 1) + m + 1)
                    pool.tensor_scalar(ax[:, m, :], z[:, m, :], ALPHA, 1.0, ALU.mult, ALU.mult).then_inc(ax_ready, 1)

            def add_bias(L):
                for m in range(TC):
                    pool.wait_ge(gained, TC * (L - 1) + m + 1)
                    pool.tensor_tensor(z[:, m, :], z[:, m, :], ln_b[:, :], ALU.add).then_inc(xtok_ready, 1)

            def load_gb(L, g, b):
                pool.wait_ge(xtok_ready, TC * L)
                pool.dma_start(ln_g[:, :], g.partition_broadcast(P)).then_inc(gb_loaded, 16)
                pool.dma_start(ln_b[:, :], b.partition_broadcast(P)).then_inc(gb_loaded, 16)

            scale_residual(0)
            add_bias(1)
            scale_residual(1)
            load_gb(1, a["l0_ln2_g"], a["l0_ln2_b"])
            pool.wait_ge(small_loaded, 16 * 5)
            for hh in range(H):
                pool.wait_ge(chan_ready, hh + 1)
                pool.tensor_scalar(chan[:, NG + hh, :], chan[:, NG + hh, :], onorm[:, 0:1], 1.0,
                                   ALU.mult, ALU.mult).then_inc(gate_ready, 1)

            def queries(t):
                if t:
                    pool.wait_ge(scores_done, t)
                else:
                    pool.wait_ge(chan_ready, H + HP)
                pool.tensor_copy(qm_now[:, :, :], qm[:, :, t * P:(t + 1) * P]).then_inc(qm_copied, 1)

            queries(0)
            for c in range(2 * H):
                if c % RING == 2:
                    queries(c // RING + 1)
                pool.wait_ge(chan_ready, QKV - MIX + c + 1)
                if c >= 2:
                    pool.wait_ge(ssq_done, c - 1)
                pool.tensor_tensor(sq[:, c % 2, :], chan[:, c, :], chan[:, c, :], ALU.mult).then_inc(sq_ready, 1)
            def mask3(m):
                return m.unsqueeze(1).to_broadcast([P, HG, P])

            def part_of(t, lev):
                for g in range(G):
                    if lev == 0:
                        pool.wait_ge(a_ready, nth(t, g))
                    if lev == 2:
                        pool.wait_ge(inv_ready, nth_level(t, g, 0, 0))
                    if lev > 2:
                        pool.wait_ge(quart_done, nth_level(t, g, lev - 2, 1))
                    pool.tensor_tensor(part[g][lev % 2][:, :, :], amat[g][:, :, :], mask3(level[:, lev, :]),
                                       ALU.mult).then_inc(part_ready, 1)

            for t in range(TC):
                part_of(t, 0)
                part_of(t, 1)
                for g in range(G):
                    pool.wait_ge(egrow_ready, nth(t, g))
                    pool.tensor_tensor(qdec[g][:, :, :], qdec[g][:, :, :], group_tiles(NQ, g, t), ALU.mult).then_inc(qdec_ready, 1)
                part_of(t, 2)
                for g in range(G):
                    pool.wait_ge(qk_ready, nth(t, g))
                    pool.tensor_tensor(qk[g][:, :, :], qk[g][:, :, :], mask3(tri[:, :]), ALU.mult).then_inc(qk_masked, 1)
                for lev in range(3, LEVELS):
                    part_of(t, lev)
            add_bias(2)
            scale_residual(2)
            load_gb(2, a["l0_ln3_g"], a["l0_ln3_b"])

        @block.scalar
        def _(act):
            def w_split_hi(n, i=0, rows=P):
                act.wait_ge(raw_loaded[n % RING], raw_count(n) + 16 * i)
                if n >= RING:
                    act.wait_ge(block_done, n - RING + 1 + RING * i)
                act.activation(w_hi[0:rows, n % RING, :], w_raw[0:rows, n % RING, :], ACT.Copy).then_inc(hi_ready, 1)

            def transposed_hi(L, m):
                act.wait_ge(xT_psum, TC * L + m + 1)
                act.activation(xT_hi[:, :, m * P:(m + 1) * P], by_tokens(m), ACT.Copy).then_inc(xT_hi_ready, 1)

            def ffn(base, hb):
                def silu(f, i=0, rows=P):
                    act.wait_ge(block_done, base + 2 * f + 1 + RING * i)
                    if f >= 2:
                        act.wait_ge(h_ready, hb + f - 1 + 2 * i)
                    act.activation(silu_g[0:rows, f % 2, :], ps[0:rows, 2 * (f % 2), :], ACT.Silu).then_inc(silu_ready, 1)

                def chunk(f, i=0):
                    silu(f, i)
                    w_split_hi(base + 2 * f + 4, i)
                    w_split_hi(base + 2 * f + 5, i)

                nb = base + NB_IN

                def out_hi(f, i=0, rows=P):
                    n = nb + f
                    w_split_hi(n, i, rows)
                    act.wait_ge(h_ready, hb + f + 1 + RING * i)
                    act.activation(h_hi[0:rows, n % RING, :], h_at(rows, f, i, RING), ACT.Copy).then_inc(h_hi_ready, 1)
                chunk(0)
                chunk(1)
                with act.Fori(0, (FC - 5) // 2) as i:
                    chunk(2, i)
                    chunk(3, i)
                chunk(FC - 3)
                silu(FC - 2)
                w_split_hi(base + 2 * FC)
                out_hi(0)
                silu(FC - 1)
                out_hi(1)
                silu(FC, rows=FR)
                out_hi(2)
                out_hi(3)
                with act.Fori(0, FC // RING - 1) as i:
                    for j in range(RING):
                        out_hi(RING + j, i)
                for f in range(FC // RING * RING, FC):
                    out_hi(f)
                out_hi(FC, rows=FR)

            def boundary(L, n0):
                def norm(m):
                    act.wait_ge(stats_ready, TC * (L - 1) + m + 1)
                    act.activation(std[:, m:m + 1], mv[:, m, 1:2], ACT.Sqrt, bias=eps[:, :]).then_inc(std_ready, 1)
                    act.wait_ge(norm_cols, TC * (L - 1) + m + 1)
                    act.activation(z[:, m, :], z[:, m, :], ACT.Identity, bias=shift[:, m:m + 1], scale=rstd[:, m:m + 1])\
                        .then_inc(normed, 1)
                if L == 0:
                    transposed_hi(0, 0)
                    transposed_hi(0, 1)
                    w_split_hi(n0)
                    w_split_hi(n0 + 1)
                elif n0 is None:
                    for m in range(TC):
                        norm(m)
                    return
                else:
                    norm(0)
                    norm(1)
                    transposed_hi(L, 0)
                    norm(2)
                    transposed_hi(L, 1)
                    w_split_hi(n0)
                    norm(3)
                    w_split_hi(n0 + 1)
                transposed_hi(L, 2)
                w_split_hi(n0 + 2)
                w_split_hi(n0 + 3)
                transposed_hi(L, 3)

            act.wait_ge(const_ready, 3)
            boundary(0, FFN1)
            act.wait_ge(small_loaded, 16 * 5)
            act.activation(wba_hi[:, :, :], wba[:, :, :], ACT.Copy).then_inc(ba_split, 1)
            ffn(FFN1, 0)
            boundary(1, MIX)


            def mem_hi(c):
                act.wait_ge(mem_psum, c + 1)
                if c == 0:
                    act.wait_ge(ax_ready, 2 * TC)
                act.activation(memT_hi[:, :, c * P:(c + 1) * P], by_tokens(3), ACT.Copy).then_inc(memT_hi_ready, 1)

            def gate(c):
                act.wait_ge(block_done, GATE + c + 1)
                act.activation(chan[:, NG + c, :], ps[:, c if c < RING else c % 2, :], ACT.Silu).then_inc(chan_ready, 1)
                w_split_hi(GATE + c + RING)

            def channel(c, i=0):
                w_split_hi(QKV + c + RING, i)
                act.wait_ge(conv_done, c + 1 + RING * i)
                dst = chan[:, c, :] if isinstance(i, int) else chan[:, bass.ds(c + RING * i, 1), :]
                act.activation(dst, dst, ACT.Silu).then_inc(chan_ready, 1)

            def column(dst, src, func, need, scale=1.0):
                act.wait_ge(col_vec, need)
                act.activation(dst, src, func, scale=scale).then_inc(col_act, 1)

            for c in range(3):
                gate(c)
            mem_hi(0)
            for c in range(3, H):
                gate(c)
            mem_hi(1)
            for j in range(HP):
                act.wait_ge(block_done, QM + j + 1)
                act.activation(qm[:, j, :], ps[:, j % 2, :], ACT.Copy).then_inc(chan_ready, 1)
                w_split_hi(QM + j + RING)
                if j == 0:
                    column(col(EA), col(AA), ACT.Exp, 1)
                    column(col(EB), col(BC), ACT.Exp, 1, -1.0)
                    column(a_log[:, :], a_log[:, :], ACT.Exp, 1)
            for j in range(2 * HP):
                act.wait_ge(block_done, KV + j + 1)
                if j < HP:
                    act.activation(km[:, j, :], ps[:, j % 2, 0:M], ACT.Copy).then_inc(chan_ready, 1)
                else:
                    act.activation(vm[:, :, (j - HP) * P:(j - HP + 1) * P], ps[:, j % 2, 0:M].rearrange("p (c n) -> p c n", c=MC),
                                   ACT.Copy).then_inc(chan_ready, 1)
                w_split_hi(KV + j + RING)
                if j == 0:
                    column(col(LNU), col(U1), ACT.Ln, 2)
            act.wait_ge(gcol_ready, 1)
            column(col(EG), col(GCUM), ACT.Exp, 2)
            column(col(EGL), col(GL), ACT.Exp, 2)
            column(col(EDEC), col(DGL), ACT.Exp, 2)

            def attend(c, i=0):
                act.wait_ge(negmax_ready, i + 1)
                for e in range(2):
                    for hp in range(HP):
                        u = e * HP + hp
                        ins = act.activation(prob[:, u, :], ps[:, 4 + e, hp * M:(hp + 1) * M], ACT.Exp,
                                             bias=neg_max[:, 1, u:u + 1], scale=MDH ** -0.5, accum_out=prob_sum[:, u:u + 1])
                ins.then_inc(exp_ready, 1)
                k = i if c == 2 else 0
                channel(c, k)
                channel(c + 1, k)
                act.wait_ge(probT_done, i + 1)
                act.activation(probT[:, :, :], by_tokens(3), ACT.Copy).then_inc(probT_ready, 1)
                channel(c + 2, k)
                act.wait_ge(pv_done, i + 1)
                act.activation(qm[:, :, bass.ds(i * P, P)], ps[:, 3, 0:HP * P].rearrange("p (h n) -> p h n", h=HP), ACT.Copy)\
                    .then_inc(mem_o_ready, 1)
                channel(c + 3, k)
            channel(0)
            channel(1)
            with act.Fori(0, TC - 1) as i:
                attend(2, i)
            attend(3 * H - RING, TC - 1)
            column(col(RR), col(R2), ACT.Sqrt, 3)
            act.wait_ge(mem_o_ready, TC)
            act.activation(xT_hi[:, H:KC, :], qm[:, :, :], ACT.Copy).then_inc(cat_hi_ready, 1)

            act.wait_ge(col_vec, 4)

            def decays(t, g):
                act.wait_ge(grow_done, nth(t, g))
                if t:
                    act.wait_ge(qk_ready, nth(t - 1, g))
                    act.wait_ge(a_ready, nth(t - 1, g))
                for j in range(HG):
                    ins = act.activation(decay[g][:, j, :], bank3(g, 0)[:, j, :], ACT.Abs, bias=unit(NEGG, g * HG + j, t))
                ins.then_inc(dist_ready, 1)
                act.wait_ge(dist_ready, nth(t, g))
                act.activation(decay[g][:, :, :], decay[g][:, :, :], ACT.Exp, scale=-1.0).then_inc(decay_ready, 1)

            def sum_squares(t):
                if t == 0:
                    act.wait_ge(cat_lo_ready, 1)
                for g in range(G):
                    act.wait_ge(o_ready, nth(t, g))
                    act.wait_ge(ss_ready, nth(t, g) - 1) if nth(t, g) > 1 else None
                    for j in range(HG):
                        ins = act.activation(squares[:, j, :], tile(NV + g * HG + j, t), ACT.Square,
                                             accum_out=unit(SS, g * HG + j, t))
                    ins.then_inc(ss_ready, 1)

            def heads_hi(j):
                for g in range(G):
                    hh = g * HG + j
                    act.wait_ge(oT_ready, j * G + g + 1)
                    act.activation(xT_hi[:, hh, 0:T - P], chan[:, NG + hh, 0:T - P], ACT.Copy).then_inc(cat_hi_ready, 1)

            for g in range(G):
                decays(0, g)
            for t in range(TC):
                for g in range(G):
                    if t:
                        act.wait_ge(o_done, nth(t - 1, g))
                    act.activation(qdec[g][:, :, :], bank3(g, 0), ACT.Exp).then_inc(egrow_ready, 1)
                for g in range(G):
                    act.wait_ge(kq_done, nth(t, g))
                    for j in range(HG):
                        ins = act.activation(kdec[g][:, j, :], bank3(g, 3)[:, j, :], ACT.Copy, scale=unit(EDEC, g * HG + j, t))
                    ins.then_inc(kdec_ready, 1)
                for lev in range(1, LEVELS):
                    for g in range(G):
                        act.wait_ge(quart_done, nth_level(t, g, lev, 1))
                        act.activation(quart[g][:, :, :], bank3(g, 1), ACT.Copy).then_inc(quart_ready, 1)
                    if lev == 1:
                        for g in range(G):
                            act.wait_ge(vT_done, nth(t, g))
                            for j in range(HG):
                                ins = act.activation(rhs[g][:, j, :], bank3(g, 0)[:, j, :], ACT.Copy, scale=unit(BR, g * HG + j, t))
                            ins.then_inc(vb_ready, 1)
                    if lev == 2 and t:
                        sum_squares(t - 1)
                    if lev >= 5 and t < TC - 1:
                        decays(t + 1, lev - 5)
                    if t == TC - 1:
                        if lev == 3:
                            column(cols_t(RO, 0, TC - 1), cols_t(RO, 0, TC - 1), ACT.Sqrt, 5)
                        if lev >= 5:
                            heads_hi(lev - 5)
                for g in range(G):
                    act.wait_ge(u_done, nth(t, g))
                    act.activation(quart[g][:, :, :], bank3(g, 1), ACT.Copy).then_inc(u_ready, 1)
                if t == TC - 1:
                    heads_hi(2)
                for g in range(G):
                    act.wait_ge(o_done, nth(t, g))
                    act.activation(group_tiles(NV, g, t), bank3(g, 3), ACT.Copy).then_inc(o_ready, 1)
            sum_squares(TC - 1)
            column(cols_t(RO, TC - 1, TC), cols_t(RO, TC - 1, TC), ACT.Sqrt, 6)
            for g in range(G):
                act.wait_ge(oT_ready, H + g + 1)
                act.activation(xT_hi[:, g * HG:(g + 1) * HG, T - P:T], group_tiles(NG, g, TC - 1), ACT.Copy).then_inc(cat_hi_ready, 1)
            for k in range(RING, KC):
                w_split_hi(WO + k)
            boundary(2, FFN2)
            ffn(FFN2, FC + 1)
            boundary(3, None)

        @block.vector
        def _(dve):
            steps = [0]

            def then_next(ins):
                steps[0] += 1
                ins.then_inc(dve_step, 1)
                dve.wait_ge(dve_step, steps[0])

            def w_split_lo(n, i=0, rows=P):
                dve.wait_ge(hi_ready, n + 1 + RING * i)
                dve.tensor_tensor(w_lo[0:rows, n % RING, :], w_raw[0:rows, n % RING, :],
                                  w_hi[0:rows, n % RING, :].bitcast(F32), ALU.subtract).then_inc(lo_ready, 1)

            def transposed_lo(L, m):
                dve.wait_ge(xT_hi_ready, TC * L + m + 1)
                dve.tensor_tensor(xT_lo[:, :, m * P:(m + 1) * P], by_tokens(m),
                                  xT_hi[:, :, m * P:(m + 1) * P].bitcast(F32), ALU.subtract).then_inc(xT_lo_ready, 1)

            def ffn(base, hb):
                def gated(f, i=0, rows=P):
                    dve.wait_ge(silu_ready, hb + f + 1 + 2 * i)
                    if rows == P:
                        dve.wait_ge(block_done, base + 2 * f + 2 + RING * i)
                        up = ps[:, 2 * (f % 2) + 1, :]
                    else:
                        up = ps[FR:P, 2 * (f % 2), :]
                    dve.tensor_tensor(h_at(rows, f, i, 2), silu_g[0:rows, f % 2, :], up, ALU.mult).then_inc(h_ready, 1)

                def chunk(f, i=0):
                    gated(f, i)
                    w_split_lo(base + 2 * f + 4, i)
                    w_split_lo(base + 2 * f + 5, i)
                nb = base + NB_IN

                def out_lo(f, i=0, rows=P):
                    n = nb + f
                    w_split_lo(n, i, rows)
                    dve.wait_ge(h_hi_ready, hb + f + 1 + RING * i)
                    dve.tensor_tensor(h_lo[0:rows, n % RING, :], h_at(rows, f, i, RING),
                                      h_hi[0:rows, n % RING, :].bitcast(F32), ALU.subtract).then_inc(h_lo_ready, 1)
                chunk(0)
                chunk(1)
                with dve.Fori(0, (FC - 5) // 2) as i:
                    chunk(2, i)
                    chunk(3, i)
                chunk(FC - 3)
                gated(FC - 2)
                w_split_lo(base + 2 * FC)
                out_lo(0)
                gated(FC - 1)
                out_lo(1)
                gated(FC, rows=FR)
                out_lo(2)
                out_lo(3)
                with dve.Fori(0, FC // RING - 1) as i:
                    for j in range(RING):
                        out_lo(RING + j, i)
                for f in range(FC // RING * RING, FC):
                    out_lo(f)
                out_lo(FC, rows=FR)

            def boundary(L, n0, factor=1.0):
                last = n0 is None

                def moments(m):
                    if m < TC - 1:
                        dve.wait_ge(acc_done, (TC - 1) * (L - 1) + m + 1)
                    else:
                        dve.wait_ge(block_done, (FFN1 + NB_IN + NB_OUT, FFN2, FFN2 + NB_IN + NB_OUT)[L - 1])
                    then_next(dve.scalar_tensor_tensor(z[:, m, :], pair_bank(m), factor, ax[:, m, :], ALU.mult, ALU.add))
                    dve.bn_stats(stats[:, m, 0, :], z[:, m, 0:D // 2])
                    then_next(dve.bn_stats(stats[:, m, 1, :], z[:, m, D // 2:D]))
                    dve.bn_aggr(mv[:, m, :], stats[:, m, :, :].rearrange("p a s -> p (a s)")).then_inc(stats_ready, 1)

                def columns(m):
                    dve.wait_ge(std_ready, TC * (L - 1) + m + 1)
                    then_next(dve.reciprocal(rstd[:, m:m + 1], std[:, m:m + 1]))
                    dve.tensor_scalar(shift[:, m:m + 1], mv[:, m, 0:1], rstd[:, m:m + 1], -1.0, ALU.mult, ALU.mult)\
                        .then_inc(norm_cols, 1)

                def gain(m):
                    dve.wait_ge(normed, TC * (L - 1) + m + 1)
                    ins = dve.tensor_tensor(z[:, m, :], z[:, m, :], ln_g[:, :], ALU.mult)
                    if last:
                        then_next(ins)
                        dve.tensor_tensor(z[:, m, :], z[:, m, :], ln_b[:, :], ALU.add).then_inc(xtok_ready, 1)
                    else:
                        ins.then_inc(gained, 1)

                if L:
                    dve.wait_ge(gb_loaded, 32 * L)
                    dve.wait_ge(ax_ready, TC * L)
                    for m in range(TC - 1):
                        moments(m)
                        columns(m)
                        gain(m)
                        if m and not last:
                            transposed_lo(L, m - 1)
                    if not last:
                        w_split_lo(n0)
                    moments(3)
                    columns(3)
                    if not last:
                        w_split_lo(n0 + 1)
                    gain(3)
                    if last:
                        return
                else:
                    transposed_lo(0, 0)
                    transposed_lo(0, 1)
                    w_split_lo(n0)
                    w_split_lo(n0 + 1)
                transposed_lo(L, 2)
                w_split_lo(n0 + 2)
                w_split_lo(n0 + 3)
                transposed_lo(L, 3)

            boundary(0, FFN1)
            dve.wait_ge(ba_split, 1)
            dve.tensor_tensor(wba_lo[:, :, :], wba[:, :, :], wba_hi[:, :, :].bitcast(F32), ALU.subtract).then_inc(ba_split, 1)
            ffn(FFN1, 0)
            boundary(1, MIX, 0.5)

            def mem_lo(c):
                dve.wait_ge(memT_hi_ready, c + 1)
                dve.tensor_tensor(memT_lo[:, :, c * P:(c + 1) * P], by_tokens(3),
                                  memT_hi[:, :, c * P:(c + 1) * P].bitcast(F32), ALU.subtract).then_inc(memT_lo_ready, 1)

            def conv(c, i=0):
                dve.wait_ge(block_done, QKV + c + 1 + RING * i)
                at = c if isinstance(i, int) else bass.ds(c + RING * i, 1)

                def y(s):
                    return chan[:, at, s:T]

                def tap(j):
                    return conv_w[:, j, c:c + 1] if isinstance(i, int) else conv_w[:, j, bass.ds(c + RING * i, 1)]
                for s in range(TAPS):
                    src = ps[:, c % 2, 0:T - s]
                    if s == 0:
                        ins = dve.tensor_scalar(y(0), src, tap(TAPS - 1), None, ALU.mult)
                    else:
                        dve.wait_ge(conv_step, (TAPS - 1) * (c + (0 if isinstance(i, int) else RING * i)) + s)
                        ins = dve.scalar_tensor_tensor(y(s), src, tap(TAPS - 1 - s), y(s), ALU.mult, ALU.add)
                    ins.then_inc(conv_step if s < TAPS - 1 else conv_done, 1)
                w_split_lo(QKV + c + RING, i)

            for c in range(3):
                w_split_lo(GATE + c + RING)
            mem_lo(0)
            w_split_lo(GATE + 3 + RING)
            dve.wait_ge(conv_psum, 1)
            dve.tensor_copy(conv_w[:, :, :].rearrange("p j c -> p (j c)"), ps[:, 5, 0:TAPS * 3 * H])
            dve.wait_ge(ba_done, 1)
            dve.tensor_copy(ba_rows[:, :], ps[0:NBA, 4, :]).then_inc(ba_copied, 1)
            w_split_lo(GATE + 4 + RING)
            w_split_lo(GATE + 5 + RING)
            mem_lo(1)
            dve.wait_ge(baT_done, 1)
            ba = ps[:, 5, P:P + TC * NBA].rearrange("p (t w h) -> p w h t", t=TC, w=2)
            dve.tensor_copy(col_ht(BC), ba[:, 0])
            then_next(dve.tensor_tensor(col_ht(GA), ba[:, 1], dt_bias[:, :].unsqueeze(2).to_broadcast([P, H, TC]), ALU.add))
            dve.scalar_tensor_tensor(col(AA), col(GA), -1.0, col(GA), ALU.mult, ALU.min).then_inc(col_vec, 1)
            w_split_lo(QM + RING)
            w_split_lo(QM + 1 + RING)
            dve.wait_ge(col_act, 3)
            dve.tensor_scalar(col(U1), col(EA), 1.0, None, ALU.add).then_inc(col_vec, 1)
            then_next(dve.tensor_scalar(col(EB1), col(EB), 1.0, None, ALU.add))
            then_next(dve.reciprocal(col(BETA), col(EB1)))
            dve.wait_ge(col_vec, 2)
            then_next(dve.scalar_tensor_tensor(col(CORR), col(U1), 1.0, col(EA), ALU.subtract, ALU.subtract))
            then_next(dve.reciprocal(col(RU), col(U1)))
            then_next(dve.tensor_tensor(col(CORR), col(CORR), col(RU), ALU.mult))
            w_split_lo(KV + RING)
            w_split_lo(KV + 1 + RING)
            dve.wait_ge(col_act, 4)
            then_next(dve.tensor_tensor(col(SP), col(LNU), col(CORR), ALU.subtract))
            then_next(dve.scalar_tensor_tensor(col(SP), col(GA), 0.0, col(SP), ALU.max, ALU.add))
            dve.scalar_tensor_tensor(col_ht(DEC), col_ht(SP), -1.0, a_log[:, :].unsqueeze(2).to_broadcast([P, H, TC]),
                                     ALU.mult, ALU.mult).then_inc(g_ready, 1)
            w_split_lo(KV + 2 + RING)
            dve.wait_ge(gcum_done, 1)
            dve.tensor_copy(col(GCUM), ps[:, 4, 64:64 + H * TC])
            then_next(dve.tensor_copy(col(GL), ps[:, 4, 96:96 + H * TC]))
            dve.tensor_scalar(col(NEGG), col(GCUM), -1.0, None, ALU.mult)
            dve.tensor_tensor(col(DGL), col(GL), col(GCUM), ALU.subtract).then_inc(gcol_ready, 1)
            w_split_lo(KV + 3 + RING)

            def attend(c, i=0):
                k = i if c == 2 else 0
                dve.wait_ge(scores_done, i + 1)
                dve.tensor_reduce(neg_max[:, 0, :], ps[:, 4:6, :].rearrange("p e (h m) -> p (e h) m", h=HP), AX.X, ALU.max)\
                    .then_inc(max_ready, 1)
                dve.wait_ge(max_ready, i + 1)
                dve.tensor_scalar(neg_max[:, 1, :], neg_max[:, 0, :], -(MDH ** -0.5), None, ALU.mult).then_inc(negmax_ready, 1)
                conv(c, k)
                dve.wait_ge(exp_ready, i + 1)
                dve.reciprocal(prob_sum[:, :], prob_sum[:, :]).then_inc(recip_ready, 1)
                dve.wait_ge(recip_ready, i + 1)
                dve.tensor_tensor(prob[:, :, :], prob[:, :, :], prob_sum[:, :].unsqueeze(2).to_broadcast([P, 2 * HP, M]),
                                  ALU.mult).then_inc(prob_ready, 1)
                for j in range(1, RING):
                    conv(c + j, k)
                    if c > 2 and j == 1:
                        dve.wait_ge(ssq_done, 2 * H)
                        then_next(dve.tensor_scalar(col(KK), ssq[:, H * TC:2 * H * TC], 1e-6, None, ALU.add))
                        dve.reciprocal(col(R2), col(KK)).then_inc(col_vec, 1)
                        then_next(dve.tensor_scalar(col(EPSQ), ssq[:, 0:H * TC], 1e-6, LN_EPS * P, ALU.add, ALU.mult))
            ssq = ps[:, 2, 0:2 * H * TC]
            conv(0)
            conv(1)
            with dve.Fori(0, TC - 1) as i:
                attend(2, i)
            attend(3 * H - RING, TC - 1)
            dve.wait_ge(col_act, 8)
            dve.tensor_tensor(col(BR), col(BETA), col(RR), ALU.mult)
            dve.wait_ge(col_vec, 3)
            then_next(dve.tensor_tensor(col(BR2), col(BETA), col(R2), ALU.mult))
            dve.scalar_tensor_tensor(col(NBG), col(BR2), -1.0, col(EG), ALU.mult, ALU.mult).then_inc(col_vec, 1)
            dve.wait_ge(cat_hi_ready, 1)
            dve.tensor_tensor(xT_lo[:, H:KC, :], qm[:, :, :], xT_hi[:, H:KC, :].bitcast(F32), ALU.subtract).then_inc(cat_lo_ready, 1)

            def system(t, g):
                dve.wait_ge(kk_done, nth(t, g))
                dve.wait_ge(decay_ready, nth(t, g))
                for j in range(HG):
                    ins = dve.scalar_tensor_tensor(amat[g][:, j, :], bank3(g, 1)[:, j, :], unit(BR2, g * HG + j, t),
                                                   decay[g][:, j, :], ALU.mult, ALU.mult)
                ins.then_inc(a_ready, 1)

            def new_state(t, g):
                dve.wait_ge(supd_done, nth(t, g))
                dve.wait_ge(o_done, nth(t, g))
                if t == 0:
                    ins = dve.tensor_copy(state[:, g * HG:(g + 1) * HG, :], bank3(g, 2))
                else:
                    for j in range(HG):
                        ins = dve.scalar_tensor_tensor(state[:, g * HG + j, :], state[:, g * HG + j, :], unit(EGL, g * HG + j, t),
                                                       bank3(g, 2)[:, j, :], ALU.mult, ALU.add)
                ins.then_inc(state_ready, 1)

            def first_level(t, g):
                dve.wait_ge(part_ready, nth_level(t, g, 0, 0))
                then_next(dve.tensor_tensor(inv[g][:, :, :], ident[:, :].unsqueeze(1).to_broadcast([P, HG, P]),
                                            part[g][0][:, :, :], ALU.subtract))
                dve.transpose(invT[g][:, :, :].rearrange("p h c -> p (h c)"), inv[g][:, :, :].rearrange("p h c -> p (h c)"))\
                    .then_inc(inv_ready, 1)

            def norm_columns(t0, t1):
                dve.wait_ge(ss_ready, nth(t1 - 1, G - 1))
                dve.scalar_tensor_tensor(cols_t(RO, t0, t1), cols_t(SS, t0, t1), 1.0 / P, cols_t(EPSQ, t0, t1), ALU.mult, ALU.add)\
                    .then_inc(col_vec, 1)

            def norm_outputs(t0, t1):
                dve.wait_ge(col_act, 9 if t0 == 0 else 10)
                then_next(dve.reciprocal(cols_t(RO, t0, t1), cols_t(RO, t0, t1)))
                for j in range(HG):
                    for g in range(G):
                        hh = g * HG + j
                        o = chan[:, NV + hh, t0 * P:t1 * P].rearrange("p (t c) -> p t c", c=P)
                        dve.tensor_tensor(o, o, col_ht(RO)[:, hh, t0:t1].unsqueeze(2).to_broadcast([P, t1 - t0, P]), ALU.mult)\
                            .then_inc(on_ready, 1)

            def gate_heads(j):
                for g in range(G):
                    hh = g * HG + j
                    dve.wait_ge(oT_done, j * G + g + 1)
                    dve.tensor_tensor(chan[:, NG + hh, 0:T - P], chan[:, NG + hh, 0:T - P], bank(g, 0), ALU.mult).then_inc(oT_ready, 1)

            def heads_lo(j):
                for g in range(G):
                    hh = g * HG + j
                    dve.wait_ge(cat_hi_ready, j * G + g + 2)
                    dve.tensor_tensor(xT_lo[:, hh, 0:T - P], chan[:, NG + hh, 0:T - P], xT_hi[:, hh, 0:T - P].bitcast(F32),
                                      ALU.subtract).then_inc(cat_lo_ready, 1)

            assert (TC - 1) == HG
            for t in range(TC):
                system(t, 0)
                if t:
                    new_state(t - 1, 0)
                system(t, 1)
                first_level(t, 0)
                if t:
                    new_state(t - 1, 1)
                first_level(t, 1)
                for g in range(G):
                    dve.wait_ge(kq_done, nth(t, g))
                    dve.tensor_tensor(qk[g][:, :, :], bank3(g, 2), decay[g][:, :, :], ALU.mult).then_inc(qk_ready, 1)
                for lev in range(1, LEVELS):
                    for g in range(G):
                        dve.wait_ge(double_done, nth_level(t, g, lev, 1))
                        ins = dve.tensor_tensor(invT[g][:, :, :], invT[g][:, :, :], bank3(g, 2), ALU.subtract)
                        if lev < LEVELS - 1:
                            ins = dve.tensor_tensor(inv[g][:, :, :], inv[g][:, :, :], bank3(g, 3), ALU.subtract)
                        ins.then_inc(inv_ready, 1)
                    if lev == 2 and t:
                        for g in range(G):
                            dve.wait_ge(ks_done, nth(t - 1, g))
                            for j in range(HG):
                                ins = dve.scalar_tensor_tensor(rhs[g][:, j, :], bank3(g, 0)[:, j, :], unit(NBG, g * HG + j, t),
                                                               rhs[g][:, j, :], ALU.mult, ALU.add)
                            ins.then_inc(rhs_ready, 1)
                    if t == TC - 1:
                        if lev == 2:
                            norm_columns(0, TC - 1)
                        if lev == 3:
                            norm_outputs(0, TC - 1)
                        if lev >= 5:
                            heads_lo(lev - 5)
                        if lev >= 4:
                            gate_heads(lev - 4)
            heads_lo(2)
            norm_columns(TC - 1, TC)
            norm_outputs(TC - 1, TC)
            for g in range(G):
                dve.wait_ge(oT_done, H + g + 1)
                dve.tensor_tensor(group_tiles(NG, g, TC - 1), group_tiles(NG, g, TC - 1), by_tokens(3)[:, g * RING:g * RING + HG, :],
                                  ALU.mult).then_inc(oT_ready, 1)
            for g in range(G):
                dve.wait_ge(cat_hi_ready, H + g + 2)
                dve.tensor_tensor(xT_lo[:, g * HG:(g + 1) * HG, T - P:T], group_tiles(NG, g, TC - 1),
                                  xT_hi[:, g * HG:(g + 1) * HG, T - P:T].bitcast(F32), ALU.subtract).then_inc(cat_lo_ready, 1)
            for k in range(RING, KC):
                w_split_lo(WO + k)
            boundary(2, FFN2, 1.0)
            ffn(FFN2, FC + 1)
            boundary(3, None, 0.5)

        @block.tensor
        def _(pe):
            def transposes(L, m):
                for k in range(KC):
                    mm = pe.transpose(by_tokens(m)[:, k, :], z[:, m, k * P:(k + 1) * P], ident[:, :])
                mm.then_inc(xT_psum, 1)

            def split_mms(dst, w, x, first=True, last=True):
                pe.matmul(dst, w[0], x[0], start=first, stop=False)
                pe.matmul(dst, w[0], x[1], start=False, stop=False)
                return pe.matmul(dst, w[1], x[0], start=False, stop=last)

            def block_ready(n, i=0):
                pe.wait_ge(hi_ready, n + 1 + RING * i)
                pe.wait_ge(lo_ready, n + 1 + RING * i)

            def project(n, bank, i=0, part=None):
                block_ready(n, i)
                s = n % RING
                ts = slice(0, T) if part is None else slice(part * T // 2, (part + 1) * T // 2)
                for k in range(KC):
                    ks = slice(k * P, (k + 1) * P)
                    mm = split_mms(ps[:, bank, ts], (w_hi[:, s, ks], w_lo[:, s, ks]), (xT_hi[:, k, ts], xT_lo[:, k, ts]),
                                   k == 0, k == KC - 1)
                if part != 0:
                    mm.then_inc(block_done, 1)

            def out_mms(n, m, acts, first, last, rows=P):
                s = n % RING
                hi, lo = acts
                for x, w in ((hi, w_hi), (hi, w_lo), (lo, w_hi)):
                    for b in range(2):
                        mm = pe.matmul(ps[:, 2 * m + b, :], x[:, m * P:(m + 1) * P], w[0:rows, s, b * T:(b + 1) * T],
                                       start=first and x is hi and w is w_hi, stop=last and x is lo)
                return mm

            def finish(n0, m, blocks, acts, rows_last=P):
                for b in blocks:
                    lastb = b == RING - 1
                    if m == 0:
                        block_ready(n0 + b)
                    mm = out_mms(n0 + b, m, acts(b), False, lastb, rows_last if lastb else P)
                    if m == TC - 1:
                        mm.then_inc(block_done, 1)
                    elif lastb:
                        mm.then_inc(acc_done, 1)

            def boundary(L, fin, n0):
                def turn(m):
                    pe.wait_ge(xtok_ready, TC * (L - 1) + m + 1) if L else pe.wait_ge(x_loaded[m], 16)
                    transposes(L, m)
                every = range(RING)
                if L:
                    for m in range(3):
                        fin(m, every)
                    if n0 is None:
                        fin(3, every)
                        return
                    turn(0)
                    fin(3, every[:2])
                    turn(1)
                    fin(3, every[2:])
                else:
                    turn(0)
                    turn(1)
                pe.wait_ge(xT_lo_ready, TC * L + 2)
                project(n0, 0, part=0)
                turn(2)
                for j in range(1, RING):
                    project(n0 + j, j, part=0)
                turn(3)
                pe.wait_ge(xT_lo_ready, TC * L + 4)
                for j in range(RING):
                    project(n0 + j, j, part=1)

            def ffn(base, hb):
                def chunk(f, i=0):
                    if f >= 2:
                        pe.wait_ge(silu_ready, hb + f - 1 + 2 * i)
                    project(base + 2 * f, 2 * (f % 2), i)
                    if f >= 2:
                        pe.wait_ge(h_ready, hb + f - 1 + 2 * i)
                    project(base + 2 * f + 1, 2 * (f % 2) + 1, i)
                with pe.Fori(0, FC // 2 - 1) as i:
                    chunk(2, i)
                    chunk(3, i)
                chunk(FC - 1)
                pe.wait_ge(h_ready, hb + FC - 1)
                project(base + NB_IN - 1, 2 * (FC % 2))
                nb = base + NB_IN

                def acts(f, rows=P):
                    s = (nb + f) % RING
                    return h_hi[0:rows, s, :], h_lo[0:rows, s, :]

                def out_block(f, i=0):
                    block_ready(nb + f, i)
                    pe.wait_ge(h_lo_ready, hb + f + 1 + RING * i)
                    for m in ((2, 3, 0, 1) if f == 0 else range(TC)):
                        if f == 0 and m < 2:
                            pe.wait_ge(h_ready, hb + FC + m)
                        mm = out_mms(nb + f, m, acts(f), f == 0, False)
                    mm.then_inc(block_done, 1)
                for f in range(RING):
                    out_block(f)
                with pe.Fori(0, FC // RING - 2) as i:
                    for j in range(RING):
                        out_block(RING + j, i)
                for f in range(RING * (FC // RING - 1), FC + 1 - RING):
                    out_block(f)
                f0 = FC + 1 - RING

                def fin(m, blocks):
                    if m == 0:
                        pe.wait_ge(h_lo_ready, hb + FC)
                        finish(nb + f0, m, blocks[:3], lambda b: acts(f0 + b))
                        pe.wait_ge(h_lo_ready, hb + FC + 1)
                        blocks = blocks[3:]
                    finish(nb + f0, m, blocks, lambda b: acts(f0 + b, P if f0 + b < FC else FR), FR)
                return fin

            pe.wait_ge(const_ready, 2)
            boundary(0, None, FFN1)
            fin = ffn(FFN1, 0)
            boundary(1, fin, MIX)

            def mem_transposes(c):
                if c == 0:
                    pe.wait_ge(mem_loaded, 16)
                else:
                    pe.wait_ge(memT_lo_ready, c)
                for k in range(KC):
                    mm = pe.transpose(by_tokens(3)[:, k, :], mem_tok[:, c, k * P:(k + 1) * P], ident[:, :])
                mm.then_inc(mem_psum, 1)

            def sums(c, i=0):
                pe.wait_ge(sq_ready, c + 1 + RING * i)
                for t in range(TC):
                    at = c * TC + t
                    dst = ps[:, 2, at:at + 1] if isinstance(i, int) else ps[:, 2, bass.ds(at + RING * TC * i, 1)]
                    mm = pe.matmul(dst, sq[:, c % 2, t * P:(t + 1) * P], ones[:, 0:1], start=True, stop=True)
                mm.then_inc(ssq_done, 1)

            def block_to_bank(c, i=0):
                pe.wait_ge(chan_ready, c - 1 + RING * i)
                project(MIX + c, c % 2, i)

            mem_transposes(0)
            pe.wait_ge(chan_ready, 1)
            project(GATE + 4, 0)
            pe.wait_ge(ba_split, 2)
            pe.wait_ge(const_ready, 4)
            pe.transpose(ps[:, 5, 0:TAPS * 3 * H], conv_rows[:, :], ident[0:TAPS * 3 * H, 0:TAPS * 3 * H]).then_inc(conv_psum, 1)
            for k in range(KC):
                mm = split_mms(ps[0:NBA, 4, :], (wba_hi[:, k, :], wba_lo[:, k, :]), (xT_hi[:, k, :], xT_lo[:, k, :]),
                               k == 0, k == KC - 1)
            mm.then_inc(ba_done, 1)
            mem_transposes(1)
            pe.wait_ge(chan_ready, 2)
            project(GATE + 5, 1)
            pe.wait_ge(ba_copied, 1)
            for t in range(TC):
                mm = pe.transpose(ps[:, 5, P + t * NBA:P + (t + 1) * NBA], ba_rows[:, t * P:(t + 1) * P], ident[0:NBA, 0:NBA])
            mm.then_inc(baT_done, 1)
            for j in range(HP):
                block_to_bank(QM - MIX + j)
            pe.wait_ge(memT_lo_ready, 2)
            for j in range(2 * HP):
                n = KV + j
                b = j % 2
                pe.wait_ge(chan_ready, n - MIX - 1)
                block_ready(n)
                s = n % RING
                if j < HP:
                    for k in range(KC):
                        ks = slice(k * P, (k + 1) * P)
                        mm = split_mms(ps[:, b, 0:M], (w_hi[:, s, ks], w_lo[:, s, ks]),
                                       (memT_hi[:, k, :], memT_lo[:, k, :]), k == 0, k == KC - 1)
                else:
                    for c in range(MC):
                        for k in range(KC):
                            ks, cs = slice(k * P, (k + 1) * P), slice(c * P, (c + 1) * P)
                            mm = split_mms(ps[:, b, cs], (memT_hi[:, k, cs], memT_lo[:, k, cs]),
                                           (w_hi[:, s, ks], w_lo[:, s, ks]), k == 0, k == KC - 1)
                mm.then_inc(block_done, 1)
            block_to_bank(QKV - MIX)
            pe.wait_ge(g_ready, 1)
            pe.wait_ge(const_ready, 6)
            pe.matmul(ps[:, 4, 64:64 + H * TC], tri[:, :], col(DEC), start=True, stop=True)
            pe.matmul(ps[:, 4, 96:96 + H * TC], ones[:, :], col(DEC), start=True, stop=True).then_inc(gcum_done, 1)
            block_to_bank(QKV - MIX + 1)
            pe.wait_ge(gcol_ready, 1)

            def attend(c, i=0):
                k = i if c == 2 else 0
                b = QKV - MIX + c
                pe.wait_ge(qm_copied, i + 1)
                for hp in range(HP):
                    for e in range(2):
                        rows = slice(e * MDH, (e + 1) * MDH)
                        mm = pe.matmul(ps[:, 4 + e, hp * M:(hp + 1) * M], qm_now[rows, hp, :], km[rows, hp, :],
                                       start=True, stop=True)
                mm.then_inc(scores_done, 1)
                for j in range(RING):
                    block_to_bank(b + j, k)
                    if c == 2:
                        sums(j, i)
                    if j == 1:
                        pe.wait_ge(prob_ready, i + 1)
                        for u in range(2 * HP):
                            for m in range(MC):
                                mm = pe.transpose(by_tokens(3)[:, u * MC + m, :], prob[:, u, m * P:(m + 1) * P], ident[:, :])
                        mm.then_inc(probT_done, 1)
                    if j == 2:
                        pe.wait_ge(probT_ready, i + 1)
                        for hp in range(HP):
                            for e in range(2):
                                for m in range(MC):
                                    mm = pe.matmul(ps[e * MDH:(e + 1) * MDH, 3, hp * P:(hp + 1) * P],
                                                   vm[:, m, (2 * hp + e) * MDH:(2 * hp + e + 1) * MDH],
                                                   probT[:, (e * HP + hp) * MC + m, :], start=(m == 0), stop=(m == MC - 1))
                        mm.then_inc(pv_done, 1)
            with pe.Fori(0, TC - 1) as i:
                attend(2, i)
            attend(3 * H - RING, TC - 1)
            pe.wait_ge(mem_o_ready, TC)
            pe.wait_ge(conv_done, 3 * H)
            pe.wait_ge(col_vec, 4)

            def grow(t):
                for g in range(G):
                    if t > 1:
                        pe.wait_ge(rhs_ready, nth(t - 2, g))
                    elif t:
                        pe.wait_ge(vb_ready, nth(0, g))
                    for j in range(HG):
                        mm = pe.matmul(bank3(g, 0)[:, j, :], unit(DEC, g * HG + j, t).to_broadcast([P, P]), tri[:, :],
                                       start=True, stop=True)
                    mm.then_inc(grow_done, 1)

            def keys_keys(t, g):
                for j in range(HG):
                    k = tile(NK + g * HG + j, t)
                    mm = pe.matmul(bank3(g, 1)[:, j, :], k, k, start=True, stop=True)
                mm.then_inc(kk_done, 1)

            def output_transposes(j):
                for g in range(G):
                    hh = g * HG + j
                    pe.wait_ge(on_ready, j * G + g + 1)
                    if j:
                        pe.wait_ge(oT_ready, (j - 1) * G + g + 1)
                    for t in range(TC - 1):
                        mm = pe.transpose(bank3(g, 0)[:, t, :], tile(NV + hh, t), ident[:, :])
                    mm.then_inc(oT_done, 1)

            grow(0)
            for g in range(G):
                keys_keys(0, g)
            for t in range(TC):
                for g in range(G):
                    if t:
                        pe.wait_ge(state_ready, nth(t - 1, g))
                        pe.wait_ge(o_ready, nth(t - 1, g))
                    for j in range(HG):
                        hh = g * HG + j
                        pe.matmul(bank3(g, 2)[:, j, :], tile(NK + hh, t), tile(NQ + hh, t), start=True, stop=True)
                        mm = pe.transpose(bank3(g, 3)[:, j, :], tile(NK + hh, t), ident[:, :])
                    mm.then_inc(kq_done, 1)
                for g in range(G):
                    pe.wait_ge(decay_ready, nth(t, g))
                    pe.wait_ge(egrow_ready, nth(t, g))
                    for j in range(HG):
                        mm = pe.transpose(bank3(g, 0)[:, j, :], tile(NV + g * HG + j, t), ident[:, :])
                    mm.then_inc(vT_done, 1)
                for lev in range(1, LEVELS):
                    for g in range(G):
                        pe.wait_ge(inv_ready, nth_level(t, g, lev - 1, 0))
                        pe.wait_ge(part_ready, nth_level(t, g, lev, 0))
                        for j in range(HG):
                            mm = pe.matmul(bank3(g, 1)[:, j, :], part[g][lev % 2][:, j, :], invT[g][:, j, :], start=True, stop=True)
                        mm.then_inc(quart_done, 1)
                    if lev == 2 and t:
                        for g in range(G):
                            pe.wait_ge(vb_ready, nth(t, g))
                            for j in range(HG):
                                hh = g * HG + j
                                mm = pe.matmul(bank3(g, 0)[:, j, :], tile(NK + hh, t), state[:, hh, :], start=True, stop=True)
                            mm.then_inc(ks_done, 1)
                    if lev == 4 and t < TC - 1:
                        grow(t + 1)
                    if lev >= 4 and t == TC - 1:
                        if lev == 4:
                            pe.wait_ge(rhs_ready, nth(t - 1, G - 1))
                        output_transposes(lev - 4)
                    for g in range(G):
                        if lev == 1:
                            pe.wait_ge(qk_ready, nth(t, g))
                            pe.wait_ge(kdec_ready, nth(t, g))
                        pe.wait_ge(quart_ready, nth_level(t, g, lev, 1))
                        for j in range(HG):
                            mm = pe.matmul(bank3(g, 2)[:, j, :], inv[g][:, j, :], quart[g][:, j, :], start=True, stop=True)
                        if lev < LEVELS - 1:
                            for j in range(HG):
                                mm = pe.matmul(bank3(g, 3)[:, j, :], quart[g][:, j, :], inv[g][:, j, :], start=True, stop=True)
                        mm.then_inc(double_done, 1)
                for g in range(G):
                    pe.wait_ge(inv_ready, nth_level(t, g, LEVELS - 1, 0))
                    if t:
                        pe.wait_ge(rhs_ready, nth(t - 1, g))
                    else:
                        pe.wait_ge(vb_ready, nth(t, g))
                    for j in range(HG):
                        mm = pe.matmul(bank3(g, 1)[:, j, :], invT[g][:, j, :], rhs[g][:, j, :], start=True, stop=True)
                    mm.then_inc(u_done, 1)
                for g in range(G):
                    pe.wait_ge(u_ready, nth(t, g))
                    if t < TC - 1:
                        keys_keys(t + 1, g)
                        for j in range(HG):
                            mm = pe.matmul(bank3(g, 2)[:, j, :], kdec[g][:, j, :], quart[g][:, j, :], start=True, stop=True)
                        mm.then_inc(supd_done, 1)
                    pe.wait_ge(qdec_ready, nth(t, g))
                    pe.wait_ge(qk_masked, nth(t, g))
                    for j in range(HG):
                        hh = g * HG + j
                        if t:
                            pe.matmul(bank3(g, 3)[:, j, :], qdec[g][:, j, :], state[:, hh, :], start=True, stop=False)
                        mm = pe.matmul(bank3(g, 3)[:, j, :], qk[g][:, j, :], quart[g][:, j, :], start=(t == 0), stop=True)
                    mm.then_inc(o_done, 1)

            def heads(k):
                return xT_hi[:, k, :], xT_lo[:, k, :]

            def project_out(m):
                for k in range(RING):
                    if m == 0:
                        block_ready(WO + k)
                    mm = out_mms(WO + k, m, heads(k), k == 0, False)
                    if m == TC - 1:
                        mm.then_inc(block_done, 1)
            pe.wait_ge(cat_lo_ready, 1 + H)
            project_out(0)
            pe.wait_ge(o_ready, nth(TC - 1, 0))
            project_out(1)
            for g in range(G):
                pe.wait_ge(o_ready, nth(TC - 1, g))
                for j in range(HG):
                    pe.wait_ge(on_ready, H + j * G + g + 1)
                    mm = pe.transpose(by_tokens(3)[:, g * RING + j, :], tile(NV + g * HG + j, TC - 1), ident[:, :])
                mm.then_inc(oT_done, 1)
            project_out(2)
            pe.wait_ge(cat_lo_ready, 1 + H + G)
            project_out(3)
            boundary(2, lambda m, blocks: finish(WO + RING, m, blocks, lambda b: heads(RING + b)), FFN2)
            fin = ffn(FFN2, FC + 1)
            boundary(3, fin, None)


_INS = ["x", "mem", "l0_ffn1_w_in", "l0_ffn1_w_out", "l0_ln1_g", "l0_ln1_b", "l0_w_in", "l0_conv_w", "l0_a_log",
        "l0_dt_bias", "l0_onorm_g", "l0_w_mem_kv", "l0_w_o", "l0_ln2_g", "l0_ln2_b", "l0_ffn2_w_in", "l0_ffn2_w_out",
        "l0_ln3_g", "l0_ln3_b"]


def kernel(**inputs):
    import numpy as np
    import concourse.bacc as bacc
    from concourse.bass_utils import run_bass_kernel_spmd

    nc = bacc.Bacc("TRN2", target_bir_lowering=False, num_devices=1)
    arrays, aps = {}, {}
    for name in _INS:
        v = np.ascontiguousarray(inputs[name])
        arrays[name + "_dram"] = v
        aps[name] = nc.dram_tensor(name + "_dram", v.shape, mybir.dt.from_np(v.dtype), kind="ExternalInput").ap()
    out = nc.dram_tensor("out_dram", (1, T, D), F32, kind="ExternalOutput").ap()
    build(nc, aps, out)
    r = run_bass_kernel_spmd(nc, [arrays], core_ids=[0])
    return r.results[0]["out_dram"]
```

```python
from contextlib import ExitStack

import concourse.bass as bass
from concourse import mybir

P = 128
T = 512
D = 1024
F = 2752
KC = D // P
TC = T // P
FC = F // P
FR = F - FC * P
NB_IN = 2 * FC + 1
NB_OUT = FC + 1
RING = 4
ALPHA = 2.0 ** 0.25
LN_EPS = 1e-5

H = 6
G = 2
HG = H // G
TAPS = 4
BASE = 32
NB = P // BASE
LEVELS = 3
U = H * TC
M = 256
MC = M // P
MDH = 64
NK, NQ, NV, NG = 0, H, 2 * H, 3 * H
NC = 4 * H
HP = 2
NBA = 2 * H

F32 = mybir.dt.float32
F32R = mybir.dt.float32r
ALU = mybir.AluOpType
ACT = mybir.ActivationFunctionType
AX = mybir.AxisListType

FFN1 = 0
MIX = FFN1 + NB_IN + NB_OUT
GATE = MIX
KV = GATE + H
QM = KV + 2 * HP
QKV = QM + HP
WO = QKV + 3 * H
FFN2 = WO + KC


def build(nc, a, out):
    with ExitStack() as ctx:
        def sb(name, shape, dt=F32):
            return ctx.enter_context(nc.sbuf_tensor(name, shape, dt))

        def sem(name):
            return ctx.enter_context(nc.semaphore(name))

        w_raw = sb("w_raw", [P, RING, D])
        w_hi = sb("w_hi", [P, RING, D], F32R)
        w_lo = sb("w_lo", [P, RING, D], F32R)
        xT_hi = sb("xT_hi", [P, KC, T], F32R)
        xT_lo = sb("xT_lo", [P, KC, T], F32R)
        ax = sb("ax", [P, TC, D])
        ident = sb("ident", [P, P])
        ones = sb("ones", [P, P])
        tri = sb("tri", [P, P])
        below = sb("below", [P, P])
        level = sb("level", [P, LEVELS, P])
        eps = sb("eps", [P, 1])
        stats = sb("stats", [P, TC, 2, 6])
        mv = sb("mv", [P, TC, 2])
        std = sb("std", [P, TC])
        rstd = sb("rstd", [P, TC])
        shift = sb("shift", [P, TC])
        wba_hi = sb("wba_hi", [P, KC, NBA], F32R)
        wba_lo = sb("wba_lo", [P, KC, NBA], F32R)
        conv_w = sb("conv_w", [P, TAPS, 3 * H])
        onorm = sb("onorm", [P, 1])
        a_log = sb("a_log", [P, H])
        dt_bias = sb("dt_bias", [P, H])
        cols = sb("cols", [P, 29, U])
        neg_max = sb("neg_max", [P, 2, 2 * HP])
        prob_sum = sb("prob_sum", [P, 2 * HP])

        block_x = sb("block_x", [U * NB, BASE, BASE])
        state = sb("state", [P, H, P])

        zoff = (nc.sbuf_base + 31) // 32 * 32
        Z_BYTES, H_BYTES, EXT_BYTES, GB_BYTES = 16384, 65536, 9216, 8192
        sb("fence", [P, Z_BYTES + H_BYTES + EXT_BYTES + GB_BYTES + 32], mybir.dt.uint8)

        def placed(name, offset, shape, dt=F32):
            return nc.alloc_sbuf_tensor_at(name, shape, dt, offset=zoff + offset)

        z = placed("z", 0, [P, TC, D])
        memT_hi = placed("memT_hi", 0, [P, KC, M], F32R)
        memT_lo = placed("memT_lo", 8192, [P, KC, M], F32R)
        HREG = Z_BYTES
        h = placed("h", HREG, [P, FC + 1, T])
        h_hi = placed("h_hi", HREG + 45056, [P, RING, T], F32R)
        h_lo = placed("h_lo", HREG + 53248, [P, RING, T], F32R)
        silu_g = placed("silu_g", HREG + 61440, [P, 2, T])
        chan = placed("chan", HREG, [P, NC, T])
        qm = placed("qm", HREG + 49152, [P, 2, T])
        km = placed("km", HREG + 53248, [P, 2, M])
        vm = placed("vm", HREG + 55296, [P, MC, M])
        sq = placed("sq", HREG + 57344, [P, 2, T])
        prob = placed("prob", HREG + 61440, [P, 2 * HP, M])
        ba_rows = placed("ba_rows", HREG + 61440, [NBA, T])
        EXT = HREG + H_BYTES
        mem_tok = placed("mem_tok", EXT, [P, MC, D])
        conv_rows = placed("conv_rows", EXT + 8192, [TAPS * 3 * H, P])
        wba = placed("wba", EXT + 8704, [P, KC, NBA])
        probT = placed("probT", EXT, [P, 2 * HP * MC, P])
        UB = HG * P * 4

        def group_buffers(name, offset):
            return [placed(f"{name}{g}", offset + g * UB, [P, HG, P]) for g in range(G)]
        kdec = group_buffers("kdec", 0)
        amat = group_buffers("amat", 2 * UB)
        qk = group_buffers("qk", 4 * UB)
        qdec = group_buffers("qdec", 6 * UB)
        inv = group_buffers("inv", 8 * UB)
        assert 10 * UB <= 16384
        invT = group_buffers("invT", HREG + 57344)
        quart = group_buffers("quart", HREG + 57344 + 2 * UB)
        assert 57344 + 4 * UB <= 65536
        part = [[placed(f"part{g}{s}", EXT + (2 * g + s) * UB, [P, HG, P]) for s in range(2)] for g in range(G)]
        rhs = group_buffers("rhs", EXT + 4 * UB)
        squares = placed("squares", HREG + 49152, [P, HG, P])
        decay = group_buffers("decay", HREG + 49152 + 4096)
        assert 4096 + 2 * UB <= 8192
        GB = EXT + EXT_BYTES
        ln_g = placed("ln_g", GB, [P, D])
        ln_b = placed("ln_b", GB + 4096, [P, D])
        kk_units = placed("kk_units", 0, [P, U, P])
        block_a = placed("block_a", 12288, [U * NB, BASE, BASE])
        block_decay = placed("block_decay", GB + 4096, [U * NB, BASE, BASE])
        diagonals = placed("diagonals", GB + 4096, [P, 2 * TC, P])
        block_t = placed("block_t", GB + 3072, [U * NB, BASE * BASE // 4])
        x_stack = placed("x_stack", GB, [P, U, BASE])
        colT = placed("colT", EXT + 4096, [U, 2, P])
        block_cols = placed("block_cols", EXT + 5120, [U * NB, 2, BASE])
        kk_dram = nc.dram_tensor("kk_blocks", (U, NB, BASE, BASE), F32, kind="Internal").ap()
        col_dram = nc.dram_tensor("unit_columns", (2, U, P), F32, kind="Internal").ap()
        x_dram = nc.dram_tensor("inverse_blocks", (U, NB, BASE, BASE), F32, kind="Internal").ap()
        assert 6 * UB <= 9216

        ps = ctx.enter_context(nc.psum_tensor("ps", [P, 8, T], F32))

        raw_loaded = [sem(f"raw_loaded{i}") for i in range(RING)]
        hi_ready = sem("hi_ready")
        lo_ready = sem("lo_ready")
        block_done = sem("block_done")
        silu_ready = sem("silu_ready")
        h_ready = sem("h_ready")
        h_hi_ready = sem("h_hi_ready")
        h_lo_ready = sem("h_lo_ready")
        acc_done = sem("acc_done")
        half_done = sem("half_done")
        stats_ready = sem("stats_ready")
        std_ready = sem("std_ready")
        norm_cols = sem("norm_cols")
        normed = sem("normed")
        gained = sem("gained")
        dve_step = sem("dve_step")
        x_loaded = [sem(f"x_loaded{m}") for m in range(TC)]
        small_loaded = sem("small_loaded")
        mem_loaded = sem("mem_loaded")
        gb_loaded = sem("gb_loaded")
        xtok_ready = sem("xtok_ready")
        xlast_ready = sem("xlast_ready")
        ax_ready = sem("ax_ready")
        xT_psum = sem("xT_psum")
        xT_hi_ready = sem("xT_hi_ready")
        xT_lo_ready = sem("xT_lo_ready")
        const_ready = sem("const_ready")
        out_stored = sem("out_stored")
        ba_split = sem("ba_split")
        conv_psum = sem("conv_psum")
        ba_done = sem("ba_done")
        ba_copied = sem("ba_copied")
        baT_done = sem("baT_done")
        kkall_done = sem("kkall_done")
        kk_copied = sem("kk_copied")
        kk_stored = sem("kk_stored")
        colT_done = sem("colT_done")
        colT_ready = sem("colT_ready")
        col_stored = sem("col_stored")
        blocks_loaded = sem("blocks_loaded")
        block_dist = sem("block_dist")
        block_decay_ready = sem("block_decay_ready")
        identity_ready = sem("identity_ready")
        solved = sem("solved")
        x_stored = sem("x_stored")
        x_loaded_back = sem("x_loaded_back")
        mem_o_ready = sem("mem_o_ready")
        mem_psum = sem("mem_psum")
        memT_hi_ready = sem("memT_hi_ready")
        memT_lo_ready = sem("memT_lo_ready")
        conv_step = sem("conv_step")
        conv_done = sem("conv_done")
        tap_ready = sem("tap_ready")
        conv_w_ready = sem("conv_w_ready")
        chan_ready = sem("chan_ready")
        gate_ready = sem("gate_ready")
        sq_ready = sem("sq_ready")
        ssq_done = sem("ssq_done")
        ssq_read = sem("ssq_read")
        scores_done = sem("scores_done")
        negmax_ready = sem("negmax_ready")
        exp_ready = sem("exp_ready")
        prob_ready = sem("prob_ready")
        probT_done = sem("probT_done")
        probT_ready = sem("probT_ready")
        pv_done = sem("pv_done")
        cat_hi_ready = sem("cat_hi_ready")
        cat_lo_ready = sem("cat_lo_ready")
        col_vec = sem("col_vec")
        col_act = sem("col_act")
        g_ready = sem("g_ready")
        gcum_done = sem("gcum_done")
        gcol_ready = sem("gcol_ready")
        grow_done = sem("grow_done")
        kk_done = sem("kk_done")
        kq_done = sem("kq_done")
        vT_done = sem("vT_done")
        dist_ready = sem("dist_ready")
        egrow_ready = sem("egrow_ready")
        decay_ready = sem("decay_ready")
        kdec_ready = sem("kdec_ready")
        vb_ready = sem("vb_ready")
        qk_masked = sem("qk_masked")
        ss_ready = sem("ss_ready")
        qdec_ready = sem("qdec_ready")
        a_ready = sem("a_ready")
        qk_ready = sem("qk_ready")
        part_ready = sem("part_ready")
        inv_ready = sem("inv_ready")
        quart_done = sem("quart_done")
        quart_ready = sem("quart_ready")
        double_done = sem("double_done")
        ks_done = sem("ks_done")
        rhs_ready = sem("rhs_ready")
        u_done = sem("u_done")
        u_ready = sem("u_ready")
        supd_done = sem("supd_done")
        o_done = sem("o_done")
        state_ready = sem("state_ready")
        o_ready = sem("o_ready")
        on_ready = sem("on_ready")
        oT_done = sem("oT_done")
        oT_ready = sem("oT_ready")

        two_piece = {FFN1 + NB_IN - 1, FFN2 + NB_IN - 1}

        def raw_count(n):
            return 16 * sum(2 if b in two_piece else 1 for b in range(n % RING, n + 1, RING))

        def by_k(n, width=P):
            return w_raw[:, n % RING, :].rearrange("p (k c) -> p k c", k=KC)[:, :, 0:width]

        def h_at(rows, f, i, step):
            return h[0:rows, f, :] if isinstance(i, int) else h[0:rows, bass.ds(f + step * i, 1), :]

        def source_chunk(c):
            return c + H if c < H else c - H if c < 2 * H else c

        def pair_bank(m):
            return ps[:, 2 * m:2 * m + 2, :].rearrange("p b t -> p (b t)")

        def by_tokens(m):
            return ps[:, 2 * m:2 * m + 2, :].rearrange("p b (k t) -> p (b k) t", t=P)

        def out_chunk(k):
            return (k + H) % KC

        def col(j):
            return cols[:, j, :]

        def col_ht(j):
            return cols[:, j, :].rearrange("p (h t) -> p h t", h=H)

        def cols_t(j, t0, t1):
            return col_ht(j)[:, :, t0:t1]

        def unit(j, hh, t):
            return cols[:, j, hh * TC + t:hh * TC + t + 1]

        (GA, AA, BC, EA, EB, LNU, U1, EB1, BETA, CORR, RU, SP, DEC, GCUM, GL, DGL, EG, EGL, EDEC,
         KK, R2, RR, BR, BR2, NBG, EPSQ, SS, RO, NEGG) = range(29)

        def bank(g, j):
            return ps[:, 4 * (G - 1 - g) + j, 0:HG * P]

        def bank3(g, j):
            return bank(g, j).rearrange("p (h c) -> p h c", h=HG)

        def tile(c, t):
            return chan[:, c, t * P:(t + 1) * P]

        def group_tiles(first, g, t):
            return chan[:, first + g * HG:first + (g + 1) * HG, t * P:(t + 1) * P]

        def nth(t, g):
            return t * G + g + 1

        def nth_level(t, g, lev, first):
            return (t * (LEVELS - first) + lev - first) * G + g + 1

        block = ctx.enter_context(nc.Block())

        @block.sync
        def _(sp):

            def load(n, dst, src, i=0):
                if n >= RING:
                    sp.wait_ge(hi_ready, n - RING + 1 + RING * i)
                    sp.wait_ge(lo_ready, n - RING + 1 + RING * i)
                sp.dma_start(dst, src).then_inc(raw_loaded[n % RING], 16)

            def load_x(m):
                sp.dma_start(z[:, m, :], a["x"][0, m * P:(m + 1) * P, :]).then_inc(x_loaded[m], 16)

            def ffn_loads(base, w_in, w_out):
                in_cols = w_in.rearrange("(k p) c -> p k c", p=P)
                out_rows = w_out[0:FC * P, :].rearrange("(f p) d -> p f d", p=P)

                def gate_up(b, f, i=0):
                    for j in range(2):
                        n = base + b + j
                        load(n, by_k(n), in_cols[:, :, bass.ds(f * P + j * F, P)], i)
                if base == FFN1:
                    for m in (0, 1):
                        load_x(m)
                    gate_up(0, 0)
                    for m in (2, 3):
                        load_x(m)
                    gate_up(2, 1)
                else:
                    gate_up(0, 0)
                    gate_up(2, 1)
                with sp.Fori(0, FC // 2 - 1) as i:
                    gate_up(4, 2 * i + 2, i)
                    gate_up(6, 2 * i + 3, i)
                gate_up(2 * FC - 2, FC - 1)
                n = base + NB_IN - 1
                load(n, by_k(n, FR), in_cols[:, :, FC * P:F])
                sp.dma_start(w_raw[:, n % RING, :].rearrange("p (k c) -> p k c", k=KC)[:, :, FR:P],
                             in_cols[:, :, F + FC * P:2 * F]).then_inc(raw_loaded[n % RING], 16)
                n = base + NB_IN
                with sp.Fori(0, FC // RING) as i:
                    for j in range(RING):
                        load(n + j, w_raw[:, (n + j) % RING, :], out_rows[:, bass.ds(i * RING + j, 1), :], i)
                for f in range(FC // RING * RING, FC):
                    load(n + f, w_raw[:, (n + f) % RING, :], out_rows[:, f, :])
                load(n + FC, w_raw[0:FR, (n + FC) % RING, :], w_out[FC * P:F, :])

            ffn_loads(FFN1, a["l0_ffn1_w_in"], a["l0_ffn1_w_out"])
            mix_cols = a["l0_w_in"].rearrange("(k p) c -> p k c", p=P)
            for c in range(H):
                load(GATE + c, by_k(GATE + c), mix_cols[:, :, (NG + c) * P:(NG + c + 1) * P])
            kv_cols = a["l0_w_mem_kv"].rearrange("(k p) c -> p k c", p=P)
            for j in range(2 * HP):
                load(KV + j, by_k(KV + j), kv_cols[:, :, j * P:(j + 1) * P])
            for j in range(HP):
                load(QM + j, by_k(QM + j), mix_cols[:, :, NC * P + NBA + j * P:NC * P + NBA + (j + 1) * P])
            for c in range(3 * H):
                at = source_chunk(c) * P
                load(QKV + c, by_k(QKV + c), mix_cols[:, :, at:at + P])
                if c == 2 * H + 3:
                    sp.wait_ge(kk_copied, 3)
                    for b in range(NB):
                        rows = slice(b * BASE, (b + 1) * BASE)
                        sp.dma_start(kk_dram[:, b, :, :].rearrange("u i c -> i u c"), kk_units[rows, :, rows]).then_inc(kk_stored, 16)
                    sp.wait_ge(colT_ready, 1)
                    sp.dma_start(col_dram.rearrange("w u p -> u w p"), colT[:, :, :]).then_inc(col_stored, 16)
                    sp.wait_ge(kk_stored, 16 * NB)
                    sp.dma_start(block_a[:, :, :], kk_dram.rearrange("u b i c -> (u b) i c")).then_inc(blocks_loaded, 16)
                    sp.wait_ge(col_stored, 16)
                    sp.dma_start(block_cols[:, :, :], col_dram.rearrange("w u (b i) -> (u b) w i", b=NB)).then_inc(blocks_loaded, 16)

            o_rows = a["l0_w_o"].rearrange("(k p) d -> p k d", p=P)
            for k in range(KC):
                if k in (RING, RING + 1):
                    half = k - RING
                    rows = slice(half * BASE // 2, (half + 1) * BASE // 2)
                    sp.wait_ge(solved, half + 1)
                    sp.dma_start(x_dram.rearrange("u b i c -> (u b) i c")[:, rows, :], block_x[:, rows, :]).then_inc(x_stored, 16)
                    sp.wait_ge(x_stored, 16 * (half + 1))
                    for b in range(NB):
                        sp.dma_start(x_stack[b * BASE + rows.start:b * BASE + rows.stop, :, :],
                                     x_dram[:, b, rows, :].rearrange("u i c -> i u c")).then_inc(x_loaded_back, 16)
                load(WO + k, w_raw[:, (WO + k) % RING, :], o_rows[:, out_chunk(k), :])
            ffn_loads(FFN2, a["l0_ffn2_w_in"], a["l0_ffn2_w_out"])
            for m in range(TC - 1):
                sp.wait_ge(xtok_ready, 2 * (TC - 1) + m + 1)
                sp.dma_start(out[0, m * P:(m + 1) * P, :], z[:, m, :]).then_inc(out_stored, 16)
            for half in range(2):
                sp.wait_ge(xlast_ready, 3 + half)
                ds = slice(half * T, (half + 1) * T)
                sp.dma_start(out[0, T - P:T, ds], z[:, TC - 1, ds]).then_inc(out_stored, 16)
            sp.wait_ge(out_stored, 16 * (TC + 1))

        @block.gpsimd
        def _(pool):
            made = [0]

            def step(ins):
                made[0] += 1
                ins.then_inc(const_ready, 1)
                pool.wait_ge(const_ready, made[0])

            step(pool.memset(ident[:, :], 0.0))
            step(pool.affine_select(out=ident[:, :], in_=ident[:, :], compare_op=ALU.not_equal, fill=1.0,
                                    base=0, pattern=[[-1, P]], channel_multiplier=1))
            step(pool.memset(eps[:, :], LN_EPS))
            step(pool.memset(ones[:, :], 1.0))
            pool.dma_start(ln_g[:, :], a["l0_ln1_g"].partition_broadcast(P)).then_inc(gb_loaded, 16)
            pool.dma_start(ln_b[:, :], a["l0_ln1_b"].partition_broadcast(P)).then_inc(gb_loaded, 16)
            pool.dma_start(wba[:, :, :], a["l0_w_in"].rearrange("(k p) c -> p k c", p=P)[:, :, NC * P:NC * P + NBA])\
                .then_inc(small_loaded, 16)
            pool.dma_start(conv_rows[:, :], a["l0_conv_w"].rearrange("j (c p) -> (j c) p", p=P)).then_inc(small_loaded, 16)
            pool.dma_start(onorm[:, :], a["l0_onorm_g"].rearrange("(p o) -> p o", o=1)).then_inc(small_loaded, 16)
            pool.dma_start(a_log[:, :], a["l0_a_log"].partition_broadcast(P)).then_inc(small_loaded, 16)
            pool.dma_start(dt_bias[:, :], a["l0_dt_bias"].partition_broadcast(P)).then_inc(small_loaded, 16)
            pool.dma_start(mem_tok[:, :, :], a["mem"][0].rearrange("(c p) d -> p c d", p=P)).then_inc(mem_loaded, 16)
            step(pool.memset(tri[:, :], 1.0))
            step(pool.affine_select(out=tri[:, :], in_=tri[:, :], compare_op=ALU.is_ge, fill=0.0,
                                    base=0, pattern=[[1, P]], channel_multiplier=-1))
            step(pool.memset(below[:, :], 1.0))
            step(pool.affine_select(out=below[:, :], in_=below[:, :], compare_op=ALU.is_gt, fill=0.0,
                                    base=0, pattern=[[-1, P]], channel_multiplier=1))
            for lev in range(LEVELS):
                s = BASE << lev
                view = level[:, lev, :].rearrange("p (b c) -> p b c", c=s)
                step(pool.memset(level[:, lev, :], 1.0))
                step(pool.affine_select(out=view, in_=view, compare_op=ALU.is_ge, fill=0.0, base=0,
                                        pattern=[[-s, P // s], [0, s]], channel_multiplier=1))
                step(pool.affine_select(out=view, in_=view, compare_op=ALU.is_gt, fill=0.0, base=s,
                                        pattern=[[s, P // s], [0, s]], channel_multiplier=-1))
            for lev in range(LEVELS - 1, 0, -1):
                step(pool.tensor_tensor(level[:, lev, :], level[:, lev, :], level[:, lev - 1, :], ALU.subtract))
            step(pool.tensor_tensor(level[:, 1:, :], level[:, 1:, :],
                                    below[:, :].unsqueeze(1).to_broadcast([P, LEVELS - 1, P]), ALU.mult))

            def scale_residual(L):
                for m in range(TC):
                    if L == 0:
                        pool.wait_ge(x_loaded[m], 16)
                    elif m < TC - 1:
                        pool.wait_ge(xtok_ready, (TC - 1) * (L - 1) + m + 1)
                    else:
                        pool.wait_ge(xlast_ready, L)
                    pool.tensor_scalar(ax[:, m, :], z[:, m, :], ALPHA, 1.0, ALU.mult, ALU.mult).then_inc(ax_ready, 1)

            def w_split_lo(n):
                pool.wait_ge(hi_ready, n + 1)
                pool.tensor_tensor(w_lo[:, n % RING, :], w_raw[:, n % RING, :], w_hi[:, n % RING, :].bitcast(F32),
                                   ALU.subtract).then_inc(lo_ready, 1)

            def boundary(L, n0):
                def add_bias(m):
                    pool.wait_ge(gained, (TC - 1) * (L - 1) + m + 1)
                    pool.tensor_tensor(z[:, m, :], z[:, m, :], ln_b[:, :], ALU.add).then_inc(xtok_ready, 1)
                add_bias(0)
                add_bias(1)
                pool.wait_ge(lo_ready, n0)
                w_split_lo(n0)
                add_bias(2)
                for j in range(1, RING):
                    w_split_lo(n0 + j)

            def last_norm():
                for m in range(TC - 1):
                    pool.wait_ge(normed, 2 * TC + m + 1)
                    pool.tensor_tensor(z[:, m, :], z[:, m, :], ln_g[:, :], ALU.mult).then_inc(gained, 1)
                    pool.wait_ge(gained, 2 * (TC - 1) + m + 1)
                    pool.tensor_tensor(z[:, m, :], z[:, m, :], ln_b[:, :], ALU.add).then_inc(xtok_ready, 1)

            def load_gb(L, g, b):
                pool.wait_ge(xtok_ready, (TC - 1) * L)
                pool.wait_ge(xlast_ready, L)
                pool.dma_start(ln_g[:, :], g.partition_broadcast(P)).then_inc(gb_loaded, 16)
                pool.dma_start(ln_b[:, :], b.partition_broadcast(P)).then_inc(gb_loaded, 16)

            scale_residual(0)
            boundary(1, MIX)
            scale_residual(1)
            pool.wait_ge(small_loaded, 16 * 5)
            for hh in range(H):
                pool.wait_ge(chan_ready, hh + 1)
                pool.tensor_scalar(chan[:, NG + hh, :], chan[:, NG + hh, :], onorm[:, 0:1], 1.0,
                                   ALU.mult, ALU.mult).then_inc(gate_ready, 1)

            for c in range(3 * H):
                n = QKV + c + RING
                if c == 0:
                    pool.wait_ge(lo_ready, n)
                w_split_lo(n)
                if H <= c < 2 * H:
                    pool.wait_ge(chan_ready, QKV - MIX + c + 1)
                    if c - H >= 2:
                        pool.wait_ge(ssq_done, c - H - 1)
                    pool.tensor_tensor(sq[:, c % 2, :], chan[:, c, :], chan[:, c, :], ALU.mult).then_inc(sq_ready, 1)
                if c == 2 * RING + 1:
                    pool.memset(block_x[:, :, :], 0.0).then_inc(identity_ready, 1)
                    pool.wait_ge(identity_ready, 1)
                    pool.memset(block_x[:, :, :].rearrange("p i c -> p (i c)")[:, 0:BASE * BASE:BASE + 1], 1.0)\
                        .then_inc(identity_ready, 1)

            def mask3(m):
                return m.unsqueeze(1).to_broadcast([P, HG, P])

            def part_of(t, lev):
                for g in range(G):
                    pool.wait_ge(a_ready, nth(t, g))
                    pool.tensor_tensor(part[g][lev % 2][:, :, :], amat[g][:, :, :], mask3(level[:, lev, :]),
                                       ALU.mult).then_inc(part_ready, 1)

            for t in range(TC):
                part_of(t, 1)
                part_of(t, 2)
                for g in range(G):
                    pool.wait_ge(egrow_ready, nth(t, g))
                    pool.tensor_tensor(qdec[g][:, :, :], qdec[g][:, :, :], group_tiles(NQ, g, t), ALU.mult).then_inc(qdec_ready, 1)
                for g in range(G):
                    pool.wait_ge(qk_ready, nth(t, g))
                    pool.tensor_tensor(qk[g][:, :, :], qk[g][:, :, :], mask3(tri[:, :]), ALU.mult).then_inc(qk_masked, 1)
            pool.wait_ge(inv_ready, nth_level(TC - 1, G - 1, 0, 0))
            load_gb(1, a["l0_ln2_g"], a["l0_ln2_b"])
            boundary(2, FFN2)
            scale_residual(2)
            load_gb(2, a["l0_ln3_g"], a["l0_ln3_b"])
            pool.wait_ge(gb_loaded, 32 * 3)
            last_norm()

        @block.scalar
        def _(act):
            def w_split_hi(n, i=0, rows=P):
                act.wait_ge(raw_loaded[n % RING], raw_count(n) + 16 * i)
                if n >= RING:
                    act.wait_ge(block_done, n - RING + 1 + RING * i)
                act.activation(w_hi[0:rows, n % RING, :], w_raw[0:rows, n % RING, :], ACT.Copy).then_inc(hi_ready, 1)

            def transposed_hi(L, m):
                act.wait_ge(xT_psum, TC * L + m + 1)
                act.activation(xT_hi[:, :, m * P:(m + 1) * P], by_tokens(m), ACT.Copy).then_inc(xT_hi_ready, 1)

            def ffn(base, hb):
                def silu(f, i=0, rows=P):
                    act.wait_ge(block_done, base + 2 * f + 1 + RING * i)
                    if f >= 2:
                        act.wait_ge(h_ready, hb + f - 1 + 2 * i)
                    act.activation(silu_g[0:rows, f % 2, :], ps[0:rows, 2 * (f % 2), :], ACT.Silu).then_inc(silu_ready, 1)

                def chunk(f, i=0):
                    silu(f, i)
                    w_split_hi(base + 2 * f + 4, i)
                    w_split_hi(base + 2 * f + 5, i)

                nb = base + NB_IN

                def out_hi(f, i=0, rows=P):
                    n = nb + f
                    w_split_hi(n, i, rows)
                    act.wait_ge(h_ready, hb + f + 1 + RING * i)
                    act.activation(h_hi[0:rows, n % RING, :], h_at(rows, f, i, RING), ACT.Copy).then_inc(h_hi_ready, 1)
                chunk(0)
                chunk(1)
                with act.Fori(0, (FC - 5) // 2) as i:
                    chunk(2, i)
                    chunk(3, i)
                chunk(FC - 3)
                silu(FC - 2)
                w_split_hi(base + 2 * FC)
                out_hi(0)
                silu(FC - 1)
                out_hi(1)
                silu(FC, rows=FR)
                out_hi(2)
                out_hi(3)
                with act.Fori(0, FC // RING - 1) as i:
                    for j in range(RING):
                        out_hi(RING + j, i)
                for f in range(FC // RING * RING, FC):
                    out_hi(f)
                out_hi(FC, rows=FR)

            def boundary(L, n0):
                def norm(m, halves=1):
                    act.wait_ge(stats_ready, TC * (L - 1) + m + 1)
                    act.activation(std[:, m:m + 1], mv[:, m, 1:2], ACT.Sqrt, bias=eps[:, :]).then_inc(std_ready, 1)
                    act.wait_ge(norm_cols, TC * (L - 1) + m + 1)
                    for half in range(halves):
                        ds = slice(half * D // halves, (half + 1) * D // halves)
                        act.activation(z[:, m, ds], z[:, m, ds], ACT.Identity, bias=shift[:, m:m + 1], scale=rstd[:, m:m + 1])\
                            .then_inc(normed, 1)
                if L == 0:
                    transposed_hi(0, 0)
                    transposed_hi(0, 1)
                    w_split_hi(n0)
                    w_split_hi(n0 + 1)
                    transposed_hi(0, 2)
                    w_split_hi(n0 + 2)
                    w_split_hi(n0 + 3)
                    transposed_hi(0, 3)
                elif n0 is None:
                    for m in range(TC):
                        norm(m, 2 if m == TC - 1 else 1)
                else:
                    norm(0)
                    norm(1)
                    transposed_hi(L, 0)
                    w_split_hi(n0)
                    norm(2)
                    transposed_hi(L, 1)
                    for j in range(1, RING):
                        w_split_hi(n0 + j)
                    norm(3)
                    transposed_hi(L, 2)
                    transposed_hi(L, 3)

            act.wait_ge(const_ready, 3)
            act.activation(std[:, 0:1], eps[:, :], ACT.Copy)
            boundary(0, FFN1)
            act.wait_ge(small_loaded, 16 * 5)
            act.activation(wba_hi[:, :, :], wba[:, :, :], ACT.Copy).then_inc(ba_split, 1)
            ffn(FFN1, 0)
            boundary(1, MIX)


            def mem_hi(c):
                act.wait_ge(mem_psum, c + 1)
                if c == 0:
                    act.wait_ge(ax_ready, 2 * TC)
                act.activation(memT_hi[:, :, c * P:(c + 1) * P], by_tokens(3), ACT.Copy).then_inc(memT_hi_ready, 1)

            def gate(c):
                act.wait_ge(block_done, GATE + c + 1)
                act.activation(chan[:, NG + c, :], ps[:, c if c < RING else c % 2, :], ACT.Silu).then_inc(chan_ready, 1)
                w_split_hi(GATE + c + RING)

            def channel(c):
                act.wait_ge(block_done, QKV + c + 1)
                act.activation(chan[:, c, :], ps[:, c % 2, :], ACT.Copy, scale=conv_w[:, TAPS - 1, c:c + 1]).then_inc(tap_ready, 1)
                if c == 3 * H - 1:
                    decays(0, 1)
                w_split_hi(QKV + c + RING)
                act.wait_ge(conv_done, c + 1)
                act.activation(chan[:, c, :], chan[:, c, :], ACT.Silu).then_inc(chan_ready, 1)

            def column(dst, src, func, need, scale=1.0):
                act.wait_ge(col_vec, need)
                act.activation(dst, src, func, scale=scale).then_inc(col_act, 1)

            for c in range(3):
                gate(c)
            mem_hi(0)
            gate(3)
            gate(4)
            mem_hi(1)
            gate(5)
            for j in range(HP):
                act.wait_ge(block_done, KV + j + 1)
                act.activation(km[:, j, :], ps[:, j % 2, 0:M], ACT.Copy).then_inc(chan_ready, 1)
                w_split_hi(KV + j + RING)
                if j == 0:
                    column(col(EA), col(AA), ACT.Exp, 1)
                    column(col(EB), col(BC), ACT.Exp, 1, -1.0)
                    column(a_log[:, :], a_log[:, :], ACT.Exp, 1)
            act.wait_ge(block_done, KV + 2 * HP)
            for c in range(MC):
                act.activation(vm[:, c, :], ps[:, 0, c * M:(c + 1) * M], ACT.Copy).then_inc(chan_ready, 1)
            w_split_hi(KV + HP + RING)
            w_split_hi(KV + HP + 1 + RING)
            column(col(LNU), col(U1), ACT.Ln, 2)
            for j in range(HP):
                act.wait_ge(block_done, QM + j + 1)
                act.activation(qm[:, j, :], ps[:, j % 2, :], ACT.Copy).then_inc(chan_ready, 1)
                w_split_hi(QM + j + RING)
            act.wait_ge(gcol_ready, 1)
            column(col(EG), col(GCUM), ACT.Exp, 2)
            column(col(EGL), col(GL), ACT.Exp, 2)
            column(col(EDEC), col(DGL), ACT.Exp, 2)

            def copy_products(b):
                act.wait_ge(kkall_done, b + 1)
                if b == 0:
                    act.wait_ge(block_done, QKV)
                act.activation(kk_units[:, b * 2 * TC:(b + 1) * 2 * TC, :], by_tokens(2 if b == 1 else 3), ACT.Copy)\
                    .then_inc(kk_copied, 1)

            def attend(i):
                c = 2 + RING * i
                if i == 2:
                    act.wait_ge(block_dist, 2)
                    act.activation(block_decay[:, :, :], block_decay[:, :, :], ACT.Exp).then_inc(block_decay_ready, 1)
                act.wait_ge(negmax_ready, i + 1)
                for e in range(2):
                    for hp in range(HP):
                        u = e * HP + hp
                        ins = act.activation(prob[:, u, :], ps[:, 4 + e, hp * M:(hp + 1) * M], ACT.Exp,
                                             bias=neg_max[:, 1, u:u + 1], scale=MDH ** -0.5, accum_out=prob_sum[:, u:u + 1])
                ins.then_inc(exp_ready, 1)
                channel(c)
                if i == 1:
                    copy_products(2)
                channel(c + 1)
                act.wait_ge(probT_done, i + 1)
                act.activation(probT[:, :, :], by_tokens(3), ACT.Copy).then_inc(probT_ready, 1)
                channel(c + 2)
                if i == 1:
                    channel(c + 3)
                act.wait_ge(pv_done, i + 1)
                act.activation(qm[:, :, i * P:(i + 1) * P], ps[:, 3, 0:HP * P].rearrange("p (h n) -> p h n", h=HP), ACT.Copy)\
                    .then_inc(mem_o_ready, 1)
                if i == 0:
                    copy_products(0)
                    copy_products(1)
                if i == TC - 1:
                    decays(0, 0)
                if i != 1:
                    channel(c + 3)
                if i == 2:
                    column(col(RR), col(R2), ACT.Sqrt, 3)

            def grown(t, g):
                if t:
                    act.wait_ge(o_done, nth(t - 1, g))
                act.activation(qdec[g][:, :, :], bank3(g, 0), ACT.Exp).then_inc(egrow_ready, 1)

            def decays(t, g):
                act.wait_ge(grow_done, nth(t, g))
                if t:
                    act.wait_ge(qk_ready, nth(t - 1, g))
                    act.wait_ge(a_ready, nth(t - 1, g))
                for j in range(HG):
                    ins = act.activation(decay[g][:, j, :], bank3(g, 0)[:, j, :], ACT.Abs, bias=unit(NEGG, g * HG + j, t))
                ins.then_inc(dist_ready, 1)
                act.wait_ge(dist_ready, nth(t, g))
                act.activation(decay[g][:, :, :], decay[g][:, :, :], ACT.Exp, scale=-1.0).then_inc(decay_ready, 1)
                if t == 0:
                    grown(t, g)

            act.wait_ge(conv_w_ready, 3)
            channel(0)
            channel(1)
            for i in range(TC):
                attend(i)
            act.wait_ge(col_vec, 4)

            def sum_squares(t):
                if t == 0:
                    act.wait_ge(cat_lo_ready, 1)
                for g in range(G):
                    act.wait_ge(o_ready, nth(t, g))
                    if nth(t, g) > 1:
                        act.wait_ge(ss_ready, nth(t, g) - 1)
                    for j in range(HG):
                        ins = act.activation(squares[:, j, :], tile(NV + g * HG + j, t), ACT.Square,
                                             accum_out=unit(SS, g * HG + j, t))
                    ins.then_inc(ss_ready, 1)

            def heads_hi(j):
                for g in range(G):
                    hh = g * HG + j
                    act.wait_ge(oT_ready, j * G + g + 1)
                    act.activation(xT_hi[:, hh, 0:T - P], chan[:, NG + hh, 0:T - P], ACT.Copy).then_inc(cat_hi_ready, 1)

            for t in range(TC):
                if t:
                    for g in range(G):
                        grown(t, g)
                for g in range(G):
                    act.wait_ge(kq_done, nth(t, g))
                    for j in range(HG):
                        ins = act.activation(kdec[g][:, j, :], bank3(g, 3)[:, j, :], ACT.Copy, scale=unit(EDEC, g * HG + j, t))
                    ins.then_inc(kdec_ready, 1)
                if t == 0:
                    act.wait_ge(mem_o_ready, TC)
                    act.activation(xT_hi[:, H:KC, :], qm[:, :, :], ACT.Copy).then_inc(cat_hi_ready, 1)
                for lev in range(1, LEVELS):
                    for g in range(G):
                        act.wait_ge(quart_done, nth_level(t, g, lev, 1))
                        act.activation(quart[g][:, :, :], bank3(g, 1), ACT.Copy).then_inc(quart_ready, 1)
                    if lev == 1:
                        for g in range(G):
                            act.wait_ge(vT_done, nth(t, g))
                            for j in range(HG):
                                ins = act.activation(rhs[g][:, j, :], bank3(g, 0)[:, j, :], ACT.Copy, scale=unit(BR, g * HG + j, t))
                            ins.then_inc(vb_ready, 1)
                        if t == TC - 1:
                            sum_squares(t - 1)
                if t == TC - 1:
                    column(cols_t(RO, 0, TC - 1), cols_t(RO, 0, TC - 1), ACT.Sqrt, 5)
                else:
                    decays(t + 1, 0)
                for g in range(G):
                    act.wait_ge(u_done, nth(t, g))
                    act.activation(quart[g][:, :, :], bank3(g, 1), ACT.Copy).then_inc(u_ready, 1)
                if t < TC - 1:
                    decays(t + 1, 1)
                    if t:
                        sum_squares(t - 1)
                for g in range(G):
                    act.wait_ge(o_done, nth(t, g))
                    act.activation(group_tiles(NV, g, t), bank3(g, 3), ACT.Copy).then_inc(o_ready, 1)
            for j in range(HG):
                heads_hi(j)
            sum_squares(TC - 1)
            column(cols_t(RO, TC - 1, TC), cols_t(RO, TC - 1, TC), ACT.Sqrt, 6)
            for g in range(G):
                act.wait_ge(oT_ready, H + g + 1)
                act.activation(xT_hi[:, g * HG:(g + 1) * HG, T - P:T], group_tiles(NG, g, TC - 1), ACT.Copy).then_inc(cat_hi_ready, 1)
            for k in range(RING, KC):
                w_split_hi(WO + k)
            boundary(2, FFN2)
            ffn(FFN2, FC + 1)
            boundary(3, None)

        @block.vector
        def _(dve):
            steps = [0]

            def then_next(ins):
                steps[0] += 1
                ins.then_inc(dve_step, 1)
                dve.wait_ge(dve_step, steps[0])

            def w_split_lo(n, i=0, rows=P):
                dve.wait_ge(hi_ready, n + 1 + RING * i)
                dve.tensor_tensor(w_lo[0:rows, n % RING, :], w_raw[0:rows, n % RING, :],
                                  w_hi[0:rows, n % RING, :].bitcast(F32), ALU.subtract).then_inc(lo_ready, 1)

            def transposed_lo(L, m):
                dve.wait_ge(xT_hi_ready, TC * L + m + 1)
                dve.tensor_tensor(xT_lo[:, :, m * P:(m + 1) * P], by_tokens(m),
                                  xT_hi[:, :, m * P:(m + 1) * P].bitcast(F32), ALU.subtract).then_inc(xT_lo_ready, 1)

            def ffn(base, hb):
                def gated(f, i=0, rows=P):
                    dve.wait_ge(silu_ready, hb + f + 1 + 2 * i)
                    if rows == P:
                        dve.wait_ge(block_done, base + 2 * f + 2 + RING * i)
                        up = ps[:, 2 * (f % 2) + 1, :]
                    else:
                        up = ps[FR:P, 2 * (f % 2), :]
                    dve.tensor_tensor(h_at(rows, f, i, 2), silu_g[0:rows, f % 2, :], up, ALU.mult).then_inc(h_ready, 1)

                def chunk(f, i=0):
                    gated(f, i)
                    w_split_lo(base + 2 * f + 4, i)
                    w_split_lo(base + 2 * f + 5, i)
                nb = base + NB_IN

                def out_lo(f, i=0, rows=P):
                    n = nb + f
                    w_split_lo(n, i, rows)
                    dve.wait_ge(h_hi_ready, hb + f + 1 + RING * i)
                    dve.tensor_tensor(h_lo[0:rows, n % RING, :], h_at(rows, f, i, RING),
                                      h_hi[0:rows, n % RING, :].bitcast(F32), ALU.subtract).then_inc(h_lo_ready, 1)
                chunk(0)
                chunk(1)
                with dve.Fori(0, (FC - 5) // 2) as i:
                    chunk(2, i)
                    chunk(3, i)
                chunk(FC - 3)
                gated(FC - 2)
                w_split_lo(base + 2 * FC)
                out_lo(0)
                gated(FC - 1)
                out_lo(1)
                gated(FC, rows=FR)
                out_lo(2)
                out_lo(3)
                with dve.Fori(0, FC // RING - 1) as i:
                    for j in range(RING):
                        out_lo(RING + j, i)
                for f in range(FC // RING * RING, FC):
                    out_lo(f)
                out_lo(FC, rows=FR)

            def boundary(L, n0, factor=1.0):
                last = n0 is None

                def residual(m, half=None):
                    if m < TC - 1:
                        dve.wait_ge(acc_done, (TC - 1) * (L - 1) + m + 1)
                    elif half == 0:
                        dve.wait_ge(half_done, 1)
                    else:
                        dve.wait_ge(block_done, (FFN1 + NB_IN + NB_OUT, FFN2, FFN2 + NB_IN + NB_OUT)[L - 1])
                    ds = slice(0, D) if half is None else slice(half * T, (half + 1) * T)
                    then_next(dve.scalar_tensor_tensor(z[:, m, ds], pair_bank(m)[:, ds], factor, ax[:, m, ds], ALU.mult, ALU.add))

                def moments(m):
                    dve.bn_stats(stats[:, m, 0, :], z[:, m, 0:D // 2])
                    then_next(dve.bn_stats(stats[:, m, 1, :], z[:, m, D // 2:D]))
                    aggregate(m)

                def aggregate(m):
                    dve.bn_aggr(mv[:, m, :], stats[:, m, :, :].rearrange("p a s -> p (a s)")).then_inc(stats_ready, 1)

                def columns(m):
                    dve.wait_ge(std_ready, TC * (L - 1) + m + 1)
                    then_next(dve.reciprocal(rstd[:, m:m + 1], std[:, m:m + 1]))
                    dve.tensor_scalar(shift[:, m:m + 1], mv[:, m, 0:1], rstd[:, m:m + 1], -1.0, ALU.mult, ALU.mult)\
                        .then_inc(norm_cols, 1)

                def gain(m):
                    dve.wait_ge(normed, TC * (L - 1) + m + 1)
                    dve.tensor_tensor(z[:, m, :], z[:, m, :], ln_g[:, :], ALU.mult).then_inc(gained, 1)

                def gain_and_bias(m, half=None):
                    ds = slice(0, D) if half is None else slice(half * T, (half + 1) * T)
                    dve.wait_ge(normed, TC * (L - 1) + m + 1 + (half or 0))
                    then_next(dve.tensor_tensor(z[:, m, ds], z[:, m, ds], ln_g[:, ds], ALU.mult))
                    dve.tensor_tensor(z[:, m, ds], z[:, m, ds], ln_b[:, ds], ALU.add).then_inc(xlast_ready, 1)

                if L == 0:
                    transposed_lo(0, 0)
                    transposed_lo(0, 1)
                    w_split_lo(n0)
                    w_split_lo(n0 + 1)
                    transposed_lo(0, 2)
                    w_split_lo(n0 + 2)
                    w_split_lo(n0 + 3)
                    transposed_lo(0, 3)
                    return
                dve.wait_ge(gb_loaded, 32 * L)
                dve.wait_ge(ax_ready, TC * L)
                for m in range(TC - 1):
                    residual(m)
                    if m and not last:
                        gain(m - 1)
                    moments(m)
                    if m == 2 and not last:
                        transposed_lo(L, 0)
                    columns(m)
                if last:
                    for half in range(2):
                        residual(3, half)
                        ins = dve.bn_stats(stats[:, 3, half, :], z[:, 3, half * T:(half + 1) * T])
                    then_next(ins)
                    aggregate(3)
                    columns(3)
                    gain_and_bias(3, 0)
                    gain_and_bias(3, 1)
                else:
                    gain(2)
                    transposed_lo(L, 1)
                    residual(3)
                    moments(3)
                    columns(3)
                    gain_and_bias(3)
                    transposed_lo(L, 2)
                    transposed_lo(L, 3)
                    dve.wait_ge(lo_ready, n0 + RING)

            boundary(0, FFN1)
            dve.wait_ge(ba_split, 1)
            dve.tensor_tensor(wba_lo[:, :, :], wba[:, :, :], wba_hi[:, :, :].bitcast(F32), ALU.subtract).then_inc(ba_split, 1)
            ffn(FFN1, 0)
            boundary(1, MIX, 0.5)

            def mem_lo(c):
                dve.wait_ge(memT_hi_ready, c + 1)
                dve.tensor_tensor(memT_lo[:, :, c * P:(c + 1) * P], by_tokens(3),
                                  memT_hi[:, :, c * P:(c + 1) * P].bitcast(F32), ALU.subtract).then_inc(memT_lo_ready, 1)

            def conv(c):
                dve.wait_ge(tap_ready, c + 1)
                for s in range(1, TAPS):
                    if s > 1:
                        dve.wait_ge(conv_step, (TAPS - 2) * c + s - 1)
                    y = chan[:, c, s:T]
                    ins = dve.scalar_tensor_tensor(y, ps[:, c % 2, 0:T - s], conv_w[:, TAPS - 1 - s, c:c + 1], y, ALU.mult, ALU.add)
                    ins.then_inc(conv_step if s < TAPS - 1 else conv_done, 1)

            for c in range(3):
                w_split_lo(GATE + c + RING)
            mem_lo(0)
            w_split_lo(GATE + 3 + RING)
            dve.wait_ge(conv_psum, 1)
            for c in range(0, 3 * H, H):
                at = source_chunk(c)
                dve.tensor_copy(conv_w[:, :, c:c + H], ps[:, 5, 0:TAPS * 3 * H].rearrange("p (j c) -> p j c", j=TAPS)[:, :, at:at + H])\
                    .then_inc(conv_w_ready, 1)
            dve.wait_ge(conv_w_ready, 3)
            dve.wait_ge(ba_done, 1)
            dve.tensor_copy(ba_rows[:, :], ps[0:NBA, 4, :]).then_inc(ba_copied, 1)
            w_split_lo(GATE + 4 + RING)
            mem_lo(1)
            w_split_lo(GATE + 5 + RING)
            dve.wait_ge(baT_done, 1)
            ba = ps[:, 5, P:P + TC * NBA].rearrange("p (t w h) -> p w h t", t=TC, w=2)
            dve.tensor_copy(col_ht(BC), ba[:, 0])
            then_next(dve.tensor_tensor(col_ht(GA), ba[:, 1], dt_bias[:, :].unsqueeze(2).to_broadcast([P, H, TC]), ALU.add))
            dve.scalar_tensor_tensor(col(AA), col(GA), -1.0, col(GA), ALU.mult, ALU.min).then_inc(col_vec, 1)
            w_split_lo(KV + RING)
            w_split_lo(KV + 1 + RING)
            dve.wait_ge(col_act, 3)
            dve.tensor_scalar(col(U1), col(EA), 1.0, None, ALU.add).then_inc(col_vec, 1)
            then_next(dve.tensor_scalar(col(EB1), col(EB), 1.0, None, ALU.add))
            then_next(dve.reciprocal(col(BETA), col(EB1)))
            dve.wait_ge(col_vec, 2)
            then_next(dve.scalar_tensor_tensor(col(CORR), col(U1), 1.0, col(EA), ALU.subtract, ALU.subtract))
            then_next(dve.reciprocal(col(RU), col(U1)))
            then_next(dve.tensor_tensor(col(CORR), col(CORR), col(RU), ALU.mult))
            w_split_lo(KV + 2 + RING)
            w_split_lo(KV + 3 + RING)
            dve.wait_ge(col_act, 4)
            then_next(dve.tensor_tensor(col(SP), col(LNU), col(CORR), ALU.subtract))
            then_next(dve.scalar_tensor_tensor(col(SP), col(GA), 0.0, col(SP), ALU.max, ALU.add))
            dve.scalar_tensor_tensor(col_ht(DEC), col_ht(SP), -1.0, a_log[:, :].unsqueeze(2).to_broadcast([P, H, TC]),
                                     ALU.mult, ALU.mult).then_inc(g_ready, 1)
            w_split_lo(QM + RING)
            dve.wait_ge(gcum_done, 1)
            dve.tensor_copy(col(GCUM), ps[:, 4, 64:64 + H * TC])
            then_next(dve.tensor_copy(col(GL), ps[:, 4, 96:96 + H * TC]))
            dve.tensor_scalar(col(NEGG), col(GCUM), -1.0, None, ALU.mult)
            dve.tensor_tensor(col(DGL), col(GL), col(GCUM), ALU.subtract).then_inc(gcol_ready, 1)
            w_split_lo(QM + 1 + RING)

            def substitute(first, last):
                for j in range(first, last):
                    shape = [U * NB, BASE - 1 - j, j + 1]
                    product = block_t[:, 0:shape[1] * shape[2]].rearrange("p (i c) -> p i c", c=j + 1)
                    then_next(dve.tensor_tensor(product, block_a[:, j + 1:BASE, j:j + 1].to_broadcast(shape),
                                                block_x[:, j:j + 1, 0:j + 1].to_broadcast(shape), ALU.mult))
                    rest = block_x[:, j + 1:BASE, 0:j + 1]
                    ins = dve.tensor_tensor(rest, rest, product, ALU.subtract)
                    if j == BASE // 2 - 1:
                        ins.then_inc(solved, 1)
                        dve.wait_ge(solved, 1)
                        continue
                    if j < BASE - 2:
                        then_next(ins)
                    else:
                        ins.then_inc(solved, 1)

            def system(t, g):
                dve.wait_ge(kk_done, nth(t, g))
                dve.wait_ge(decay_ready, nth(t, g))
                for j in range(HG):
                    ins = dve.scalar_tensor_tensor(amat[g][:, j, :], bank3(g, 1)[:, j, :], unit(BR2, g * HG + j, t),
                                                   decay[g][:, j, :], ALU.mult, ALU.mult)
                ins.then_inc(a_ready, 1)

            def squared_keys(b):
                us = slice(b * 2 * TC, (b + 1) * 2 * TC)
                dve.wait_ge(kk_copied, b + 1)
                then_next(dve.tensor_tensor(diagonals[:, :, :], kk_units[:, us, :],
                                            ident[:, :].unsqueeze(1).to_broadcast([P, 2 * TC, P]), ALU.mult))
                then_next(dve.tensor_reduce(cols[:, KK, us], diagonals[:, :, :], AX.X, ALU.add))

            cuts = (0, 4, 9, 14, 17, 20, 25, BASE - 1)

            def substitute_part(k):
                substitute(cuts[k], cuts[k + 1])

            def attend(i):
                c = 2 + RING * i
                dve.wait_ge(scores_done, i + 1)
                then_next(dve.tensor_reduce(neg_max[:, 0, :], ps[:, 4:6, :].rearrange("p e (h m) -> p (e h) m", h=HP), AX.X, ALU.max))
                dve.tensor_scalar(neg_max[:, 1, :], neg_max[:, 0, :], -(MDH ** -0.5), None, ALU.mult).then_inc(negmax_ready, 1)
                if i == 2:
                    dve.wait_ge(block_decay_ready, 1)
                    then_next(dve.tensor_tensor(block_a[:, :, :], block_a[:, :, :], block_decay[:, :, :], ALU.mult))
                    then_next(dve.tensor_tensor(block_a[:, :, :], block_a[:, :, :],
                                                block_cols[:, 1, :].unsqueeze(2).to_broadcast([U * NB, BASE, BASE]), ALU.mult))
                conv(c)
                dve.wait_ge(exp_ready, i + 1)
                then_next(dve.reciprocal(prob_sum[:, :], prob_sum[:, :]))
                dve.tensor_tensor(prob[:, :, :], prob[:, :, :], prob_sum[:, :].unsqueeze(2).to_broadcast([P, 2 * HP, M]),
                                  ALU.mult).then_inc(prob_ready, 1)
                if i == 2:
                    dve.wait_ge(identity_ready, 2)
                    substitute_part(0)
                if i == 3:
                    substitute_part(4)
                if i == 1:
                    squared_keys(1)
                conv(c + 1)
                if i == 2:
                    substitute_part(1)
                if i == 1:
                    squared_keys(2)
                    then_next(dve.tensor_scalar(col(KK), col(KK), 1e-6, None, ALU.add))
                    then_next(dve.reciprocal(col(R2), col(KK)))
                    dve.tensor_tensor(col(BR2), col(BETA), col(R2), ALU.mult).then_inc(col_vec, 1)
                if i == 3:
                    dve.wait_ge(ssq_done, H)
                    dve.tensor_scalar(col(EPSQ), ps[:, 2, 0:U], 1e-6, LN_EPS * P, ALU.add, ALU.mult).then_inc(ssq_read, 1)
                    dve.wait_ge(col_act, 8)
                    dve.tensor_tensor(col(BR), col(BETA), col(RR), ALU.mult)
                    dve.scalar_tensor_tensor(col(NBG), col(BR2), -1.0, col(EG), ALU.mult, ALU.mult).then_inc(col_vec, 1)
                    substitute_part(5)
                conv(c + 2)
                if i == 2:
                    substitute_part(2)
                if i == 3:
                    substitute_part(6)
                    system(0, 0)
                if i == 1:
                    dve.wait_ge(colT_done, 1)
                    dve.tensor_copy(colT[:, :, :].rearrange("u w p -> u (w p)"), ps[0:U, 3, 0:2 * P]).then_inc(colT_ready, 1)
                conv(c + 3)
                if i == 0:
                    squared_keys(0)
                if i == 1:
                    dve.wait_ge(blocks_loaded, 32)
                    gc = block_cols[:, 0, :]
                    shape = [U * NB, BASE, BASE]
                    dve.tensor_tensor(block_decay[:, :, :], gc.unsqueeze(2).to_broadcast(shape),
                                      gc.unsqueeze(1).to_broadcast(shape), ALU.subtract).then_inc(block_dist, 1)
                    dve.wait_ge(block_dist, 1)
                    dve.tensor_scalar(block_decay[:, :, :], block_decay[:, :, :], 0.0, None, ALU.min).then_inc(block_dist, 1)
                if i == 2:
                    substitute_part(3)
            conv(0)
            conv(1)
            for i in range(TC):
                attend(i)

            def new_state(t, g):
                dve.wait_ge(supd_done, nth(t, g))
                dve.wait_ge(o_done, nth(t, g))
                if t == 0:
                    ins = dve.tensor_copy(state[:, g * HG:(g + 1) * HG, :], bank3(g, 2))
                else:
                    for j in range(HG):
                        ins = dve.scalar_tensor_tensor(state[:, g * HG + j, :], state[:, g * HG + j, :], unit(EGL, g * HG + j, t),
                                                       bank3(g, 2)[:, j, :], ALU.mult, ALU.add)
                ins.then_inc(state_ready, 1)

            def first_level(t, g):
                if t == 0:
                    dve.wait_ge(x_loaded_back, 2 * 16 * NB)
                shape = [P, HG, NB, BASE]
                x = x_stack[:, :, :].rearrange("p (h t) c -> p h t c", h=H)[:, g * HG:(g + 1) * HG, t, :]
                within = level[:, 0, :].rearrange("p (b c) -> p b c", b=NB)
                then_next(dve.tensor_tensor(inv[g][:, :, :].rearrange("p h (b c) -> p h b c", b=NB),
                                            x.unsqueeze(2).to_broadcast(shape), within.unsqueeze(1).to_broadcast(shape), ALU.mult))
                dve.transpose(invT[g][:, :, :].rearrange("p h c -> p (h c)"), inv[g][:, :, :].rearrange("p h c -> p (h c)"))\
                    .then_inc(inv_ready, 1)

            def norm_columns(t0, t1):
                dve.wait_ge(ss_ready, nth(t1 - 1, G - 1))
                dve.scalar_tensor_tensor(cols_t(RO, t0, t1), cols_t(SS, t0, t1), 1.0 / P, cols_t(EPSQ, t0, t1), ALU.mult, ALU.add)\
                    .then_inc(col_vec, 1)

            def norm_outputs(t0, t1):
                dve.wait_ge(col_act, 9 if t0 == 0 else 10)
                then_next(dve.reciprocal(cols_t(RO, t0, t1), cols_t(RO, t0, t1)))
                for j in range(HG):
                    for g in range(G):
                        hh = g * HG + j
                        o = chan[:, NV + hh, t0 * P:t1 * P].rearrange("p (t c) -> p t c", c=P)
                        dve.tensor_tensor(o, o, col_ht(RO)[:, hh, t0:t1].unsqueeze(2).to_broadcast([P, t1 - t0, P]), ALU.mult)\
                            .then_inc(on_ready, 1)

            def gate_heads(j):
                for g in range(G):
                    hh = g * HG + j
                    spare = (0, 2, 1)[j]
                    dve.wait_ge(oT_done, j * G + g + 1)
                    dve.tensor_tensor(chan[:, NG + hh, 0:T - P], chan[:, NG + hh, 0:T - P], bank(g, spare), ALU.mult).then_inc(oT_ready, 1)

            def heads_lo(j):
                for g in range(G):
                    hh = g * HG + j
                    dve.wait_ge(cat_hi_ready, j * G + g + 2)
                    dve.tensor_tensor(xT_lo[:, hh, 0:T - P], chan[:, NG + hh, 0:T - P], xT_hi[:, hh, 0:T - P].bitcast(F32),
                                      ALU.subtract).then_inc(cat_lo_ready, 1)

            assert (TC - 1) == HG
            for t in range(TC):
                if t:
                    system(t, 0)
                if t:
                    new_state(t - 1, 0)
                system(t, 1)
                first_level(t, 0)
                if t:
                    new_state(t - 1, 1)
                first_level(t, 1)
                for g in range(G):
                    dve.wait_ge(kq_done, nth(t, g))
                    dve.tensor_tensor(qk[g][:, :, :], bank3(g, 2), decay[g][:, :, :], ALU.mult).then_inc(qk_ready, 1)
                if t == 0:
                    dve.wait_ge(cat_hi_ready, 1)
                    dve.tensor_tensor(xT_lo[:, H:KC, :], qm[:, :, :], xT_hi[:, H:KC, :].bitcast(F32), ALU.subtract)\
                        .then_inc(cat_lo_ready, 1)
                for lev in range(1, LEVELS):
                    for g in range(G):
                        dve.wait_ge(double_done, nth_level(t, g, lev, 1))
                        ins = dve.tensor_tensor(invT[g][:, :, :], invT[g][:, :, :], bank3(g, 2), ALU.subtract)
                        if lev < LEVELS - 1:
                            ins = dve.tensor_tensor(inv[g][:, :, :], inv[g][:, :, :], bank3(g, 3), ALU.subtract)
                        ins.then_inc(inv_ready, 1)
                    if lev == 1 and t:
                        for g in range(G):
                            dve.wait_ge(ks_done, nth(t - 1, g))
                            for j in range(HG):
                                ins = dve.scalar_tensor_tensor(rhs[g][:, j, :], bank3(g, 0)[:, j, :], unit(NBG, g * HG + j, t),
                                                               rhs[g][:, j, :], ALU.mult, ALU.add)
                            ins.then_inc(rhs_ready, 1)
                        if t == TC - 1:
                            norm_columns(0, TC - 1)
            norm_outputs(0, TC - 1)
            for j in range(HG):
                gate_heads(j)
            for j in range(HG):
                heads_lo(j)
            norm_columns(TC - 1, TC)
            norm_outputs(TC - 1, TC)
            for g in range(G):
                dve.wait_ge(oT_done, H + g + 1)
                dve.tensor_tensor(group_tiles(NG, g, TC - 1), group_tiles(NG, g, TC - 1), by_tokens(3)[:, g * RING:g * RING + HG, :],
                                  ALU.mult).then_inc(oT_ready, 1)
            for g in range(G):
                dve.wait_ge(cat_hi_ready, H + g + 2)
                dve.tensor_tensor(xT_lo[:, g * HG:(g + 1) * HG, T - P:T], group_tiles(NG, g, TC - 1),
                                  xT_hi[:, g * HG:(g + 1) * HG, T - P:T].bitcast(F32), ALU.subtract).then_inc(cat_lo_ready, 1)
            dve.wait_ge(lo_ready, WO + RING)
            for k in range(RING, KC):
                w_split_lo(WO + k)
            boundary(2, FFN2, 1.0)
            ffn(FFN2, FC + 1)
            boundary(3, None, 0.5)

        @block.tensor
        def _(pe):
            def transposes(L, m):
                for k in range(KC):
                    mm = pe.transpose(by_tokens(m)[:, k, :], z[:, m, k * P:(k + 1) * P], ident[:, :])
                mm.then_inc(xT_psum, 1)

            def split_mms(dst, w, x, first=True, last=True):
                pe.matmul(dst, w[0], x[0], start=first, stop=False)
                pe.matmul(dst, w[0], x[1], start=False, stop=False)
                return pe.matmul(dst, w[1], x[0], start=False, stop=last)

            def block_ready(n, i=0):
                pe.wait_ge(hi_ready, n + 1 + RING * i)
                pe.wait_ge(lo_ready, n + 1 + RING * i)

            def project(n, bank, i=0, part=None):
                block_ready(n, i)
                s = n % RING
                ts = slice(0, T) if part is None else slice(part * T // 2, (part + 1) * T // 2)
                for k in range(KC):
                    ks = slice(k * P, (k + 1) * P)
                    mm = split_mms(ps[:, bank, ts], (w_hi[:, s, ks], w_lo[:, s, ks]), (xT_hi[:, k, ts], xT_lo[:, k, ts]),
                                   k == 0, k == KC - 1)
                if part != 0:
                    mm.then_inc(block_done, 1)

            def out_mms(n, m, acts, first, last, rows=P, banks=(0, 1)):
                s = n % RING
                hi, lo = acts
                for x, w in ((hi, w_hi), (hi, w_lo), (lo, w_hi)):
                    for b in banks:
                        mm = pe.matmul(ps[:, 2 * m + b, :], x[:, m * P:(m + 1) * P], w[0:rows, s, b * T:(b + 1) * T],
                                       start=first and x is hi and w is w_hi, stop=last and x is lo)
                return mm

            def finish(n0, m, blocks, acts, rows_last=P, by_bank=False):
                for banks in ((0,), (1,)) if by_bank else ((0, 1),):
                    for b in blocks:
                        lastb = b == RING - 1
                        if m == 0:
                            block_ready(n0 + b)
                        mm = out_mms(n0 + b, m, acts(b), False, lastb, rows_last if lastb else P, banks)
                        if m < TC - 1:
                            if lastb:
                                mm.then_inc(acc_done, 1)
                        elif banks == (0,):
                            if lastb:
                                mm.then_inc(half_done, 1)
                        else:
                            mm.then_inc(block_done, 1)

            def boundary(L, fin, n0):
                def turn(m):
                    if L == 0:
                        pe.wait_ge(x_loaded[m], 16)
                    elif m < TC - 1:
                        pe.wait_ge(xtok_ready, (TC - 1) * (L - 1) + m + 1)
                    else:
                        pe.wait_ge(xlast_ready, L)
                    transposes(L, m)
                every = range(RING)
                if L == 0:
                    turn(0)
                    turn(1)
                else:
                    for m in range(3):
                        fin(m, every)
                    if n0 is None:
                        fin(3, every, True)
                        return
                    turn(0)
                    fin(3, every[:-1])
                    turn(1)
                    fin(3, every[-1:])
                pe.wait_ge(xT_lo_ready, TC * L + 2)
                project(n0, 0, part=0)
                turn(2)
                project(n0 + 1, 1, part=0)
                if L == 0:
                    turn(3)
                project(n0 + 2, 2, part=0)
                if L:
                    turn(3)
                project(n0 + 3, 3, part=0)
                pe.wait_ge(xT_lo_ready, TC * L + 4)
                for j in range(RING):
                    project(n0 + j, j, part=1)

            def ffn(base, hb):
                def chunk(f, i=0):
                    if f >= 2:
                        pe.wait_ge(silu_ready, hb + f - 1 + 2 * i)
                    project(base + 2 * f, 2 * (f % 2), i)
                    if f >= 2:
                        pe.wait_ge(h_ready, hb + f - 1 + 2 * i)
                    project(base + 2 * f + 1, 2 * (f % 2) + 1, i)
                with pe.Fori(0, FC // 2 - 1) as i:
                    chunk(2, i)
                    chunk(3, i)
                chunk(FC - 1)
                pe.wait_ge(h_ready, hb + FC - 1)
                project(base + NB_IN - 1, 2 * (FC % 2))
                nb = base + NB_IN

                def acts(f, rows=P):
                    s = (nb + f) % RING
                    return h_hi[0:rows, s, :], h_lo[0:rows, s, :]

                def out_block(f, i=0):
                    block_ready(nb + f, i)
                    pe.wait_ge(h_lo_ready, hb + f + 1 + RING * i)
                    for m in ((2, 3, 0, 1) if f == 0 else range(TC)):
                        if f == 0 and m < 2:
                            pe.wait_ge(h_ready, hb + FC + m)
                        mm = out_mms(nb + f, m, acts(f), f == 0, False)
                    mm.then_inc(block_done, 1)
                for f in range(RING):
                    out_block(f)
                with pe.Fori(0, FC // RING - 2) as i:
                    for j in range(RING):
                        out_block(RING + j, i)
                for f in range(RING * (FC // RING - 1), FC + 1 - RING):
                    out_block(f)
                f0 = FC + 1 - RING

                def fin(m, blocks, by_bank=False):
                    if m == 0:
                        pe.wait_ge(h_lo_ready, hb + FC)
                        finish(nb + f0, m, blocks[:3], lambda b: acts(f0 + b))
                        pe.wait_ge(h_lo_ready, hb + FC + 1)
                        blocks = blocks[3:]
                    finish(nb + f0, m, blocks, lambda b: acts(f0 + b, P if f0 + b < FC else FR), FR, by_bank)
                return fin

            pe.wait_ge(const_ready, 2)
            boundary(0, None, FFN1)
            fin = ffn(FFN1, 0)
            boundary(1, fin, MIX)

            def mem_transposes(c):
                if c == 0:
                    pe.wait_ge(mem_loaded, 16)
                else:
                    pe.wait_ge(memT_lo_ready, c)
                for k in range(KC):
                    mm = pe.transpose(by_tokens(3)[:, k, :], mem_tok[:, c, k * P:(k + 1) * P], ident[:, :])
                mm.then_inc(mem_psum, 1)

            def sums(c):
                pe.wait_ge(sq_ready, c - H + 1)
                for t in range(TC):
                    at = (c - H) * TC + t
                    mm = pe.matmul(ps[:, 2, at:at + 1], sq[:, c % 2, t * P:(t + 1) * P], ones[:, 0:1], start=True, stop=True)
                mm.then_inc(ssq_done, 1)

            def block_to_bank(c):
                if c < QKV - MIX + 2:
                    pe.wait_ge(chan_ready, c - 1)
                else:
                    pe.wait_ge(conv_done, c - 1 - (QKV - MIX))
                project(MIX + c, c % 2)

            mem_transposes(0)
            pe.wait_ge(chan_ready, 1)
            project(GATE + 4, 0)
            pe.wait_ge(ba_split, 2)
            pe.wait_ge(const_ready, 4)
            pe.transpose(ps[:, 5, 0:TAPS * 3 * H], conv_rows[:, :], ident[0:TAPS * 3 * H, 0:TAPS * 3 * H]).then_inc(conv_psum, 1)
            for k in range(KC):
                mm = split_mms(ps[0:NBA, 4, :], (wba_hi[:, k, :], wba_lo[:, k, :]), (xT_hi[:, k, :], xT_lo[:, k, :]),
                               k == 0, k == KC - 1)
            mm.then_inc(ba_done, 1)
            mem_transposes(1)
            pe.wait_ge(chan_ready, 2)
            project(GATE + 5, 1)
            pe.wait_ge(ba_copied, 1)
            for t in range(TC):
                mm = pe.transpose(ps[:, 5, P + t * NBA:P + (t + 1) * NBA], ba_rows[:, t * P:(t + 1) * P], ident[0:NBA, 0:NBA])
            mm.then_inc(baT_done, 1)
            pe.wait_ge(memT_lo_ready, 2)
            for j in range(HP):
                n = KV + j
                pe.wait_ge(chan_ready, n - MIX - 1)
                block_ready(n)
                s = n % RING
                for k in range(KC):
                    ks = slice(k * P, (k + 1) * P)
                    mm = split_mms(ps[:, j % 2, 0:M], (w_hi[:, s, ks], w_lo[:, s, ks]),
                                   (memT_hi[:, k, :], memT_lo[:, k, :]), k == 0, k == KC - 1)
                mm.then_inc(block_done, 1)
            n = KV + HP
            pe.wait_ge(chan_ready, n - MIX - 1)
            block_ready(n + 1)
            s = n % RING
            assert s + 1 < RING and MC * M == T
            for c in range(MC):
                for k in range(KC):
                    ks, cs = slice(k * P, (k + 1) * P), slice(c * P, (c + 1) * P)
                    mm = split_mms(ps[:, 0, c * M:(c + 1) * M].rearrange("p (s n) -> p s n", s=2), (memT_hi[:, k, cs], memT_lo[:, k, cs]),
                                   (w_hi[:, s:s + 2, ks], w_lo[:, s:s + 2, ks]), k == 0, k == KC - 1)
            mm.then_inc(block_done, 2)
            pe.wait_ge(chan_ready, QM - MIX)
            for j in range(HP):
                block_to_bank(QM - MIX + j)
            block_to_bank(QKV - MIX)
            pe.wait_ge(g_ready, 1)
            pe.wait_ge(const_ready, 6)
            pe.matmul(ps[:, 4, 64:64 + H * TC], tri[:, :], col(DEC), start=True, stop=True)
            pe.matmul(ps[:, 4, 96:96 + H * TC], ones[:, :], col(DEC), start=True, stop=True).then_inc(gcum_done, 1)
            block_to_bank(QKV - MIX + 1)
            pe.wait_ge(gcol_ready, 1)

            def products(b, bank0):
                pe.wait_ge(chan_ready, QKV - MIX + 2 * b + 2)
                for hh in (2 * b, 2 * b + 1):
                    for t in range(TC):
                        mm = pe.matmul(ps[:, bank0 + hh % 2, t * P:(t + 1) * P], tile(NK + hh, t), tile(NK + hh, t), start=True, stop=True)
                mm.then_inc(kkall_done, 1)

            def attend(i):
                c = 2 + RING * i
                if i == 1:
                    pe.wait_ge(kk_copied, 2)
                for hp in range(HP):
                    for e in range(2):
                        rows = slice(e * MDH, (e + 1) * MDH)
                        mm = pe.matmul(ps[:, 4 + e, hp * M:(hp + 1) * M], qm[rows, hp, i * P:(i + 1) * P], km[rows, hp, :],
                                       start=True, stop=True)
                mm.then_inc(scores_done, 1)
                for j in range(RING):
                    if (i, j) == (TC - 1, RING - 1):
                        grow(0, 0)
                        keys_keys(0, 0)
                        keys_queries(0, 0)
                    block_to_bank(QKV - MIX + c + j)
                    if H <= c + j - 2 < 2 * H:
                        sums(c + j - 2)
                    if i == 1 and j == 0:
                        products(2, 6)
                    if j == 1:
                        if i == 1:
                            pe.wait_ge(kk_copied, 3)
                        pe.wait_ge(prob_ready, i + 1)
                        for u in range(2 * HP):
                            for m in range(MC):
                                mm = pe.transpose(by_tokens(3)[:, u * MC + m, :], prob[:, u, m * P:(m + 1) * P], ident[:, :])
                        mm.then_inc(probT_done, 1)
                    if i == 1 and j == 2:
                        pe.wait_ge(col_vec, 3)
                        pe.wait_ge(mem_o_ready, 1)
                        pe.transpose(ps[0:U, 3, 0:P], col(GCUM), ident[:, :])
                        pe.transpose(ps[0:U, 3, P:2 * P], col(BR2), ident[:, :]).then_inc(colT_done, 1)
                    if j == (3 if i == 1 else 2):
                        pe.wait_ge(probT_ready, i + 1)
                        if i == 1:
                            pe.wait_ge(colT_ready, 1)
                        for hp in range(HP):
                            for e in range(2):
                                for m in range(MC):
                                    mm = pe.matmul(ps[e * MDH:(e + 1) * MDH, 3, hp * P:(hp + 1) * P],
                                                   vm[:, m, (2 * hp + e) * MDH:(2 * hp + e + 1) * MDH],
                                                   probT[:, (e * HP + hp) * MC + m, :], start=(m == 0), stop=(m == MC - 1))
                        mm.then_inc(pv_done, 1)
                        if i == 0:
                            products(0, 6)
                            products(1, 4)
            def grow(t, g):
                if t > 1:
                    pe.wait_ge(rhs_ready, nth(t - 2, g))
                elif t:
                    pe.wait_ge(vb_ready, nth(0, g))
                for j in range(HG):
                    mm = pe.matmul(bank3(g, 0)[:, j, :], unit(DEC, g * HG + j, t).to_broadcast([P, P]), tri[:, :],
                                   start=True, stop=True)
                mm.then_inc(grow_done, 1)

            def keys_keys(t, g):
                for j in range(HG):
                    k = tile(NK + g * HG + j, t)
                    mm = pe.matmul(bank3(g, 1)[:, j, :], k, k, start=True, stop=True)
                mm.then_inc(kk_done, 1)

            def keys_queries(t, g):
                for j in range(HG):
                    hh = g * HG + j
                    pe.matmul(bank3(g, 2)[:, j, :], tile(NK + hh, t), tile(NQ + hh, t), start=True, stop=True)
                    mm = pe.transpose(bank3(g, 3)[:, j, :], tile(NK + hh, t), ident[:, :])
                mm.then_inc(kq_done, 1)

            def value_transposes(t, g):
                pe.wait_ge(decay_ready, nth(t, g))
                pe.wait_ge(egrow_ready, nth(t, g))
                if t == 0:
                    pe.wait_ge(chan_ready, QKV - MIX + NV + (g + 1) * HG)
                for j in range(HG):
                    mm = pe.transpose(bank3(g, 0)[:, j, :], tile(NV + g * HG + j, t), ident[:, :])
                mm.then_inc(vT_done, 1)

            for i in range(TC):
                attend(i)

            pe.wait_ge(conv_done, 3 * H - 1)
            grow(0, 1)
            value_transposes(0, 0)
            pe.wait_ge(ssq_read, 1)
            pe.wait_ge(mem_o_ready, TC)
            keys_queries(0, 1)
            pe.wait_ge(conv_done, 3 * H)
            keys_keys(0, 1)

            def output_transposes(j):
                for g in range(G):
                    hh = g * HG + j
                    pe.wait_ge(on_ready, j * G + g + 1)
                    for t in range(TC - 1):
                        mm = pe.transpose(bank3(g, (0, 2, 1)[j])[:, t, :], tile(NV + hh, t), ident[:, :])
                    mm.then_inc(oT_done, 1)

            for t in range(TC):
                if t:
                    for g in range(G):
                        pe.wait_ge(state_ready, nth(t - 1, g))
                        pe.wait_ge(o_ready, nth(t - 1, g))
                        keys_queries(t, g)
                for g in range(G):
                    if (t, g) != (0, 0):
                        value_transposes(t, g)
                for lev in range(1, LEVELS):
                    for g in range(G):
                        pe.wait_ge(inv_ready, nth_level(t, g, lev - 1, 0))
                        pe.wait_ge(part_ready, nth_level(t, g, lev, 1))
                        for j in range(HG):
                            mm = pe.matmul(bank3(g, 1)[:, j, :], part[g][lev % 2][:, j, :], invT[g][:, j, :], start=True, stop=True)
                        mm.then_inc(quart_done, 1)
                    for g in range(G):
                        if lev == 1:
                            pe.wait_ge(qk_ready, nth(t, g))
                            pe.wait_ge(kdec_ready, nth(t, g))
                        pe.wait_ge(quart_ready, nth_level(t, g, lev, 1))
                        for j in range(HG):
                            mm = pe.matmul(bank3(g, 2)[:, j, :], inv[g][:, j, :], quart[g][:, j, :], start=True, stop=True)
                        if lev < LEVELS - 1:
                            for j in range(HG):
                                mm = pe.matmul(bank3(g, 3)[:, j, :], quart[g][:, j, :], inv[g][:, j, :], start=True, stop=True)
                        mm.then_inc(double_done, 1)
                    if lev == 1 and t:
                        for g in range(G):
                            pe.wait_ge(vb_ready, nth(t, g))
                            for j in range(HG):
                                hh = g * HG + j
                                mm = pe.matmul(bank3(g, 0)[:, j, :], tile(NK + hh, t), state[:, hh, :], start=True, stop=True)
                            mm.then_inc(ks_done, 1)
                if t < TC - 1:
                    for g in range(G):
                        grow(t + 1, g)
                for g in range(G):
                    pe.wait_ge(inv_ready, nth_level(t, g, LEVELS - 1, 0))
                    if t:
                        pe.wait_ge(rhs_ready, nth(t - 1, g))
                    else:
                        pe.wait_ge(vb_ready, nth(t, g))
                    for j in range(HG):
                        mm = pe.matmul(bank3(g, 1)[:, j, :], invT[g][:, j, :], rhs[g][:, j, :], start=True, stop=True)
                    mm.then_inc(u_done, 1)
                if t == TC - 1:
                    output_transposes(0)
                    output_transposes(1)
                for g in range(G):
                    pe.wait_ge(u_ready, nth(t, g))
                    if t < TC - 1:
                        keys_keys(t + 1, g)
                        for j in range(HG):
                            mm = pe.matmul(bank3(g, 2)[:, j, :], kdec[g][:, j, :], quart[g][:, j, :], start=True, stop=True)
                        mm.then_inc(supd_done, 1)
                    pe.wait_ge(qdec_ready, nth(t, g))
                    pe.wait_ge(qk_masked, nth(t, g))
                    for j in range(HG):
                        hh = g * HG + j
                        if t:
                            pe.matmul(bank3(g, 3)[:, j, :], qdec[g][:, j, :], state[:, hh, :], start=True, stop=False)
                        mm = pe.matmul(bank3(g, 3)[:, j, :], qk[g][:, j, :], quart[g][:, j, :], start=(t == 0), stop=True)
                    mm.then_inc(o_done, 1)

            output_transposes(2)

            def heads(k):
                c = out_chunk(k)
                return xT_hi[:, c, :], xT_lo[:, c, :]

            def project_out(m, blocks):
                for k in blocks:
                    if m == 0:
                        block_ready(WO + k)
                    mm = out_mms(WO + k, m, heads(k), k == 0, False)
                    if m == TC - 1:
                        mm.then_inc(block_done, 1)
            mem_blocks, first_heads = range(HP), range(HP, RING)
            pe.wait_ge(oT_ready, H)
            project_out(0, mem_blocks)
            pe.wait_ge(o_ready, nth(TC - 1, G - 1))
            project_out(1, mem_blocks)
            project_out(2, mem_blocks)
            pe.wait_ge(cat_lo_ready, 1 + H)
            project_out(0, first_heads)
            for g in range(G):
                for j in range(HG):
                    pe.wait_ge(on_ready, H + j * G + g + 1)
                    mm = pe.transpose(by_tokens(3)[:, g * RING + j, :], tile(NV + g * HG + j, TC - 1), ident[:, :])
                mm.then_inc(oT_done, 1)
            project_out(1, first_heads)
            project_out(2, first_heads)
            pe.wait_ge(cat_lo_ready, 1 + H + G)
            project_out(3, range(RING))
            boundary(2, lambda m, blocks: finish(WO + RING, m, blocks, lambda b: heads(RING + b)), FFN2)
            fin = ffn(FFN2, FC + 1)
            boundary(3, fin, None)


_INS = ["x", "mem", "l0_ffn1_w_in", "l0_ffn1_w_out", "l0_ln1_g", "l0_ln1_b", "l0_w_in", "l0_conv_w", "l0_a_log",
        "l0_dt_bias", "l0_onorm_g", "l0_w_mem_kv", "l0_w_o", "l0_ln2_g", "l0_ln2_b", "l0_ffn2_w_in", "l0_ffn2_w_out",
        "l0_ln3_g", "l0_ln3_b"]


def kernel(**inputs):
    import numpy as np
    import concourse.bacc as bacc
    from concourse.bass_utils import run_bass_kernel_spmd

    nc = bacc.Bacc("TRN2", target_bir_lowering=False, num_devices=1)
    arrays, aps = {}, {}
    for name in _INS:
        v = np.ascontiguousarray(inputs[name])
        arrays[name + "_dram"] = v
        aps[name] = nc.dram_tensor(name + "_dram", v.shape, mybir.dt.from_np(v.dtype), kind="ExternalInput").ap()
    out = nc.dram_tensor("out_dram", (1, T, D), F32, kind="ExternalOutput").ap()
    build(nc, aps, out)
    r = run_bass_kernel_spmd(nc, [arrays], core_ids=[0])
    return r.results[0]["out_dram"]
```
